# Optimizing a Trainium2 kernel written in Bass

```python
import math
import jax, jax.numpy as jnp
from jax import lax
import numpy as np

D_MODEL = 2048
BATCH = 1
SEQ = 256
DEPTH = 1
DEC_BATCH = 8
DEC_SEQ = 8
PAST_LEN = 256
PAGE_SIZE = 128

MIX_W = D_MODEL
NSA_W = MIX_W // 2
POOL_W = MIX_W - NSA_W
HEAD_DIM = 64
N_HEADS = NSA_W // HEAD_DIM
N_KV = 4
GROUP = N_HEADS // N_KV
KV_W = N_KV * HEAD_DIM
CMP_BLOCK = 32
CMP_STRIDE = 16
SEL_BLOCK = 64
SEL_TOP = 16
WINDOW = 512
Q_BLOCK = 64
POOL_SIZES = (2, 4, 8, 16)
N_POOL = len(POOL_SIZES)
POOL_GW = POOL_W // N_POOL
POOL_BUF = max(POOL_SIZES) - 1
PEER_HEADS = 8
PEER_QDIM = 256
N_KEYS = 128
N_EXPERTS = N_KEYS * N_KEYS
PEER_TOPK = 16
PEER_TBLOCK = 128
IN_COLS = NSA_W + 3 * 2 * KV_W + 3 * N_HEADS + POOL_W
EPS = 1e-6
NEG = -1e30
FORCE_BONUS = 1e4

kernel_name = 'hymba_nsa_pool_peer_step'

def rms_norm(x, g):
    xf = x.astype(jnp.float32)
    y = xf * lax.rsqrt(jnp.mean(xf * xf, axis=-1, keepdims=True) + EPS)
    return (y * g.astype(jnp.float32)).astype(x.dtype)

def masked_softmax(s, mask, axis):
    s = jnp.where(mask, s, NEG)
    e = jnp.where(mask, jnp.exp(s - jnp.max(s, axis=axis, keepdims=True)), 0.0)
    return e / jnp.maximum(jnp.sum(e, axis=axis, keepdims=True), 1e-30)

def alibi_slopes():
    h = np.arange(1, N_HEADS + 1, dtype=np.float32)
    return jnp.asarray((2.0 ** (-8.0 * h / N_HEADS)).reshape(N_KV, GROUP), jnp.float32)

def adaln(c, w_ada, b_ada):
    m = jax.nn.silu(c) @ w_ada + b_ada
    return m.reshape(c.shape[0], 6, D_MODEL)

def modulate(x, shift, scale, g):
    return rms_norm(x, g) * (1.0 + scale[:, None, :]) + shift[:, None, :]

def mix_inputs(h, w_in, g_qnorm, g_knorm):
    B, T, _ = h.shape
    z = h @ w_in
    offs = [NSA_W, NSA_W + 2 * KV_W, NSA_W + 4 * KV_W, NSA_W + 6 * KV_W, NSA_W + 6 * KV_W + 3 * N_HEADS]
    q, kvc, kvs, kvw, gl, u = jnp.split(z, offs, axis=-1)
    q = rms_norm(q.reshape(B, T, N_KV, GROUP, HEAD_DIM), g_qnorm)
    kvc = kvc.reshape(B, T, 2, N_KV, HEAD_DIM)
    kvs = kvs.reshape(B, T, 2, N_KV, HEAD_DIM)
    kvw = kvw.reshape(B, T, 2, N_KV, HEAD_DIM)
    kvs = jnp.stack([rms_norm(kvs[:, :, 0], g_knorm[1]), kvs[:, :, 1]], axis=2)
    kvw = jnp.stack([rms_norm(kvw[:, :, 0], g_knorm[2]), kvw[:, :, 1]], axis=2)
    gates = jax.nn.sigmoid(gl.reshape(B, T, N_KV, GROUP, 3))
    return q, kvc, kvs, kvw, gates, u

def compressed_kv(kv_rows, cmp_pe, w_cmp, g_k):
    T = kv_rows.shape[1]
    nc = (T - CMP_BLOCK) // CMP_STRIDE + 1
    idx = np.arange(nc)[:, None] * CMP_STRIDE + np.arange(CMP_BLOCK)[None, :]
    blk = kv_rows[:, idx] + jnp.swapaxes(cmp_pe, 0, 1)
    comp = jnp.einsum('bnlcgd,cglde->bncge', blk, w_cmp)
    kc = rms_norm(comp[:, :, 0], g_k)
    vc = comp[:, :, 1]
    pos_c = jnp.asarray(np.arange(nc) * CMP_STRIDE + CMP_BLOCK - 1, jnp.int32)
    return kc, vc, pos_c

def select_blocks(kv_rows):
    B, T = kv_rows.shape[:2]
    ns = -(-T // SEL_BLOCK)
    kv = jnp.pad(kv_rows, ((0, 0), (0, ns * SEL_BLOCK - T), (0, 0), (0, 0), (0, 0)))
    kv = kv.reshape(B, ns, SEL_BLOCK, 2, N_KV, HEAD_DIM)
    return kv[:, :, :, 0], kv[:, :, :, 1]

def cmp_to_sel(nc, ns):
    pos = np.arange(nc)[:, None] * CMP_STRIDE + np.arange(CMP_BLOCK)[None, :]
    sel = pos // SEL_BLOCK
    return jnp.asarray((sel[:, :, None] == np.arange(ns)[None, None, :]).mean(axis=1), jnp.float32)

def nsa_block(q, pos_q, gates, kc, vc, pos_c, ks_blk, vs_blk, kw, vw, pos_w, slopes):
    B, Tq = q.shape[:2]
    scale = HEAD_DIM ** -0.5
    f32 = jnp.float32
    dist_c = (pos_q[:, None] - pos_c[None, :]).astype(f32)
    s_c = jnp.einsum('bqgrd,bngd->bgrqn', q, kc, preferred_element_type=f32) * scale \
        - slopes[None, :, :, None, None] * dist_c
    p_c = masked_softmax(s_c, dist_c >= 0, -1)
    o_c = jnp.einsum('bgrqn,bngd->bqgrd', p_c, vc.astype(f32))
    ns = ks_blk.shape[1]
    imp = jnp.einsum('bgrqn,ns->bqgs', p_c, cmp_to_sel(kc.shape[1], ns))
    sel_ids = jnp.arange(ns)
    blk_q = pos_q // SEL_BLOCK
    forced = (sel_ids[None, :] == 0) | (sel_ids[None, :] == blk_q[:, None]) | (sel_ids[None, :] == blk_q[:, None] - 1)
    valid = sel_ids[None, :] * SEL_BLOCK <= pos_q[:, None]
    imp = jnp.where(valid[None, :, None, :], imp + FORCE_BONUS * forced[None, :, None, :].astype(f32), NEG)
    _, idx = lax.top_k(imp, min(SEL_TOP, ns))
    b_i = jnp.arange(B)[:, None, None, None]
    g_i = jnp.arange(N_KV)[None, None, :, None]
    kg = ks_blk[b_i, idx, :, g_i]
    vg = vs_blk[b_i, idx, :, g_i]
    pos_s = idx[..., None] * SEL_BLOCK + jnp.arange(SEL_BLOCK)
    dist_s = (pos_q[None, :, None, None, None] - pos_s).astype(f32)[:, :, :, None]
    s_s = jnp.einsum('bqgrd,bqgnkd->bqgrnk', q, kg, preferred_element_type=f32) * scale \
        - slopes[None, None, :, :, None, None] * dist_s
    p_s = masked_softmax(s_s, dist_s >= 0, (-2, -1))
    o_s = jnp.einsum('bqgrnk,bqgnkd->bqgrd', p_s, vg.astype(f32))
    dist_w = (pos_q[:, None] - pos_w[None, :])
    mask_w = (dist_w >= 0) & (dist_w <= WINDOW) & (pos_w[None, :] >= 0)
    s_w = jnp.einsum('bqgrd,bkgd->bgrqk', q, kw, preferred_element_type=f32) * scale \
        - slopes[None, :, :, None, None] * dist_w.astype(f32)
    p_w = masked_softmax(s_w, mask_w, -1)
    o_w = jnp.einsum('bgrqk,bkgd->bqgrd', p_w, vw.astype(f32))
    g = gates.astype(f32)
    out = g[..., 0:1] * o_c + g[..., 1:2] * o_s + g[..., 2:3] * o_w
    return out.astype(q.dtype)

def nsa_prompt(q, gates, kvc, kvs, kvw, cmp_pe, w_cmp, g_knorm, slopes):
    B, T = q.shape[:2]
    kc, vc, pos_c = compressed_kv(kvc, cmp_pe, w_cmp, g_knorm[0])
    ks_blk, vs_blk = select_blocks(kvs)
    kvw_pad = jnp.pad(kvw, ((0, 0), (WINDOW, 0), (0, 0), (0, 0), (0, 0)))
    qb = min(Q_BLOCK, T)

    def body(i):
        s = i * qb
        qi = lax.dynamic_slice_in_dim(q, s, qb, axis=1)
        gi = lax.dynamic_slice_in_dim(gates, s, qb, axis=1)
        wi = lax.dynamic_slice_in_dim(kvw_pad, s, qb + WINDOW, axis=1)
        pos_q = s + jnp.arange(qb)
        pos_w = s - WINDOW + jnp.arange(qb + WINDOW)
        return nsa_block(qi, pos_q, gi, kc, vc, pos_c, ks_blk, vs_blk, wi[:, :, 0], wi[:, :, 1], pos_w, slopes)

    out = lax.map(body, jnp.arange(T // qb))
    return jnp.moveaxis(out, 0, 1).reshape(B, T, N_KV, GROUP, HEAD_DIM)

def nsa_sample(q, gates, kvc, kvs, kvw, cache_kv_cmp, cache_kv_slc, cache_kv_win, page_table,
               cmp_pe, w_cmp, g_knorm, slopes):
    B, T = q.shape[:2]
    past_len = page_table.shape[1] * PAGE_SIZE
    full_c = jnp.concatenate([cache_kv_cmp[page_table].reshape((B, past_len) + cache_kv_cmp.shape[2:]), kvc], axis=1)
    full_s = jnp.concatenate([cache_kv_slc[page_table].reshape((B, past_len) + cache_kv_slc.shape[2:]), kvs], axis=1)
    kc, vc, pos_c = compressed_kv(full_c, cmp_pe, w_cmp, g_knorm[0])
    ks_blk, vs_blk = select_blocks(full_s)
    w_buf = cache_kv_win.shape[1]
    w_ctx = jnp.concatenate([cache_kv_win, kvw], axis=1)
    pos_q = past_len + jnp.arange(T)
    pos_w = past_len - w_buf + jnp.arange(w_buf + T)
    out = nsa_block(q, pos_q, gates, kc, vc, pos_c, ks_blk, vs_blk, w_ctx[:, :, 0], w_ctx[:, :, 1], pos_w, slopes)
    return out, w_ctx[:, -w_buf:]

def pool_mix(u, prefix, pos, w_pool, pool_scale):
    B, T, _ = u.shape
    ext = jnp.concatenate([prefix, u], axis=1).astype(jnp.float32)
    cs = jnp.concatenate([jnp.zeros((B, 1, POOL_W), jnp.float32), jnp.cumsum(ext, axis=1)], axis=1)
    outs = []
    for gi, w in enumerate(POOL_SIZES):
        c0, c1 = gi * POOL_GW, (gi + 1) * POOL_GW
        hi = cs[:, POOL_BUF + 1:POOL_BUF + 1 + T, c0:c1]
        lo = cs[:, POOL_BUF + 1 - w:POOL_BUF + 1 - w + T, c0:c1]
        cnt = jnp.minimum(w, pos + 1).astype(jnp.float32)[None, :, None]
        outs.append((hi - lo) / cnt - ext[:, POOL_BUF:, c0:c1])
    d = jnp.stack(outs, axis=2)
    y = jnp.einsum('btgc,gce->btge', d, w_pool.astype(jnp.float32)).reshape(B, T, POOL_W)
    return (y * pool_scale.astype(jnp.float32)).astype(u.dtype)

def peer(h, peer_wq, peer_subkeys, peer_u, peer_v):
    B, T, D = h.shape
    n = B * T
    nb = -(-n // PEER_TBLOCK)
    xt = jnp.pad(h.reshape(n, D), ((0, nb * PEER_TBLOCK - n), (0, 0))).reshape(nb, PEER_TBLOCK, D)

    def body(xb):
        q = (xb @ peer_wq).reshape(PEER_TBLOCK, PEER_HEADS, 2, PEER_QDIM // 2)
        s = jnp.einsum('thpd,phkd->thpk', q, peer_subkeys, preferred_element_type=jnp.float32)
        s1, i1 = lax.top_k(s[:, :, 0], PEER_TOPK)
        s2, i2 = lax.top_k(s[:, :, 1], PEER_TOPK)
        cand = (s1[..., :, None] + s2[..., None, :]).reshape(PEER_TBLOCK, PEER_HEADS, PEER_TOPK * PEER_TOPK)
        cid = (i1[..., :, None] * N_KEYS + i2[..., None, :]).reshape(PEER_TBLOCK, PEER_HEADS, PEER_TOPK * PEER_TOPK)
        sc, j = lax.top_k(cand, PEER_TOPK)
        eid = jnp.take_along_axis(cid, j, axis=-1)
        g = jax.nn.softmax(sc, axis=-1)
        a = jax.nn.gelu(jnp.einsum('td,thkd->thk', xb, peer_u[eid], preferred_element_type=jnp.float32),
                        approximate=False)
        return jnp.einsum('thk,thkd->td', (g * a).astype(peer_v.dtype), peer_v[eid])

    y = lax.map(body, xt).reshape(nb * PEER_TBLOCK, D)[:n]
    return y.reshape(B, T, D).astype(h.dtype)

def mix_out(o_nsa, o_pool, w_out):
    B, T = o_pool.shape[:2]
    return jnp.concatenate([o_nsa.reshape(B, T, NSA_W), o_pool], axis=-1) @ w_out

def setup_inputs(seed: int = 0) -> dict:
    key = jax.random.key(seed)
    ks = jax.random.split(key, 26)
    n_pages = PAST_LEN // PAGE_SIZE
    n_phys = (DEC_BATCH * n_pages * 5) // 4
    w_buf = min(WINDOW, PAST_LEN)
    nrm = jax.random.normal
    page_table = jax.random.permutation(ks[6], n_phys)[:DEC_BATCH * n_pages].reshape(DEC_BATCH, n_pages).astype(jnp.int32)
    return {
        'x_prompt': nrm(ks[0], (BATCH, SEQ, D_MODEL), jnp.float32),
        'x_sample': nrm(ks[1], (DEC_BATCH, DEC_SEQ, D_MODEL), jnp.float32),
        'cache_kv_cmp': nrm(ks[2], (n_phys, PAGE_SIZE, 2, N_KV, HEAD_DIM), jnp.float32),
        'cache_kv_slc': nrm(ks[3], (n_phys, PAGE_SIZE, 2, N_KV, HEAD_DIM), jnp.float32),
        'cache_kv_win': nrm(ks[4], (DEC_BATCH, w_buf, 2, N_KV, HEAD_DIM), jnp.float32),
        'state_pool': nrm(ks[5], (DEC_BATCH, POOL_BUF, POOL_W), jnp.float32),
        'page_table': page_table,
        'c_prompt': nrm(ks[7], (BATCH, D_MODEL), jnp.float32),
        'c_sample': nrm(ks[8], (DEC_BATCH, D_MODEL), jnp.float32),
        'w_ada': nrm(ks[9], (D_MODEL, 6 * D_MODEL), jnp.float32) * (0.5 * D_MODEL ** -0.5),
        'b_ada': nrm(ks[10], (6 * D_MODEL,), jnp.float32) * 0.01,
        'g_norm1': 1.0 + 0.1 * nrm(ks[11], (D_MODEL,), jnp.float32),
        'g_norm2': 1.0 + 0.1 * nrm(ks[12], (D_MODEL,), jnp.float32),
        'w_in': nrm(ks[13], (D_MODEL, IN_COLS), jnp.float32) * D_MODEL ** -0.5,
        'w_out': nrm(ks[14], (MIX_W, D_MODEL), jnp.float32) * MIX_W ** -0.5,
        'g_qnorm': 1.0 + 0.1 * nrm(ks[15], (HEAD_DIM,), jnp.float32),
        'g_knorm': 1.0 + 0.1 * nrm(ks[16], (3, HEAD_DIM), jnp.float32),
        'cmp_pe': 0.5 * nrm(ks[17], (2, CMP_BLOCK, N_KV, HEAD_DIM), jnp.float32),
        'w_cmp': nrm(ks[18], (2, N_KV, CMP_BLOCK, HEAD_DIM, HEAD_DIM), jnp.float32) * (CMP_BLOCK * HEAD_DIM) ** -0.5,
        'w_pool': nrm(ks[19], (N_POOL, POOL_GW, POOL_GW), jnp.float32) * POOL_GW ** -0.5,
        'pool_scale': 1.0 + 0.1 * nrm(ks[20], (POOL_W,), jnp.float32),
        'peer_wq': nrm(ks[21], (D_MODEL, PEER_HEADS * PEER_QDIM), jnp.float32) * D_MODEL ** -0.5,
        'peer_subkeys': nrm(ks[22], (2, PEER_HEADS, N_KEYS, PEER_QDIM // 2), jnp.float32) * (PEER_QDIM // 2) ** -0.5,
        'peer_u': nrm(ks[23], (N_EXPERTS, D_MODEL), jnp.float32) * D_MODEL ** -0.5,
        'peer_v': nrm(ks[24], (N_EXPERTS, D_MODEL), jnp.float32) * (PEER_HEADS * PEER_TOPK) ** -0.5,
    }

def reference(x_prompt, x_sample, cache_kv_cmp, cache_kv_slc, cache_kv_win, state_pool, page_table,
              c_prompt, c_sample, w_ada, b_ada, g_norm1, g_norm2, w_in, w_out, g_qnorm, g_knorm,
              cmp_pe, w_cmp, w_pool, pool_scale, peer_wq, peer_subkeys, peer_u, peer_v):
    slopes = alibi_slopes()

    Bp, Tp = x_prompt.shape[:2]
    mod_p = adaln(c_prompt, w_ada, b_ada)
    h = modulate(x_prompt, mod_p[:, 0], mod_p[:, 1], g_norm1)
    q, kvc_p, kvs_p, kvw_p, gates, u_p = mix_inputs(h, w_in, g_qnorm, g_knorm)
    o_nsa = nsa_prompt(q, gates, kvc_p, kvs_p, kvw_p, cmp_pe, w_cmp, g_knorm, slopes)
    o_pool = pool_mix(u_p, jnp.zeros((Bp, POOL_BUF, POOL_W), u_p.dtype), jnp.arange(Tp), w_pool, pool_scale)
    x1 = x_prompt + mod_p[:, 2][:, None, :] * mix_out(o_nsa, o_pool, w_out)
    h2 = modulate(x1, mod_p[:, 3], mod_p[:, 4], g_norm2)
    y_prompt = x1 + mod_p[:, 5][:, None, :] * peer(h2, peer_wq, peer_subkeys, peer_u, peer_v)
    win_p = kvw_p[:, -min(WINDOW, Tp):]
    pool_p = u_p[:, -POOL_BUF:]

    Ts = x_sample.shape[1]
    past_len = page_table.shape[1] * PAGE_SIZE
    mod_s = adaln(c_sample, w_ada, b_ada)
    h = modulate(x_sample, mod_s[:, 0], mod_s[:, 1], g_norm1)
    q, kvc_s, kvs_s, kvw_s, gates, u_s = mix_inputs(h, w_in, g_qnorm, g_knorm)
    o_nsa, win_s = nsa_sample(q, gates, kvc_s, kvs_s, kvw_s, cache_kv_cmp, cache_kv_slc, cache_kv_win,
                              page_table, cmp_pe, w_cmp, g_knorm, slopes)
    o_pool = pool_mix(u_s, state_pool, past_len + jnp.arange(Ts), w_pool, pool_scale)
    x1 = x_sample + mod_s[:, 2][:, None, :] * mix_out(o_nsa, o_pool, w_out)
    h2 = modulate(x1, mod_s[:, 3], mod_s[:, 4], g_norm2)
    y_sample = x1 + mod_s[:, 5][:, None, :] * peer(h2, peer_wq, peer_subkeys, peer_u, peer_v)
    pool_s = jnp.concatenate([state_pool, u_s], axis=1)[:, -POOL_BUF:]

    return (y_prompt, y_sample, kvc_p, kvs_p, win_p, pool_p, kvc_s, kvs_s, win_s, pool_s)


_drawn_inputs = setup_inputs


def setup_inputs(seed=0):
    import zlib

    import numpy as np

    out = dict(_drawn_inputs(seed))
    spreads = {}
    factors = {'cache_kv_slc': 2.789,
     'b_ada': 4.236,
     'g_norm2': 8.0,
     'g_qnorm': 8.0,
     'pool_scale': 3.14,
     'peer_wq': 4.093,
     'peer_subkeys': 4.107,
     'peer_u': 4.549,
     'peer_v': 4.066}
    for name, (base, spread) in spreads.items():
        noise = np.random.default_rng([zlib.crc32(name.encode()), seed]).standard_normal(out[name].shape)
        drawn = base * np.exp(spread * noise) if base else spread * noise
        out[name] = __import__('jax').numpy.asarray(drawn.astype(out[name].dtype))
    for name, factor in factors.items():
        out[name] = (out[name] * factor).astype(out[name].dtype)
    return out
```

```python
import numpy as np

import concourse.bass as bass
from concourse import mybir
from contextlib import ExitStack

F32 = mybir.dt.float32
I32 = mybir.dt.int32
U32 = mybir.dt.uint32
ALU = mybir.AluOpType
ACT = mybir.ActivationFunctionType
X_AXIS = mybir.AxisListType.X

D = 2048
NK = D // 128
TP = 256
DB, DT = 8, 8
TS = DB * DT
TOK = TP + TS
TILES = 3
PAST, PAGE = 256, 128
HD, NKV, GROUP = 64, 4, 4
NH = NKV * GROUP
NSA_W = NH * HD
KVW = NKV * HD
POOL_W = D - NSA_W
POOL_SIZES = (2, 4, 8, 16)
POOL_GW = POOL_W // 4
POOL_BUF = 15
CMP_BLOCK, CMP_STRIDE = 32, 16
NC_ = (TP - CMP_BLOCK) // CMP_STRIDE + 1
NS_C = DB * NC_
NSEQ = DB + 2
IN_COLS = NSA_W + 6 * KVW + 3 * NH + POOL_W
COL_C, COL_S, COL_W = NSA_W, NSA_W + 2 * KVW, NSA_W + 4 * KVW
COL_GL = NSA_W + 6 * KVW
COL_U = COL_GL + 3 * NH
PH, PK, TOPK = 8, 128, 16
HP = 2 * PH
EPS = 1e-6
SC_QK = HD ** -0.5
MASKED = -1e30
NSLOT = 8
SECTION = 512
KP = 4

C_ID, C_BLK, C_SELF, C_SELT, C_FOLD, C_IOTA, C_VALID, C_PAGE = 0, 128, 256, 280, 536, 600, 616, 618
C_N = 620


def constants():
    c = np.zeros((128, C_N), np.float32)
    p = np.arange(128)
    c[p, C_ID + p] = 1.0
    c[:, C_BLK:C_BLK + 128] = (p[:, None] // 64 == p[None, :] // 64) / 64.0
    for j in range(4):
        for b in range(DB):
            c[32 * j + b, C_SELF + b] = c[32 * j + b, C_SELF + DB + b] = 1.0
        c[32 * j + DB, C_SELF + 2 * DB] = 1.0
        c[32 * j + DB, C_SELT:C_SELT + 128] = 1.0
        for m in range(128):
            c[32 * j + (m % TS) // DT, C_SELT + 128 + m] = 1.0
    c[DB + 1, C_SELF:C_SELF + 2 * DB + 1] = 1.0
    c[DB + 1, C_SELT:C_SELT + 256] = 1.0
    c[p, C_FOLD + p % 64] = 1.0
    c[:, C_IOTA:C_IOTA + 16] = np.arange(16)
    c[:, C_VALID] = p >= CMP_BLOCK - 1
    c[:, C_VALID + 1] = 1.0
    c[:, C_PAGE] = p
    slopes = (2.0 ** (-8.0 * np.arange(1, NH + 1) / NH)).astype(np.float32)
    inv = 1.0 / SC_QK
    q, k = np.arange(128), np.arange(256)
    dist = (128 + q[:, None] - k[None, :])
    bias = np.where(dist[:, None] >= 0, -inv * slopes[None, :, None] * dist[:, None], MASKED)
    pos_c = np.arange(NC_) * CMP_STRIDE + CMP_BLOCK - 1
    bc = np.zeros((128, 2, 2, 8, NC_), np.float32)
    for gi in range(2):
        for t in range(2):
            for gp in range(2):
                for r in range(GROUP):
                    dc = 128 * t + q[:, None] - pos_c[None, :]
                    s = slopes[(2 * gp + gi) * GROUP + r]
                    bc[:, gi, t, gp * 4 + r] = np.where(dc >= 0, -inv * s * dc, MASKED)
    rows = np.arange(128)
    s_row, t_row = slopes[rows // DT], rows % DT
    bs = np.full((128, DB, PAST + TS), MASKED, np.float64)
    bcs = np.full((128, DB, NS_C), MASKED, np.float64)
    for b in range(DB):
        bs[:, b, :PAST] = -inv * s_row[:, None] * (PAST + t_row[:, None] - np.arange(PAST)[None])
        dn = t_row[:, None] - np.arange(DT)[None]
        bs[:, b, PAST + b * DT:PAST + (b + 1) * DT] = np.where(dn >= 0, -inv * s_row[:, None] * dn, MASKED)
        bcs[:, b, b * NC_:(b + 1) * NC_] = -inv * s_row[:, None] * (PAST + t_row[:, None] - pos_c[None])
    pool = np.zeros((128, 4, 3 * 128 + 128), np.float32)
    for i, w in enumerate(POOL_SIZES):
        for t in range(TP):
            cnt = min(w, t + 1)
            for s in range(max(0, t - w + 1), t + 1):
                v = 1.0 / cnt - (s == t)
                if t < 128:
                    pool[s, i, t] = v
                elif s < 128:
                    pool[s, i, 128 + t - 128] = v
                else:
                    pool[s - 128, i, 256 + t - 128] = v
        for b in range(DB):
            for t in range(DT):
                for s in range(t - w + 1, t + 1):
                    v = 1.0 / w - (s == t)
                    if s < 0:
                        pool[b * POOL_BUF + POOL_BUF + s, i, 384 + b * DT + t] = v
                    else:
                        pool[b * DT + s, i, 448 + b * DT + t] = v
    f = lambda a: np.ascontiguousarray(a, dtype=np.float32)
    return {"k_const": c, "k_bias": f(bias.reshape(128, -1)), "k_bias_c": f(bc.reshape(128, -1)),
            "k_bias_s": f(bs.reshape(128, -1)), "k_bias_cs": f(bcs.reshape(128, -1)),
            "k_pool": f(pool.reshape(128, -1))}


def build(nc, I, O, scratch):
    ctx = ExitStack()
    with ctx:
        arena = ctx.enter_context(nc.sbuf_tensor("arena", [128, 53200], F32))
        PS = ctx.enter_context(nc.psum_tensor("PS", [128, 8, 512], F32))

        def sem(name):
            return ctx.enter_context(nc.semaphore(name))

        def view(at, *dims):
            n = int(np.prod(dims))
            v = arena[:, at:at + n]
            if len(dims) == 1:
                return v
            names = "abcde"[:len(dims)]
            return v.rearrange(f"p ({' '.join(names)}) -> p {' '.join(names)}",
                               **{k: d for k, d in zip(names[1:], dims[1:])})

        R_MOD, R_RING, R_H, R_Z, R_P = 0, 12288, 28672, 34816, 45712
        mod = view(R_MOD, 6 * D)
        ring = view(R_RING, NSLOT, KP, SECTION)
        hT = view(R_H, NK, 3 * 128)
        Z = view(R_Z, TILES, IN_COLS)
        X = view(R_Z, TILES, D)
        at = [R_P]

        def keep(*dims):
            v = view(at[0], *dims)
            at[0] += int(np.prod(dims))
            return v
        cst = keep(C_N)
        ident, blk = cst[:, C_ID:C_ID + 128], cst[:, C_BLK:C_BLK + 128]
        selF = cst[:, C_SELF:C_SELF + 17]
        selT = cst[:, C_SELT:C_SELT + 256].rearrange("p (a b) -> p a b", a=2)
        fold = cst[:, C_FOLD:C_FOLD + 64]
        iota = cst[:, C_IOTA:C_IOTA + 16]
        A1T, B1T = keep(NK, 17), keep(NK, 17)
        g1T = keep(NK)
        gq, gk = keep(HD), keep(3, HD)
        gkc = keep(1)
        psT = keep(8)
        sumsq, rstd = keep(4), keep(4)
        cT_at = at[0]
        cT = keep(NK, 32)
        skT_at = at[0]
        skT = keep(HP, PK)
        att_at = at[0]
        KC = keep(2, 9 * NC_)
        VCp = keep(256)
        biasC = keep(2, 16, NC_)
        PC = keep(2, 16, NC_)
        stat = keep(128)
        qkr = keep(3, 24)
        mxv, nm, sm = keep(2, 4), keep(2, 4), keep(2, 4)
        gates_s = keep(DB, 3)
        pgf = keep(16)
        pgi = keep(16).bitcast(I32)
        pgx = keep(16).bitcast(I32)
        assert at[0] <= 53200, at[0]
        cin = view(R_H, D)
        csig = view(R_H + D, D)
        sk_raw = view(R_H + 2 * D, HP, 128)
        sq_junk = view(R_Z + 3 * D, D)
        g1_raw = view(R_Z + 4 * D, 128)
        ps_raw = view(R_Z + 4 * D + 128, 128)

        QT = view(R_MOD, 8, TP)
        QTs = view(R_MOD + 8 * TP, 2, DB, 4 * DT)
        KT = view(R_MOD + 8 * TOK, 2, 2, TOK)
        VCs = view(R_MOD + 8 * TOK + 4 * TOK, 256)
        CT = view(R_RING, 4, NSEQ, 256)
        WC = [view(R_RING + 10240, 2, CMP_BLOCK, HD), view(R_H, 2, CMP_BLOCK, HD)]
        cpage = view(R_RING + 14336, 4, 512)
        sq_z = view(R_H + 4096, 24, HD)
        VCT = view(R_H + 4096, 2, 9 * NC_)
        kc_sq = view(R_H + 4096 + 300, 2 * 9 * NC_)
        pe_raw = view(R_H + 5632, 512)
        poolB = view(R_RING, 4, 512)
        past_u = view(R_RING + 2048, POOL_W)
        WP = view(R_RING + 3072, 4, 2, POOL_GW)
        DTt = view(R_RING + 5120, 8, TOK)
        biasP = view(R_RING + 7680, NH, 256)
        Pp = view(R_RING + 11776, 2, 2, 512)
        PTp = view(R_RING + 13824, 2, 1280)
        biasS = view(R_RING, DB, PAST + TS)
        biasCS = view(R_RING + 2560, DB, NS_C)
        kvpage = view(R_RING + 3520, 2, 2, 2, 512)
        KTb = view(R_RING + 7680, 2, 2, 2, 256)
        Ps = view(R_RING + 9728, 2, 760)
        PTs = view(R_RING + 11264, 2, 7 * 128)
        OT = view(R_H, NK, 3 * 128)
        X1 = view(R_Z, TILES, D)
        GB = view(R_Z + 6144, 2, 2, SECTION)
        TMP = view(R_Z + 8192, 4, SECTION)
        GB2 = view(R_Z + 6144, 2, D)
        H2 = view(R_MOD, TILES, D)
        H2T = view(R_H, NK, 3 * 128)
        g2b = view(att_at, D)
        QPT = view(R_MOD + 6144, NK, 3 * 128)
        SC = view(R_H, TILES, HP, PK)
        cand = view(R_MOD + 6144, PH, TOPK, TOPK)
        onehot = view(R_MOD + 8192, PH, TOPK, TOPK)
        tk = R_MOD + 10240
        val1, idx1, idx1f = view(tk, HP, TOPK), view(tk + 256, HP, TOPK).bitcast(U32), view(tk + 512, HP, TOPK)
        val2, idx2 = view(tk + 768, PH, TOPK), view(tk + 896, PH, TOPK).bitcast(U32)
        ab_i = view(tk + 1024, 2, PH, TOPK).bitcast(U32)
        ab_f = view(tk + 1280, 2, PH, TOPK)
        picked = view(tk + 1536, 2, PH, TOPK)
        smax = view(tk + 1792, PH)
        eid = view(skT_at, TILES, PH, TOPK)
        gw = view(skT_at + 384, TILES, PH, TOPK)
        dots = view(skT_at + 768, TILES, 128)
        wgt = view(skT_at + 1152, TILES, 128)
        eid_s = view(skT_at + 1536, 64)
        gw_s = view(skT_at + 1600, 64)
        idxs = view(skT_at + 1664, 2, 8).bitcast(I32)
        stage_a = view(skT_at + 1680, 16)
        stage_w = view(skT_at + 1696, 16)
        rows_ring = view(R_RING, NSLOT, D)
        acc = view(att_at, D)

        s_cst, s_cin, s_x, s_sk, s_gain = sem("consts_in"), sem("cond_in"), sem("x_in"), sem("subkeys_in"), sem("gains_in")
        s_piece = [sem(f"piece_in{i}") for i in range(NSLOT)]
        s_free = sem("piece_used")
        s_sig, s_silu, s_cps, s_cT = sem("sigma_ready"), sem("silu_ready"), sem("cond_T_psum"), sem("cond_T_ready")
        s_adaC, s_bada = sem("ada_copied"), sem("bias_ada_in")
        s_sq, s_ms, s_rt, s_rs, s_xn = sem("squares"), sem("mean_sq"), sem("root"), sem("rstd"), sem("x_normed")
        s_gT, s_gTc = sem("gain_T_psum"), sem("gain_T")
        s_m1, s_m1c = sem("mod1_psum"), sem("mod1_ready")
        s_xt, s_hA, s_hD = sem("x_T_psum"), sem("h_prompt_ready"), sem("h_sample_ready")
        s_zA, s_zD = sem("z_tiles12_ready"), sem("z_tile0_ready")
        s_gexp, s_zms, s_zrt, s_norm = sem("gate_exp"), sem("z_mean_sq"), sem("z_root"), sem("qk_normed")
        s_wc, s_pe, s_ctz, s_pt_in, s_pgi, s_pgx = sem("w_cmp_in"), sem("cmp_pe_in"), sem("cmp_zeroed"), sem("page_table_in"), sem("page_rows_f"), sem("page_rows")
        s_cpage = [sem(f"cmp_page_in{i}") for i in range(4)]
        s_ct, s_ctc, s_cmp = sem("cmp_T_psum"), sem("cmp_T"), sem("cmp_psum")
        s_kc1, s_kcm, s_kc2, s_kc3, s_kc = sem("kc_squares"), sem("kc_mean"), sem("kc_meaned"), sem("kc_root"), sem("kc_ready")
        s_vct, s_vcp, s_vc = sem("vc_T"), sem("vc_psum"), sem("vc_ready")
        s_qt, s_qtA, s_qtD = sem("qk_T_psum"), sem("q_T"), sem("k_T")
        s_plin, s_dp, s_dt, s_yp, s_yo = sem("pool_in"), sem("pool_d_psum"), sem("pool_d"), sem("pool_y_psum"), sem("pool_y")
        s_bp, s_bc, s_bs = sem("bias_prompt_in"), sem("bias_cmp_in"), sem("bias_sample_in")
        s_csc, s_cmx, s_cex, s_pc = sem("cmp_scores"), sem("cmp_shifted"), sem("cmp_exp"), sem("cmp_probs")
        s_S, s_mx, s_exp, s_pn = sem("scores"), sem("row_max"), sem("exps"), sem("probs")
        s_T, s_TA, s_TD, s_o, s_oc = sem("probs_T_psum"), sem("probs_T_a"), sem("probs_T_d"), sem("out_psum"), sem("out_ready")
        s_kvp = [sem("kv_page_in0"), sem("kv_page_in1")]
        s_gso, s_gsi = sem("gates_out"), sem("gates_in")
        s_kt, s_ktA, s_ktD = sem("cache_kT_psum"), sem("cache_ksT"), sem("cache_kwT")
        q_S, q_mx, q_exp, q_pn = sem("smp_scores"), sem("smp_row_max"), sem("smp_exps"), sem("smp_probs")
        q_T, q_TA, q_TD, q_o, q_oc = sem("smp_T_psum"), sem("smp_T_a"), sem("smp_T_d"), sem("smp_out_psum"), sem("smp_out")
        s_out = sem("outputs_stored")
        s_zout = sem("z_outputs_stored")
        s_x1in, s_gp, s_gb, s_x1 = sem("x_again_in"), sem("gate1_psum"), sem("gate1"), sem("x1_ready")
        s_sq2, s_ms2, s_rt2 = sem("squares2"), sem("mean_sq2"), sem("root2")
        s_g2in, s_m2, s_h2 = sem("g_norm2_in"), sem("mod2_psum"), sem("h2_ready")
        s_ht, s_htA, s_htD = sem("h2_T_psum"), sem("h2_T_a"), sem("h2_T_d")
        s_g2p, s_g2 = sem("gate2_psum"), sem("gate2")
        s_qA, s_qD = sem("peer_q_a"), sem("peer_q_d")
        s_skp, s_skc = sem("subkeys_T_psum"), sem("subkeys_T")
        s_scp, s_sc = sem("peer_scores_psum"), sem("peer_scores")
        s_e2, s_e2x, s_eid = sem("expert_logits"), sem("expert_exp"), sem("experts_ready")
        s_row = [sem(f"row_in{i}") for i in range(NSLOT)]
        s_idx, s_rowfree, s_pdma = sem("row_indices"), sem("row_used"), sem("pool_dma_go")
        s_stage, s_dots, s_gelu, s_wgt = sem("dots_staged"), sem("dots_ready"), sem("gelu_ready"), sem("weights_staged")
        s_facc, s_fold, s_y, s_yst = sem("acc_ready"), sem("folded"), sem("y_ready"), sem("y_stored")
        dve_chain = sem("dve_chain")
        n_link = [0]

        def link(ins):
            n_link[0] += 1
            ins.then_inc(dve_chain, 1)
            nc.vector.wait_ge(dve_chain, n_link[0])

        def wait(eng, s, n):
            if n > 0:
                eng.wait_ge(s, n)

        ADA_N = 6 * D // SECTION
        ADA_FIRST = 8
        w_ada_v = I["w_ada"].rearrange("(c p) n -> p c n", p=128)
        w_in_v = I["w_in"].rearrange("(c p) n -> p c n", p=128)
        w_wq_v = I["peer_wq"].rearrange("(c p) n -> p c n", p=128)
        w_out_nsa = I["w_out"][0:NSA_W, :].rearrange("(gp gi r d) n -> gp gi d r n", gp=2, gi=2, r=4)
        w_out_pool = I["w_out"][NSA_W:D, :].rearrange("(c p) n -> p c n", p=128)
        IN_SEC = [0, 512, COL_C, COL_S, COL_W, COL_U, COL_U + 512]
        NIN = len(IN_SEC)
        ADA_WITH = [3, 3] + [2] * 5
        pieces = [("ada", s, p) for s in range(ADA_FIRST) for p in range(4)]
        ada_next = ADA_FIRST
        for n in range(NIN):
            pieces += [("in", n, p) for p in range(4)]
            for _ in range(ADA_WITH[n]):
                pieces += [("ada", ada_next, p) for p in range(4)]
                ada_next += 1
        assert ada_next == ADA_N
        pieces += [("gl", 0, 0)]
        n_early = len(pieces)
        pieces += [("out", n, p) for n in range(4) for p in range(4)]
        pieces += [("wq", n, p) for n in range(4) for p in range(4)]
        index = {p: i for i, p in enumerate(pieces)}
        count, arrived = [0] * NSLOT, []
        for i, p in enumerate(pieces):
            count[i % NSLOT] += 32 if p[0] == "out" and p[2] < 2 else 16
            arrived.append(count[i % NSLOT])

        def used(eng, kind, n, p=3):
            eng.wait_ge(s_free, index[(kind, n, p)] + 1)

        gl_w = view(R_RING + (index[("gl", 0, 0)] % NSLOT) * KP * SECTION, NK, 48)

        def load_piece(eng, i):
            kind, n, p = pieces[i]
            dst, done = ring[:, i % NSLOT], s_piece[i % NSLOT]
            wait(eng, s_free, i - NSLOT + 1)
            cols = slice(n * SECTION, (n + 1) * SECTION)
            if kind == "ada":
                eng.dma_start(dst, w_ada_v[:, KP * p:KP * p + KP, cols]).then_inc(done, 16)
            elif kind == "in":
                eng.dma_start(dst, w_in_v[:, KP * p:KP * p + KP, IN_SEC[n]:IN_SEC[n] + SECTION]).then_inc(done, 16)
            elif kind == "wq":
                eng.dma_start(dst, w_wq_v[:, KP * p:KP * p + KP, cols]).then_inc(done, 16)
            elif kind == "gl":
                eng.dma_start(gl_w, w_in_v[:, :, COL_GL:COL_GL + 48]).then_inc(done, 16)
            elif p < 2:
                for gi in range(2):
                    eng.dma_start(dst[64 * gi:64 * gi + 64], w_out_nsa[p, gi, :, :, cols]).then_inc(done, 16)
            else:
                eng.dma_start(dst, w_out_pool[:, KP * (p - 2):KP * (p - 2) + KP, cols]).then_inc(done, 16)

        CBLK = [("page", m // 2, m % 2) for m in range(16)] + [("prompt", DB, 0), ("prompt", DB, 1), ("pe", DB + 1, 0)]
        b_ada = I["b_ada"].rearrange("(a n) -> a n", a=1)
        b_row = slice(DB + 1, DB + 2)
        N_ZOUT = 6 + 2 + 1 + 2 * DB
        UNITS = [(t, gp, r) for t in range(2) for gp in range(2) for r in range(4)]
        SPANS = [(0, 320), (320, 640), (640, 760)]
        PHASES = [("u", 0), ("u", 1), ("v", 0), ("u", 2), ("v", 1), ("v", 2)]
        NROWS = [128, 128, 64]
        HANDED = 16
        BASE = [sum(NROWS[t] for _, t in PHASES[:i]) for i in range(len(PHASES))]

        def base_copy(ph):
            return BASE[ph] // 16

        def z_section(t, n):
            v = Z[:, t, IN_SEC[n]:IN_SEC[n] + SECTION]
            return v.rearrange("p (r gi d) -> p gi r d", r=4, gi=2) if n < 2 else v

        def in_bank(t, n):
            v = PS[:, 3 * (n % 2) + t, :]
            return v.rearrange("p (gi r d) -> p gi r d", gi=2, r=4) if n < 2 else v

        block = ctx.enter_context(nc.Block())

        @block.sync
        def _(sp):
            sp.dma_start(cin[0:DB, :], I["c_sample"]).then_inc(s_cin, 16)
            sp.dma_start(cin[DB:DB + 1, :], I["c_prompt"]).then_inc(s_cin, 16)
            sp.dma_start(cst, I["k_const"]).then_inc(s_cst, 16)
            for i in range(n_early):
                if i == index[("ada", ADA_FIRST, 0)]:
                    sp.wait_ge(s_adaC, ADA_FIRST)
                    sp.dma_start(mod[b_row, 0:2 * D], b_ada[:, 0:2 * D]).then_inc(s_bada, 16)
                load_piece(sp, i)
                if i == 8:
                    xs = I["x_sample"].rearrange("b t d -> (b t) d")
                    sp.dma_start(X[:, 0:2, :], I["x_prompt"][0].rearrange("(t p) d -> p t d", p=128)).then_inc(s_x, 16)
                    sp.dma_start(X[0:TS, 2, :], xs).then_inc(s_x, 16)
                    sp.dma_start(X[TS:128, 2, :], xs).then_inc(s_x, 16)
                    sp.dma_start(g1_raw[0:NK, :], I["g_norm1"].rearrange("(c p) -> c p", p=128)).then_inc(s_gain, 16)
                    sp.dma_start(ps_raw[0:8, :], I["pool_scale"].rearrange("(c p) -> c p", p=128)).then_inc(s_gain, 16)
                    sp.dma_start(gq, I["g_qnorm"].rearrange("(a d) -> a d", a=1).to_broadcast([128, HD])).then_inc(s_gain, 16)
                    sp.dma_start(gk.rearrange("p a b -> p (a b)"), I["g_knorm"].rearrange("(a k) d -> a (k d)", a=1).to_broadcast([128, 3 * HD])).then_inc(s_gain, 16)
                    for gi in range(2):
                        sp.dma_start(gkc[64 * gi:64 * gi + 64, :], I["g_knorm"][0].rearrange("(d a) -> d a", a=1)).then_inc(s_gain, 16)
                    sp.dma_start(sk_raw, I["peer_subkeys"].rearrange("p h k d -> k (p h) d")).then_inc(s_sk, 16)
                    sp.dma_start(biasC.rearrange("p a b c -> p (a b c)"), I["k_bias_c"]).then_inc(s_bc, 16)
            sp.wait_ge(s_adaC, ADA_N)
            sp.dma_start(mod[b_row, 2 * D:6 * D], b_ada[:, 2 * D:6 * D]).then_inc(s_bada, 16)
            sp.wait_ge(s_free, n_early)
            wc = I["w_cmp"].rearrange("c (gp gi) l d e -> c gi gp d l e", gi=2)
            for c in range(2):
                for gi in range(2):
                    for gp in range(2):
                        sp.dma_start(WC[c][64 * gi:64 * gi + 64, gp], wc[c, gi, gp]).then_inc(s_wc, 16)
            for c in range(2):
                sp.dma_start(pe_raw[0:CMP_BLOCK, c * 256:(c + 1) * 256], I["cmp_pe"][c].rearrange("l g d -> l (g d)")).then_inc(s_pe, 16)
            sp.wait_ge(s_cmp, 2)
            sp.dma_start(poolB.rearrange("p a b -> p (a b)"), I["k_pool"]).then_inc(s_plin, 16)
            sp.dma_start(past_u[0:DB * POOL_BUF, :], I["state_pool"].rearrange("b s c -> (b s) c")).then_inc(s_plin, 16)
            for i in range(4):
                sp.dma_start(WP[:, i], I["w_pool"][i].rearrange("(c p) e -> p c e", p=128)).then_inc(s_plin, 16)
            sp.dma_start(biasP.rearrange("p a b -> p (a b)"), I["k_bias"]).then_inc(s_bp, 16)
            sp.wait_ge(s_yp, 8)
            sp.dma_start(biasS.rearrange("p a b -> p (a b)"), I["k_bias_s"]).then_inc(s_bs, 16)
            sp.dma_start(biasCS.rearrange("p a b -> p (a b)"), I["k_bias_cs"]).then_inc(s_bs, 16)
            sp.wait_ge(q_oc, 2 * DB)
            for i in range(n_early, n_early + NSLOT):
                load_piece(sp, i)
            sp.wait_ge(s_zout, 16 * N_ZOUT)
            sp.dma_start(X1[:, 0:2, :], I["x_prompt"][0].rearrange("(t p) d -> p t d", p=128)).then_inc(s_x1in, 16)
            sp.dma_start(X1[0:TS, 2, :], xs).then_inc(s_x1in, 16)
            sp.dma_start(X1[TS:128, 2, :], xs).then_inc(s_x1in, 16)
            sp.dma_start(g2b, I["g_norm2"].rearrange("(a d) -> a d", a=1).to_broadcast([128, D])).then_inc(s_g2in, 16)
            for i in range(n_early + NSLOT, len(pieces)):
                load_piece(sp, i)
            for t in range(2):
                sp.wait_ge(s_y, t + 1)
                sp.dma_start(O["y_prompt"][0, t * 128:(t + 1) * 128, :], acc).then_inc(s_yst, 16)
            sp.wait_ge(s_y, 3)
            sp.dma_start(O["y_sample"].rearrange("b t d -> (b t) d"), acc[0:TS, :]).then_inc(s_yst, 16)
            sp.wait_ge(s_yst, 48)
            sp.wait_ge(s_out, 32)

        @block.gpsimd
        def _(pool):
            pool.dma_start(O["win_sample"][:, 0:PAST - DT].rearrange("b s c g d -> b (s c g d)"),
                           I["cache_kv_win"][:, DT:PAST].rearrange("b s c g d -> b (s c g d)")).then_inc(s_out, 16)
            pool.dma_start(O["pool_sample"][:, 0:POOL_BUF - DT, :], I["state_pool"][:, DT:POOL_BUF, :]).then_inc(s_out, 16)
            pool.dma_start(pgi, I["page_table"].rearrange("(a b) j -> a (b j)", a=1).to_broadcast([128, 16])).then_inc(s_pt_in, 16)
            pool.wait_ge(s_free, n_early)
            nc.gpsimd.memset(CT[:, :, DB + 1, :], 0.0).then_inc(s_ctz, 1)
            cmp_rows = I["cache_kv_cmp"].rearrange("n s c g d -> (n s) (c g d)")
            slc_rows = I["cache_kv_slc"].rearrange("n s c g d -> (n s) (c g d)")
            win_rows = I["cache_kv_win"].rearrange("b (j s) c g d -> b s j (c g d)", j=2)
            pool.wait_ge(s_pgx, 1)
            for m in range(16):
                wait(pool, s_ct, m - 3)
                pool.indirect_dma_start(out=cpage[:, m % 4, :], out_offset=None, in_=cmp_rows,
                                        in_offset=bass.IndirectOffsetOnAxis(ap=pgx[:, m:m + 1], axis=0)).then_inc(s_cpage[m % 4], 16)
            pool.wait_ge(s_norm, 1)
            for t in range(2):
                for name, col in (("cmp_prompt", COL_C), ("slc_prompt", COL_S), ("win_prompt", COL_W)):
                    pool.dma_start(O[name][0, t * 128:(t + 1) * 128].rearrange("s c g d -> s (c g d)"), Z[:, t, col:col + 512]).then_inc(s_zout, 16)
            for name, col in (("cmp_sample", COL_C), ("slc_sample", COL_S)):
                pool.dma_start(O[name].rearrange("b t c g d -> (b t) (c g d)"), Z[0:TS, 2, col:col + 512]).then_inc(s_zout, 16)
            pool.dma_start(O["pool_prompt"][0], Z[128 - POOL_BUF:128, 1, COL_U:COL_U + POOL_W]).then_inc(s_zout, 16)
            for b in range(DB):
                pool.dma_start(O["win_sample"][b, PAST - DT:PAST].rearrange("s c g d -> s (c g d)"), Z[b * DT:b * DT + DT, 2, COL_W:COL_W + 512]).then_inc(s_zout, 16)
            for b in range(DB):
                pool.dma_start(O["pool_sample"][b, POOL_BUF - DT:POOL_BUF, :], Z[b * DT:b * DT + DT, 2, COL_U:COL_U + POOL_W]).then_inc(s_zout, 16)
            pool.dma_start(scratch, Z[0:TS, 2, COL_GL:COL_GL + 48]).then_inc(s_gso, 16)
            pool.wait_ge(s_gso, 16)
            sv = scratch.rearrange("(b t) (h x) -> h t b x", t=DT, x=3)
            for h in range(NH):
                pool.dma_start(gates_s[DT * h:DT * h + DT, :, :], sv[h]).then_inc(s_gsi, 16)
            pool.wait_ge(s_yp, 8)
            for b in range(DB):
                if b >= 2:
                    pool.wait_ge(q_o, b - 1)
                for j in range(2):
                    m = 2 * b + j
                    pool.indirect_dma_start(out=kvpage[:, b % 2, 0, j, :], out_offset=None, in_=slc_rows,
                                            in_offset=bass.IndirectOffsetOnAxis(ap=pgx[:, m:m + 1], axis=0)).then_inc(s_kvp[b % 2], 16)
                pool.dma_start(kvpage[:, b % 2, 1], win_rows[b]).then_inc(s_kvp[b % 2], 16)
            u_rows, v_rows = I["peer_u"], I["peer_v"]
            for ph, (kind, t) in enumerate(PHASES):
                table = u_rows if kind == "u" else v_rows
                base = BASE[ph]
                with pool.Fori(0, NROWS[t] // 16, 1) as it:
                    for half in range(2):
                        pool.wait_ge(s_idx, it * 2 + (base // 8 + half + 1))
                        for s in range(8):
                            pool.wait_ge(s_rowfree, it * 16 + (base + half * 8 + s - 7 + HANDED))
                            pool.sem_inc(s_pdma, 1)
                            pool.indirect_dma_start(out=rows_ring[:, s, :], out_offset=None, in_=table,
                                                    in_offset=bass.IndirectOffsetOnAxis(ap=idxs[:, half, s:s + 1], axis=0)).then_inc(s_row[s], 16)

        @block.scalar
        def _(act):
            act.wait_ge(s_cin, 32)
            nc.scalar.activation(csig[0:9, :], cin[0:9, :], ACT.Exp, scale=-1.0).then_inc(s_sig, 1)
            ada_done = [0]

            def ada_out(n):
                for s in range(ada_done[0], ada_done[0] + n):
                    used(act, "ada", s)
                    nc.scalar.activation(mod[:, s * SECTION:(s + 1) * SECTION], PS[:, 6 + s % 2, :], ACT.Copy).then_inc(s_adaC, 1)
                ada_done[0] += n
            ada_out(3)
            act.wait_ge(s_x, 48)
            for t in range(TILES):
                wait(act, s_sq, t)
                nc.scalar.activation(sq_junk, X[:, t, :], ACT.Square, accum_out=sumsq[:, t:t + 1]).then_inc(s_sq, 1)
            ada_out(2)
            act.wait_ge(s_ms, 1)
            nc.scalar.activation(rstd[:, 0:3], sumsq[:, 0:3], ACT.Sqrt).then_inc(s_rt, 1)
            act.wait_ge(s_rs, 1)
            for t in range(TILES):
                nc.scalar.activation(X[:, t, :], X[:, t, :], ACT.Copy, scale=rstd[:, t:t + 1]).then_inc(s_xn, 1)
            ada_out(3)
            act.wait_ge(s_m1c, 1)
            for c in range(NK):
                act.wait_ge(s_xt, c + 1)
                nc.scalar.activation(hT[:, c, 0:TP], PS[:, c % 3, 0:TP], ACT.Identity, scale=A1T[:, c, 16:17], bias=B1T[:, c, 16:17]).then_inc(s_hA, 1)
            for n in range(NIN):
                used(act, "in", n)
                for t in (1, 2):
                    nc.scalar.activation(z_section(t, n), in_bank(t, n), ACT.Copy).then_inc(s_zA, 1)
                ada_out(ADA_WITH[n])
            used(act, "gl", 0, 0)
            for t in range(TILES):
                nc.scalar.activation(Z[:, t, COL_GL:COL_GL + 48], PS[:, 3 + t, 0:48], ACT.Exp, scale=-1.0).then_inc(s_gexp, 1)

            def ct_out(m):
                kind, seq, j = CBLK[m]
                n = CMP_BLOCK if kind == "pe" else 128
                if m == 0 or kind == "pe":
                    act.wait_ge(s_ctz, 1)
                act.wait_ge(s_ct, m + 1)
                nc.scalar.activation(CT[:, :, seq, j * 128:j * 128 + n], PS[:, m % 4, :].rearrange("p (a b) -> p a b", a=4)[:, :, 0:n], ACT.Copy).then_inc(s_ctc, 1)
            for m in range(10):
                ct_out(m)
            act.wait_ge(s_zms, 1)
            nc.scalar.activation(qkr, qkr, ACT.Sqrt).then_inc(s_zrt, 1)
            for m in range(10, len(CBLK)):
                ct_out(m)
            act.wait_ge(s_kc2, 1)
            nc.scalar.activation(kc_sq, kc_sq, ACT.Sqrt).then_inc(s_kc3, 1)
            for t in range(TILES):
                n = 128 if t < 2 else TS
                act.wait_ge(s_qt, t + 1)
                for i in range(2):
                    src = PS[:, 3 * (t % 2) + i, :].rearrange("p (a b) -> p a b", a=4)[:, :, 0:n]
                    if t < 2:
                        nc.scalar.activation(QT[:, 4 * i:4 * i + 4, t * 128:(t + 1) * 128], src, ACT.Copy).then_inc(s_qtA, 1)
                    else:
                        nc.scalar.activation(QTs[:, i].rearrange("p b (r t) -> p r b t", r=4), src.rearrange("p r (b t) -> p r b t", t=DT), ACT.Copy).then_inc(s_qtA, 1)
            act.wait_ge(s_cmx, 1)
            nc.scalar.activation(PC, PC, ACT.Exp, scale=SC_QK).then_inc(s_cex, 1)
            act.wait_ge(s_kc, 1)
            for i in range(8):
                act.wait_ge(s_yp, i + 1)
                nc.scalar.activation(OT[:, 8 + i, 0:TOK], PS[:, 4 + i % 2, 0:TOK], ACT.Copy, scale=psT[:, i:i + 1]).then_inc(s_yo, 1)
                nc.scalar.activation(OT[:, 8 + i, TOK:384], PS[:, 4 + i % 2, TP:TOK], ACT.Copy, scale=psT[:, i:i + 1]).then_inc(s_yo, 1)

            def p_exp(u):
                t = UNITS[u][0]
                nk = 128 * (t + 1)
                act.wait_ge(s_mx, u + 1)
                for gi in range(2):
                    for br in range(2):
                        k = 2 * gi + br
                        v = Pp[:, u % 2, gi, br * nk:(br + 1) * nk]
                        nc.scalar.activation(v, v, ACT.Exp, bias=nm[:, u % 2, k:k + 1], scale=SC_QK, accum_out=sm[:, u % 2, k:k + 1]).then_inc(s_exp, 1)
            p_exp(0)
            for u, (t, gp, r) in enumerate(UNITS):
                if u + 1 < len(UNITS):
                    p_exp(u + 1)
                act.wait_ge(s_T, u + 1)
                n = 256 * (t + 1)
                nc.scalar.activation(PTp[:, u % 2, 0:n], PS[:, 4, 0:n], ACT.Copy).then_inc(s_TA, 1)
                nc.scalar.activation(PTp[0:NC_, u % 2, 1024:1280], PS[0:NC_, 6, 0:256], ACT.Copy).then_inc(s_TA, 1)
                act.wait_ge(s_o, u + 1)
                nc.scalar.activation(OT[:, gp * 4 + r, t * 128:(t + 1) * 128], PS[:, 7, 0:128], ACT.Copy).then_inc(s_oc, 1)
            def kt_out(b):
                act.wait_ge(s_kt, b + 1)
                nc.scalar.activation(KTb[:, b % 2, 0], PS[:, 4, :].rearrange("p (a b) -> p a b", a=2), ACT.Copy).then_inc(s_ktA, 1)

            def q_exp_(b):
                act.wait_ge(q_mx, b + 1)
                for k, (lo, hi) in enumerate(SPANS):
                    v = Ps[:, b % 2, lo:hi]
                    nc.scalar.activation(v, v, ACT.Exp, bias=nm[:, b % 2, k:k + 1], scale=SC_QK, accum_out=sm[:, b % 2, k:k + 1]).then_inc(q_exp, 1)
            kt_out(0)
            q_exp_(0)
            for b in range(DB):
                if b + 1 < DB:
                    kt_out(b + 1)
                    q_exp_(b + 1)
                act.wait_ge(q_T, b + 1)
                nc.scalar.activation(PTs[:, b % 2, 0:512], PS[:, 6, :], ACT.Copy).then_inc(q_TA, 1)
                act.wait_ge(q_o, b + 1)
                for dup in range(2):
                    o = TP + dup * TS + b * DT
                    nc.scalar.activation(OT[:, 0:8, o:o + DT], PS[:, 7, 448:512].rearrange("p (a b) -> p a b", a=8), ACT.Copy).then_inc(q_oc, 1)
            for n in range(4):
                act.wait_ge(s_gp, n + 1)
                wait(act, s_x1, 3 * (n - 1))
                if n == 0:
                    act.wait_ge(s_zout, 16 * N_ZOUT)
                for k in range(2):
                    nc.scalar.activation(GB[:, n % 2, k], PS[:, 6 + k, :], ACT.Copy).then_inc(s_gb, 1)
            act.wait_ge(s_x1, 12)
            for t in range(TILES):
                nc.scalar.activation(H2[:, t, :], X1[:, t, :], ACT.Square, accum_out=sumsq[:, t:t + 1]).then_inc(s_sq2, 1)
            act.wait_ge(s_ms2, 1)
            nc.scalar.activation(rstd[:, 0:3], sumsq[:, 0:3], ACT.Sqrt).then_inc(s_rt2, 1)
            for c in range(0, NK, 2):
                act.wait_ge(s_ht, c + 1)
                nc.scalar.activation(H2T[:, c, 0:TOK], PS[:, c % 8, 0:TOK], ACT.Copy).then_inc(s_htA, 1)
            for i in range(8):
                act.wait_ge(s_g2p, i + 1)
                nc.scalar.activation(GB2[:, i // 4, (i % 4) * SECTION:(i % 4 + 1) * SECTION], PS[:, i, :], ACT.Copy).then_inc(s_g2, 1)
            for i in range(0, HP, 2):
                used(act, "wq", i // 4)
                nc.scalar.activation(QPT[:, i, 0:TOK], PS[:, i % 8, 0:TOK], ACT.Copy).then_inc(s_qA, 1)
                nc.scalar.activation(QPT[:, i, TOK:384], PS[:, i % 8, TP:TOK], ACT.Copy).then_inc(s_qA, 1)
            for k in range(12):
                act.wait_ge(s_scp, k + 1)
                t, q4 = k // 4, k % 4
                nc.scalar.activation(SC[:, t, 4 * q4:4 * q4 + 4, :].rearrange("p a b -> p (a b)"), PS[:, k % 8, :], ACT.Copy).then_inc(s_sc, 1)
            for t in range(TILES):
                act.wait_ge(s_e2, t + 1)
                nc.scalar.activation(gw[:, t], gw[:, t], ACT.Exp).then_inc(s_e2x, 1)
            act.wait_ge(s_eid, 1)
            for ph, (kind, t) in enumerate(PHASES):
                if kind == "v":
                    act.wait_ge(s_dots, t + 1)
                    nc.scalar.activation(dots[:, t, 0:NROWS[t]], dots[:, t, 0:NROWS[t]], ACT.Gelu).then_inc(s_gelu, 1)
                src = eid[:, t].rearrange("p a b -> p (a b)") if t < 2 else eid_s
                base = BASE[ph] // 8
                with act.Fori(0, NROWS[t] // 16, 1) as it:
                    for half in range(2):
                        act.wait_ge(s_rowfree, it * 16 + (base + half - 1) * 8 + HANDED)
                        nc.scalar.activation(idxs[:, half, :], src[:, bass.ds(it * 16 + half * 8, 8)], ACT.Copy).then_inc(s_idx, 1)

        @block.tensor
        def _(pe):
            def need(i):
                pe.wait_ge(s_piece[i % NSLOT], arrived[i])

            def ada_section(s):
                wait(pe, s_adaC, s - 1)
                for p in range(4):
                    i = index[("ada", s, p)]
                    need(i)
                    for j in range(4):
                        last = nc.tensor.matmul(PS[32 * j:32 * j + 32, 6 + s % 2, :], cT[:, 4 * p + j, :], ring[:, i % NSLOT, j, :],
                                                start=(p == 0), stop=(p == 3), tile_position=(0, 32 * j))
                    last.then_inc(s_free, 1)

            pe.wait_ge(s_cst, 16)
            pe.wait_ge(s_silu, 1)
            for c in range(NK):
                last = nc.tensor.transpose(PS[:, 0, c * 9:c * 9 + 9], cin[0:9, c * 128:(c + 1) * 128], ident[0:9, 0:9])
            last.then_inc(s_cps, 1)
            pe.wait_ge(s_cT, 1)
            for s in range(ADA_FIRST):
                ada_section(s)
            pe.wait_ge(s_gain, 16 * 6)
            nc.tensor.transpose(PS[:, 0, 0:NK], g1_raw[0:NK, :], ident[0:NK, 0:NK])
            nc.tensor.transpose(PS[:, 0, 16:24], ps_raw[0:8, :], ident[0:8, 0:8]).then_inc(s_gT, 1)
            pe.wait_ge(s_sk, 16)
            for i in range(HP):
                last = nc.tensor.transpose(PS[:, 2 + i // 4, (i % 4) * 128:(i % 4 + 1) * 128], sk_raw[:, i, :], ident)
            last.then_inc(s_skp, 1)
            pe.wait_ge(s_bada, 16)
            pe.wait_ge(s_gTc, 1)
            for k in range(2):
                for c in range(NK):
                    last = nc.tensor.matmul(PS[:, k, c * 17:c * 17 + 17], mod[:, k * D + c * 128:k * D + (c + 1) * 128], selF, start=True, stop=True)
            last.then_inc(s_m1, 1)
            pe.wait_ge(s_m1c, 1)
            pe.wait_ge(s_skc, 1)
            pe.wait_ge(s_xn, 3)
            for c in range(NK):
                wait(pe, s_hA, c - 2)
                wait(pe, s_hD, c - 2)
                for t in range(TILES):
                    last = nc.tensor.transpose(PS[:, c % 3 + 3 * (t // 2), (t % 2) * 128:(t % 2 + 1) * 128], X[:, t, c * 128:(c + 1) * 128], ident)
                last.then_inc(s_xt, 1)
            pe.wait_ge(s_hA, NK)
            pe.wait_ge(s_hD, NK)
            ada_i = ADA_FIRST
            for n in range(NIN):
                wait(pe, s_zA, 2 * (n - 1))
                wait(pe, s_zD, n - 1)
                for p in range(4):
                    i = index[("in", n, p)]
                    need(i)
                    for t in range(TILES):
                        for j in range(KP):
                            c = KP * p + j
                            last = nc.tensor.matmul(PS[:, 3 * (n % 2) + t, :], hT[:, c, t * 128:(t + 1) * 128], ring[:, i % NSLOT, j, :],
                                                    start=(c == 0), stop=(c == NK - 1))
                    last.then_inc(s_free, 1)
                for _ in range(ADA_WITH[n]):
                    ada_section(ada_i)
                    ada_i += 1
            pe.wait_ge(s_zA, 2 * (NIN - 1))
            pe.wait_ge(s_zD, NIN - 1)
            need(index[("gl", 0, 0)])
            for t in range(TILES):
                for c in range(NK):
                    last = nc.tensor.matmul(PS[:, 3 + t, 0:48], hT[:, c, t * 128:(t + 1) * 128], gl_w[:, c, :], start=(c == 0), stop=(c == NK - 1))
            last.then_inc(s_free, 1)
            pe.wait_ge(s_zA, 2 * NIN)
            pe.wait_ge(s_zD, NIN)
            pe.wait_ge(s_gexp, 3)
            for m, (kind, seq, j) in enumerate(CBLK):
                wait(pe, s_ctc, m - 3)
                if kind == "page":
                    pe.wait_ge(s_cpage[m % 4], 16 * (m // 4 + 1))
                    src, n = cpage[:, m % 4, :], 128
                elif kind == "prompt":
                    src, n = Z[:, j, COL_C:COL_C + 512], 128
                else:
                    pe.wait_ge(s_pe, 32)
                    src, n = pe_raw[0:CMP_BLOCK, :], CMP_BLOCK
                for k in range(4):
                    last = nc.tensor.transpose(PS[:, m % 4, k * 128:k * 128 + n], src[:, k * 128:(k + 1) * 128], ident[0:n, 0:n])
                last.then_inc(s_ct, 1)
            pe.wait_ge(s_wc, 128)
            pe.wait_ge(s_ctc, len(CBLK))
            for c in range(2):
                for gp in range(2):
                    for l in range(CMP_BLOCK):
                        for gi in range(2):
                            h = slice(64 * gi, 64 * gi + 64)
                            last = nc.tensor.matmul(PS[h, 4 + c, gp * 150:gp * 150 + 150], WC[c][h, gp, l, :],
                                                    CT[h, 2 * c + gp, :, l:l + CMP_STRIDE * (NC_ - 1) + 1:CMP_STRIDE],
                                                    start=(l == 0), stop=(l == CMP_BLOCK - 1), tile_position=(64 * gi, 64 * gi))
                last.then_inc(s_cmp, 1)
            pe.wait_ge(s_kc1, 1)
            nc.tensor.matmul(PS[:, 6, 0:270], blk, kc_sq, start=True, stop=True).then_inc(s_kcm, 1)
            pe.wait_ge(s_vct, 1)
            for gp in range(2):
                nc.tensor.transpose(PS[0:NS_C, 7, gp * 128:(gp + 1) * 128], VCT[:, gp, 0:NS_C], ident)
            for gp in range(2):
                last = nc.tensor.transpose(PS[0:NC_, 7, 256 + gp * 128:256 + (gp + 1) * 128], VCT[:, gp, NS_C:NS_C + NC_], ident)
            last.then_inc(s_vcp, 1)
            pe.wait_ge(s_norm, 1)
            for t in range(TILES):
                n = 128 if t < 2 else TS
                wait(pe, s_qtA, 2 * (t - 1))
                wait(pe, s_qtD, t - 1)
                bank = 3 * (t % 2)
                for gp in range(2):
                    for r in range(4):
                        nc.tensor.transpose(PS[:, bank + gp, r * 128:r * 128 + n], Z[0:n, t, gp * 512 + r * 128:gp * 512 + (r + 1) * 128], ident[0:n, 0:n])
                for br, col in enumerate((COL_S, COL_W)):
                    for gp in range(2):
                        k = 2 * br + gp
                        last = nc.tensor.transpose(PS[:, bank + 2, k * 128:k * 128 + n], Z[0:n, t, col + gp * 128:col + (gp + 1) * 128], ident[0:n, 0:n])
                last.then_inc(s_qt, 1)
            pe.wait_ge(s_kc, 1)
            pe.wait_ge(s_vc, 1)
            pe.wait_ge(s_qtA, 6)
            pe.wait_ge(s_qtD, 3)
            for t in range(2):
                for k in range(8):
                    for gi in range(2):
                        h = slice(64 * gi, 64 * gi + 64)
                        last = nc.tensor.matmul(PS[:, 6 + gi, (t * 8 + k) * NC_:(t * 8 + k + 1) * NC_], QT[h, k, t * 128:(t + 1) * 128],
                                                KC[h, k // 4, NS_C:NS_C + NC_], start=True, stop=True, tile_position=(64 * gi, 0))
            last.then_inc(s_csc, 1)
            pe.wait_ge(s_plin, 16 * 6)
            for c in range(8):
                w = c // 2
                wait(pe, s_dt, c - 3)
                u = [Z[:, t, COL_U + c * 128:COL_U + (c + 1) * 128] for t in range(TILES)]
                bank = PS[:, c % 4, :]
                nc.tensor.matmul(bank[:, 0:128], u[0], poolB[:, w, 0:128], start=True, stop=True)
                nc.tensor.matmul(bank[:, 128:256], u[0], poolB[:, w, 128:256], start=True, stop=False)
                nc.tensor.matmul(bank[:, 128:256], u[1], poolB[:, w, 256:384], start=False, stop=True)
                n = DB * POOL_BUF
                nc.tensor.matmul(bank[:, 256:320], past_u[0:n, c * 128:(c + 1) * 128], poolB[0:n, w, 384:448], start=True, stop=False)
                nc.tensor.matmul(bank[:, 256:320], u[2][0:TS, :], poolB[0:TS, w, 448:512], start=False, stop=True).then_inc(s_dp, 1)
            pe.wait_ge(s_dt, 8)
            for i in range(8):
                w, eh = i // 2, i % 2
                wait(pe, s_yo, 2 * (i - 1))
                for ch in range(2):
                    last = nc.tensor.matmul(PS[:, 4 + i % 2, 0:TOK], WP[:, w, ch, eh * 128:(eh + 1) * 128], DTt[:, 2 * w + ch, :], start=(ch == 0), stop=(ch == 1))
                last.then_inc(s_yp, 1)
            pe.wait_ge(s_yo, 16)
            pe.wait_ge(s_cmx, 1)

            def p_scores(u):
                t, gp, r = UNITS[u]
                nk = 128 * (t + 1)
                wait(pe, s_mx, u - 1)
                for br in range(2):
                    for gi in range(2):
                        h = slice(64 * gi, 64 * gi + 64)
                        last = nc.tensor.matmul(PS[:, 2 * (u % 2) + gi, br * nk:(br + 1) * nk], QT[h, gp * 4 + r, t * 128:(t + 1) * 128],
                                                KT[h, br, gp, 0:nk], start=True, stop=True, tile_position=(64 * gi, 0))
                last.then_inc(s_S, 1)
            pe.wait_ge(s_pc, 1)
            p_scores(0)
            for u, (t, gp, r) in enumerate(UNITS):
                nk = 128 * (t + 1)
                if u + 1 < len(UNITS):
                    p_scores(u + 1)
                pe.wait_ge(s_pn, u + 1)
                wait(pe, s_TA, 2 * u)
                wait(pe, s_TD, u)
                for gi in range(2):
                    for k in range(2 * (t + 1)):
                        nc.tensor.transpose(PS[:, 4 + gi, k * 128:(k + 1) * 128], Pp[:, u % 2, gi, k * 128:(k + 1) * 128], ident)
                    last = nc.tensor.transpose(PS[0:NC_, 6, gi * 128:(gi + 1) * 128], PC[:, gi, t * 8 + gp * 4 + r, :], ident)
                last.then_inc(s_T, 1)
                pe.wait_ge(s_TA, 2 * u + 2)
                pe.wait_ge(s_TD, u + 1)
                wait(pe, s_oc, u)
                for gi in range(2):
                    g = 2 * gp + gi
                    o = PS[64 * gi:64 * gi + 64, 7, 0:128]
                    nc.tensor.matmul(o, VCp[0:NC_, g * 64:(g + 1) * 64], PTp[0:NC_, u % 2, 1024 + gi * 128:1024 + (gi + 1) * 128], start=True, stop=False, tile_position=(0, 64 * gi))
                    for br, col in enumerate((COL_S, COL_W)):
                        for k in range(t + 1):
                            c = br * (t + 1) + k
                            last = nc.tensor.matmul(o, Z[:, k, col + 256 + g * 64:col + 256 + (g + 1) * 64], PTp[:, u % 2, gi * 512 + c * 128:gi * 512 + (c + 1) * 128],
                                                    start=False, stop=(br == 1 and k == t), tile_position=(0, 64 * gi))
                last.then_inc(s_o, 1)
            pe.wait_ge(s_oc, len(UNITS))

            def s_keys(b):
                pe.wait_ge(s_kvp[b % 2], 48 * (b // 2 + 1))
                wait(pe, s_ktA, b)
                wait(pe, s_ktD, b)
                for br in range(2):
                    for gp in range(2):
                        for j in range(2):
                            last = nc.tensor.transpose(PS[:, 4 + br, gp * 256 + j * 128:gp * 256 + (j + 1) * 128], kvpage[:, b % 2, br, j, gp * 128:(gp + 1) * 128], ident)
                last.then_inc(s_kt, 1)

            def s_scores(b):
                pe.wait_ge(s_ktA, b + 1)
                pe.wait_ge(s_ktD, b + 1)
                wait(pe, q_mx, b - 1)
                for g in range(4):
                    gp, gi = g // 2, g % 2
                    h, o = slice(64 * gi, 64 * gi + 64), slice(32 * g, 32 * g + 32)
                    q = QTs[h, gp, b, :]
                    kw = dict(start=True, stop=True, tile_position=(64 * gi, 32 * g))
                    for br in range(2):
                        bank = PS[o, 2 * (b % 2) + br, :]
                        nc.tensor.matmul(bank[:, 0:PAST], q, KTb[h, b % 2, br, gp, :], **kw)
                        nc.tensor.matmul(bank[:, PAST:PAST + TS], q, KT[h, br, gp, TP:TOK], **kw)
                    last = nc.tensor.matmul(bank[:, 320:440], q, KC[h, gp, 0:NS_C], **kw)
                last.then_inc(q_S, 1)
            s_keys(0)
            s_scores(0)
            for b in range(DB):
                if b + 1 < DB:
                    s_keys(b + 1)
                    s_scores(b + 1)
                pe.wait_ge(q_pn, b + 1)
                wait(pe, q_TA, b)
                wait(pe, q_TD, b)
                wait(pe, q_oc, 2 * b)
                P = Ps[:, b % 2, :]
                for k, at_ in enumerate((0, 128, 320, 448)):
                    nc.tensor.transpose(PS[:, 6, k * 128:(k + 1) * 128], P[:, at_:at_ + 128], ident)
                for k, at_ in enumerate((256, 576)):
                    nc.tensor.transpose(PS[0:TS, 7, k * 128:(k + 1) * 128], P[:, at_:at_ + TS], ident)
                nc.tensor.transpose(PS[0:NS_C, 7, 256:384], P[:, 640:760], ident).then_inc(q_T, 1)
                pe.wait_ge(q_TA, b + 1)
                pe.wait_ge(q_TD, 2 * b + 2)
                for g in range(4):
                    gp, gi = g // 2, g % 2
                    o = PS[64 * gi:64 * gi + 64, 7, 448 + gp * 32:448 + gp * 32 + 32]
                    pt = PTs[:, b % 2, :].rearrange("p (a b) -> p a b", a=7)[:, :, 32 * g:32 * g + 32]
                    v = slice(256 + g * 64, 256 + (g + 1) * 64)
                    steps = [(kvpage[:, b % 2, br, j, v], pt[:, 2 * br + j]) for br in range(2) for j in range(2)]
                    steps += [(Z[0:TS, 2, col + 256 + g * 64:col + 256 + (g + 1) * 64], pt[0:TS, 4 + br]) for br, col in enumerate((COL_S, COL_W))]
                    steps += [(VCs[0:NS_C, g * 64:(g + 1) * 64], pt[0:NS_C, 6])]
                    for i, (lhs, rhs) in enumerate(steps):
                        last = nc.tensor.matmul(o, lhs, rhs, start=(i == 0), stop=(i == len(steps) - 1), tile_position=(0, 64 * gi))
                last.then_inc(q_o, 1)
            pe.wait_ge(q_oc, 2 * DB)
            pe.wait_ge(s_bada, 32)

            for n in range(4):
                wait(pe, s_gb, 2 * n)
                for k in range(2):
                    last = nc.tensor.matmul(PS[:, 6 + k, :], selT[:, k, :], mod[:, 2 * D + n * SECTION:2 * D + (n + 1) * SECTION], start=True, stop=True)
                last.then_inc(s_gp, 1)
                wait(pe, s_x1, 3 * (n - 1))
                for p in range(4):
                    i = index[("out", n, p)]
                    need(i)
                    for t in range(TILES):
                        for j in range(KP):
                            c = KP * p + j
                            last = nc.tensor.matmul(PS[:, 3 * (n % 2) + t, :], OT[:, c, t * 128:(t + 1) * 128], ring[:, i % NSLOT, j, :],
                                                    start=(c == 0), stop=(c == NK - 1))
                    last.then_inc(s_free, 1)
            pe.wait_ge(s_gb, 8)
            for n in range(4):
                pe.wait_ge(s_x1, 12)
                wait(pe, s_h2, 3 * (n - 1))
                for m, chunk in enumerate((4, 3)):
                    for k in range(2):
                        last = nc.tensor.matmul(PS[:, 4 * (n % 2) + 2 * m + k, :], selT[:, k, :], mod[:, chunk * D + n * SECTION:chunk * D + (n + 1) * SECTION], start=True, stop=True)
                last.then_inc(s_m2, 1)
            pe.wait_ge(s_h2, 12)
            for c in range(NK):
                if c >= 8:
                    pe.wait_ge(s_htA if c % 2 == 0 else s_htD, (c - 8) // 2 + 1)
                for t in range(TILES):
                    n = 128 if t < 2 else TS
                    last = nc.tensor.transpose(PS[:, c % 8, t * 128:t * 128 + n], H2[0:n, t, c * 128:(c + 1) * 128], ident[0:n, 0:n])
                last.then_inc(s_ht, 1)
            pe.wait_ge(s_htA, 8)
            pe.wait_ge(s_htD, 8)
            for i in range(8):
                nc.tensor.matmul(PS[:, i, :], selT[:, i // 4, :], mod[:, 5 * D + (i % 4) * SECTION:5 * D + (i % 4 + 1) * SECTION], start=True, stop=True).then_inc(s_g2p, 1)
            pe.wait_ge(s_g2, 8)
            for n in range(4):
                wait(pe, s_qA, 4 * (n - 1))
                wait(pe, s_qD, 4 * (n - 1))
                for p in range(4):
                    i = index[("wq", n, p)]
                    need(i)
                    for m in range(4):
                        for j in range(KP):
                            c = KP * p + j
                            last = nc.tensor.matmul(PS[:, 4 * (n % 2) + m, 0:TOK], ring[:, i % NSLOT, j, m * 128:(m + 1) * 128], H2T[:, c, 0:TOK],
                                                    start=(c == 0), stop=(c == NK - 1))
                    last.then_inc(s_free, 1)
            pe.wait_ge(s_qA, 16)
            pe.wait_ge(s_qD, 16)
            for k in range(12):
                t = k // 4
                wait(pe, s_sc, k - 7)
                for i in range(4):
                    hp = 4 * (k % 4) + i
                    h, p = hp // 2, hp % 2
                    last = nc.tensor.matmul(PS[:, k % 8, i * 128:(i + 1) * 128], QPT[:, hp, t * 128:(t + 1) * 128], skT[:, p * PH + h, :], start=True, stop=True)
                last.then_inc(s_scp, 1)
            pe.wait_ge(s_sc, 12)
            pe.wait_ge(s_facc, 1)
            for n in range(4):
                last = nc.tensor.matmul(PS[0:TS, n, :], fold, acc[:, n * SECTION:(n + 1) * SECTION], start=True, stop=True)
            last.then_inc(s_fold, 1)

        @block.vector
        def _(dve):
            V = nc.vector
            V.memset(cT, 0.0).then_inc(s_stage, 1)
            dve.wait_ge(s_cst, 16)
            dve.wait_ge(s_pt_in, 16)
            link(V.tensor_scalar(pgf, pgi, float(PAGE), cst[:, C_PAGE:C_PAGE + 1], ALU.mult, ALU.add))
            V.tensor_copy(pgx, pgf).then_inc(s_pgx, 1)
            dve.wait_ge(s_cin, 32)
            dve.wait_ge(s_sig, 1)
            link(V.tensor_scalar(csig[0:9, :], csig[0:9, :], 1.0, None, ALU.add))
            link(V.reciprocal(csig[0:9, :], csig[0:9, :]))
            V.tensor_tensor(cin[0:9, :], cin[0:9, :], csig[0:9, :], ALU.mult).then_inc(s_silu, 1)
            dve.wait_ge(s_cps, 1)
            dve.wait_ge(s_stage, 1)
            V.tensor_copy(cT[:, :, 0:9], PS[:, 0, 0:144].rearrange("p (a b) -> p a b", b=9)).then_inc(s_cT, 1)
            dve.wait_ge(s_sq, 3)
            V.tensor_scalar(sumsq[:, 0:3], sumsq[:, 0:3], 1.0 / D, EPS, ALU.mult, ALU.add).then_inc(s_ms, 1)
            dve.wait_ge(s_rt, 1)
            V.reciprocal(rstd[:, 0:3], rstd[:, 0:3]).then_inc(s_rs, 1)
            dve.wait_ge(s_gT, 1)
            V.tensor_copy(psT, PS[:, 0, 16:24])
            link(V.tensor_copy(g1T, PS[:, 0, 0:16]))
            V.tensor_copy(stat[:, 0:1], g1T[:, 0:1]).then_inc(s_gTc, 1)
            dve.wait_ge(s_skp, 1)
            for i in range(4):
                last = V.tensor_copy(skT[:, 4 * i:4 * i + 4, :].rearrange("p a b -> p (a b)"), PS[:, 2 + i, :])
            last.then_inc(s_skc, 1)
            dve.wait_ge(s_m1, 1)
            bank = [PS[:, k, 0:272].rearrange("p (a b) -> p a b", b=17) for k in range(2)]
            V.tensor_copy(B1T, bank[0])
            V.scalar_tensor_tensor(out=A1T, in0=bank[1], scalar=1.0, in1=g1T.unsqueeze(2).to_broadcast([128, NK, 17]), op0=ALU.add, op1=ALU.mult).then_inc(s_m1c, 1)
            dve.wait_ge(s_m1c, 1)
            for c in range(NK):
                dve.wait_ge(s_xt, c + 1)
                o = hT[:, c, TP:384].rearrange("p (b t) -> p b t", t=DT)
                link(V.tensor_tensor(o, PS[:, 3 + c % 3, 0:128].rearrange("p (b t) -> p b t", t=DT), A1T[:, c, 0:16].unsqueeze(2).to_broadcast([128, 16, DT]), ALU.mult))
                V.tensor_tensor(o, o, B1T[:, c, 0:16].unsqueeze(2).to_broadcast([128, 16, DT]), ALU.add).then_inc(s_hD, 1)
            for n in range(NIN):
                used(dve, "in", n)
                V.tensor_copy(z_section(0, n), in_bank(0, n)).then_inc(s_zD, 1)
            dve.wait_ge(s_gexp, 3)
            dve.wait_ge(s_zA, 2 * NIN)
            link(V.tensor_scalar(Z[:, :, COL_GL:COL_GL + 48], Z[:, :, COL_GL:COL_GL + 48], 1.0, None, ALU.add))
            V.reciprocal(Z[:, :, COL_GL:COL_GL + 48], Z[:, :, COL_GL:COL_GL + 48])
            parts = [(0, 0, NH), (COL_S, NH, NKV), (COL_W, NH + NKV, NKV)]
            for t in range(TILES):
                for col, h0, n in parts:
                    v = Z[:, t, col:col + n * HD].rearrange("p (h d) -> p h d", d=HD)
                    last = V.tensor_tensor(sq_z[:, h0:h0 + n, :], v, v, ALU.mult)
                link(last)
                link(V.tensor_reduce(qkr[:, t, :], sq_z, X_AXIS, ALU.add))
            V.tensor_scalar(qkr, qkr, 1.0 / HD, EPS, ALU.mult, ALU.add).then_inc(s_zms, 1)
            dve.wait_ge(s_zrt, 1)
            link(V.reciprocal(qkr, qkr))
            for t in range(TILES):
                for col, h0, n in parts:
                    v = Z[:, t, col:col + n * HD].rearrange("p (h d) -> p h d", d=HD)
                    last = V.tensor_tensor(v, v, qkr[:, t, h0:h0 + n].unsqueeze(2).to_broadcast([128, n, HD]), ALU.mult)
            link(last)
            for t in range(TILES):
                for k, (col, h0, n) in enumerate(parts):
                    v = Z[:, t, col:col + n * HD].rearrange("p (h d) -> p h d", d=HD)
                    g = gq if k == 0 else gk[:, k, :]
                    last = V.tensor_tensor(v, v, g.unsqueeze(1).to_broadcast([128, n, HD]), ALU.mult)
            last.then_inc(s_norm, 1)
            dve.wait_ge(s_cmp, 2)
            for c, to in ((0, KC), (1, VCT)):
                for gp in range(2):
                    last = V.tensor_scalar(to[:, gp, :], PS[:, 4 + c, gp * 150:gp * 150 + 135], PS[:, 4 + c, gp * 150 + 135:gp * 150 + 136], None, ALU.add)
            last.then_inc(s_vct, 1)
            dve.wait_ge(s_vct, 1)
            kcf = KC.rearrange("p a b -> p (a b)")
            V.tensor_tensor(kc_sq, kcf, kcf, ALU.mult).then_inc(s_kc1, 1)
            dve.wait_ge(s_kcm, 1)
            V.tensor_scalar(kc_sq, PS[:, 6, 0:270], EPS, None, ALU.add).then_inc(s_kc2, 1)
            dve.wait_ge(s_kc3, 1)
            link(V.reciprocal(kc_sq, kc_sq))
            link(V.tensor_tensor(kcf, kcf, kc_sq, ALU.mult))
            V.tensor_scalar(kcf, kcf, gkc[:, 0:1], None, ALU.mult).then_inc(s_kc, 1)
            dve.wait_ge(s_vcp, 1)
            V.tensor_copy(VCs[0:NS_C, :], PS[0:NS_C, 7, 0:256])
            V.tensor_copy(VCp[0:NC_, :], PS[0:NC_, 7, 256:512]).then_inc(s_vc, 1)
            for t in range(TILES):
                n = 128 if t < 2 else TS
                dve.wait_ge(s_qt, t + 1)
                V.tensor_copy(KT[:, :, :, t * 128:t * 128 + n].rearrange("p a b c -> p (a b) c"),
                              PS[:, 3 * (t % 2) + 2, :].rearrange("p (a b) -> p a b", a=4)[:, :, 0:n]).then_inc(s_qtD, 1)
            dve.wait_ge(s_csc, 1)
            dve.wait_ge(s_bc, 16)
            for gi in range(2):
                last = V.tensor_tensor(PC[:, gi], PS[:, 6 + gi, 0:16 * NC_].rearrange("p (a b) -> p a b", a=16), biasC[:, gi], ALU.add)
            link(last)
            cmax = stat[:, 0:32].rearrange("p (a b) -> p a b", a=2)
            link(V.tensor_reduce(cmax, PC, X_AXIS, ALU.max))
            V.tensor_tensor(PC.rearrange("p a b c -> p (a b) c"), PC.rearrange("p a b c -> p (a b) c"), stat[:, 0:32].unsqueeze(2).to_broadcast([128, 32, NC_]), ALU.subtract).then_inc(s_cmx, 1)
            dve.wait_ge(s_cex, 1)
            link(V.tensor_reduce(cmax, PC, X_AXIS, ALU.add))
            link(V.reciprocal(stat[:, 0:32], stat[:, 0:32]))
            for gi in range(2):
                for t in range(2):
                    gate = Z[:, t, COL_GL:COL_GL + 48].rearrange("p (gp gi r x) -> p gp gi r x", gp=2, gi=2, r=4)[:, :, gi, :, 0]
                    c = cmax[:, gi, t * 8:t * 8 + 8].rearrange("p (a b) -> p a b", a=2)
                    last = V.scalar_tensor_tensor(out=c, in0=gate, scalar=cst[:, C_VALID + t:C_VALID + t + 1], in1=c, op0=ALU.mult, op1=ALU.mult)
            link(last)
            V.tensor_tensor(PC.rearrange("p a b c -> p (a b) c"), PC.rearrange("p a b c -> p (a b) c"), stat[:, 0:32].unsqueeze(2).to_broadcast([128, 32, NC_]), ALU.mult).then_inc(s_pc, 1)
            for c in range(8):
                dve.wait_ge(s_dp, c + 1)
                V.tensor_copy(DTt[:, c, :], PS[:, c % 4, 0:TOK]).then_inc(s_dt, 1)

            dve.wait_ge(s_bp, 16)

            def p_max(u):
                t, gp, r = UNITS[u]
                nk = 128 * (t + 1)
                dve.wait_ge(s_S, u + 1)
                wait(dve, s_T, u - 1)
                for gi in range(2):
                    h = (2 * gp + gi) * GROUP + r
                    for br in range(2):
                        k = 2 * gi + br
                        last = V.tensor_tensor_reduce(out=Pp[:, u % 2, gi, br * nk:(br + 1) * nk], in0=PS[:, 2 * (u % 2) + gi, br * nk:(br + 1) * nk],
                                                      in1=biasP[:, h, 256 - nk:256], scale=1.0, scalar=-3.0e38, op0=ALU.add, op1=ALU.max, accum_out=mxv[:, u % 2, k:k + 1])
                link(last)
                V.tensor_scalar(nm[:, u % 2, 0:4], mxv[:, u % 2, 0:4], -SC_QK, None, ALU.mult).then_inc(s_mx, 1)
            p_max(0)
            for u, (t, gp, r) in enumerate(UNITS):
                nk = 128 * (t + 1)
                if u + 1 < len(UNITS):
                    p_max(u + 1)
                dve.wait_ge(s_exp, 4 * u + 4)
                link(V.reciprocal(sm[:, u % 2, 0:4], sm[:, u % 2, 0:4]))
                gate = Z[:, t, COL_GL:COL_GL + 48].rearrange("p (gp gi r x) -> p gp gi r x", gp=2, gi=2, r=4)[:, gp, :, r, 1:3]
                s4 = sm[:, u % 2, 0:4].rearrange("p (a b) -> p a b", a=2)
                link(V.tensor_tensor(s4, s4, gate, ALU.mult))
                for k in range(4):
                    v = Pp[:, u % 2, k // 2, (k % 2) * nk:(k % 2 + 1) * nk]
                    last = V.tensor_scalar(v, v, sm[:, u % 2, k:k + 1], None, ALU.mult)
                last.then_inc(s_pn, 1)
                dve.wait_ge(s_T, u + 1)
                n = 256 * (t + 1)
                V.tensor_copy(PTp[:, u % 2, 512:512 + n], PS[:, 5, 0:n]).then_inc(s_TD, 1)

            dve.wait_ge(s_bs, 32)
            dve.wait_ge(s_gsi, 16 * NH)

            def kt_out(b):
                dve.wait_ge(s_kt, b + 1)
                V.tensor_copy(KTb[:, b % 2, 1], PS[:, 5, :].rearrange("p (a b) -> p a b", a=2)).then_inc(s_ktD, 1)

            def s_max(b):
                dve.wait_ge(q_S, b + 1)
                wait(dve, q_T, b - 1)
                src = [PS[:, 2 * (b % 2), 0:320], PS[:, 2 * (b % 2) + 1, 0:320], PS[:, 2 * (b % 2) + 1, 320:440]]
                bias = [biasS[:, b], biasS[:, b], biasCS[:, b]]
                for k, (lo, hi) in enumerate(SPANS):
                    last = V.tensor_tensor_reduce(out=Ps[:, b % 2, lo:hi], in0=src[k], in1=bias[k], scale=1.0, scalar=-3.0e38, op0=ALU.add, op1=ALU.max, accum_out=mxv[:, b % 2, k:k + 1])
                link(last)
                V.tensor_scalar(nm[:, b % 2, 0:3], mxv[:, b % 2, 0:3], -SC_QK, None, ALU.mult).then_inc(q_mx, 1)
            kt_out(0)
            s_max(0)
            for b in range(DB):
                if b + 1 < DB:
                    kt_out(b + 1)
                    s_max(b + 1)
                dve.wait_ge(q_exp, 3 * b + 3)
                link(V.reciprocal(sm[:, b % 2, 0:3], sm[:, b % 2, 0:3]))
                for k, x in enumerate((1, 2, 0)):
                    last = V.tensor_tensor(sm[:, b % 2, k:k + 1], sm[:, b % 2, k:k + 1], gates_s[:, b, x:x + 1], ALU.mult)
                link(last)
                for k, (lo, hi) in enumerate(SPANS):
                    last = V.tensor_scalar(Ps[:, b % 2, lo:hi], Ps[:, b % 2, lo:hi], sm[:, b % 2, k:k + 1], None, ALU.mult)
                last.then_inc(q_pn, 1)
                dve.wait_ge(q_T, b + 1)
                V.tensor_copy(PTs[0:TS, b % 2, 512:768], PS[0:TS, 7, 0:256]).then_inc(q_TD, 1)
                V.tensor_copy(PTs[0:NS_C, b % 2, 768:896], PS[0:NS_C, 7, 256:384]).then_inc(q_TD, 1)

            dve.wait_ge(s_x1in, 48)
            for n in range(4):
                used(dve, "out", n)
                dve.wait_ge(s_gb, 2 * n + 2)
                for t in range(TILES):
                    last = V.tensor_tensor(TMP[:, t], PS[:, 3 * (n % 2) + t, :], GB[:, n % 2, t // 2], ALU.mult)
                link(last)
                for t in range(TILES):
                    v = X1[:, t, n * SECTION:(n + 1) * SECTION]
                    V.tensor_tensor(v, v, TMP[:, t], ALU.add).then_inc(s_x1, 1)
                dve.wait_ge(s_x1, 3 * n + 3)
            dve.wait_ge(s_sq2, 3)
            V.tensor_scalar(sumsq[:, 0:3], sumsq[:, 0:3], 1.0 / D, EPS, ALU.mult, ALU.add).then_inc(s_ms2, 1)
            dve.wait_ge(s_rt2, 1)
            link(V.reciprocal(rstd[:, 0:3], rstd[:, 0:3]))
            dve.wait_ge(s_g2in, 16)
            for n in range(4):
                cols = slice(n * SECTION, (n + 1) * SECTION)
                b0 = 4 * (n % 2)
                dve.wait_ge(s_m2, n + 1)
                for k in range(2):
                    last = V.scalar_tensor_tensor(out=TMP[:, 2 * (n % 2) + k], in0=PS[:, b0 + k, :], scalar=1.0, in1=g2b[:, cols], op0=ALU.add, op1=ALU.mult)
                link(last)
                for t in range(TILES):
                    last = V.scalar_tensor_tensor(out=H2[:, t, cols], in0=X1[:, t, cols], scalar=rstd[:, t:t + 1], in1=TMP[:, 2 * (n % 2) + t // 2], op0=ALU.mult, op1=ALU.mult)
                link(last)
                for t in range(TILES):
                    V.tensor_tensor(H2[:, t, cols], H2[:, t, cols], PS[:, b0 + 2 + t // 2, :], ALU.add).then_inc(s_h2, 1)
            for c in range(1, NK, 2):
                dve.wait_ge(s_ht, c + 1)
                V.tensor_copy(H2T[:, c, 0:TOK], PS[:, c % 8, 0:TOK]).then_inc(s_htD, 1)
            dve.wait_ge(s_g2, 8)
            for i in range(1, HP, 2):
                used(dve, "wq", i // 4)
                V.tensor_copy(QPT[:, i, 0:TOK], PS[:, i % 8, 0:TOK]).then_inc(s_qD, 1)
                V.tensor_copy(QPT[:, i, TOK:384], PS[:, i % 8, TP:TOK]).then_inc(s_qD, 1)

            dve.wait_ge(s_sc, 12)

            def top16(vals, val, idx, n):
                for lo in (0, 8):
                    for i in range(n):
                        last = V.max(val[:, i, lo:lo + 8], vals[i])
                    link(last)
                    for i in range(n):
                        last = V.max_index(idx[:, i, lo:lo + 8], val[:, i, lo:lo + 8], vals[i])
                    if lo == 0:
                        link(last)
                        for i in range(n):
                            last = V.match_replace(vals[i], val[:, i, 0:8], vals[i], -3.0e38)
                    link(last)

            def experts(t):
                top16([SC[:, t, i, :] for i in range(HP)], val1, idx1, HP)
                link(V.tensor_copy(idx1f, idx1))
                v1 = val1.rearrange("p (h two) k -> p h two k", two=2)
                i1 = idx1f.rearrange("p (h two) k -> p h two k", two=2)
                shape = [128, PH, TOPK, TOPK]
                link(V.tensor_tensor(cand, v1[:, :, 0, :].unsqueeze(3).to_broadcast(shape), v1[:, :, 1, :].unsqueeze(2).to_broadcast(shape), ALU.add))
                top16([cand[:, h].rearrange("p a b -> p (a b)") for h in range(PH)], val2, idx2, PH)
                V.tensor_scalar(ab_i[:, 0], idx2, 4, None, ALU.logical_shift_right)
                link(V.tensor_scalar(ab_i[:, 1], idx2, 15, None, ALU.bitwise_and))
                link(V.tensor_copy(ab_f, ab_i))
                for half in range(2):
                    link(V.tensor_tensor(onehot, iota.unsqueeze(1).unsqueeze(1).to_broadcast(shape), ab_f[:, half].unsqueeze(3).to_broadcast(shape), ALU.is_equal))
                    link(V.tensor_tensor(onehot, onehot, i1[:, :, half, :].unsqueeze(2).to_broadcast(shape), ALU.mult))
                    link(V.tensor_reduce(picked[:, half], onehot, X_AXIS, ALU.add))
                link(V.scalar_tensor_tensor(out=eid[:, t], in0=picked[:, 0], scalar=float(PK), in1=picked[:, 1], op0=ALU.mult, op1=ALU.add))
                V.tensor_tensor(gw[:, t], val2, val2[:, :, 0:1].to_broadcast([128, PH, TOPK]), ALU.subtract).then_inc(s_e2, 1)
                dve.wait_ge(s_e2x, t + 1)
                link(V.tensor_reduce(smax, gw[:, t], X_AXIS, ALU.add))
                link(V.reciprocal(smax, smax))
                link(V.tensor_tensor(gw[:, t], gw[:, t], smax.unsqueeze(2).to_broadcast([128, PH, TOPK]), ALU.mult))
            for t in range(TILES):
                experts(t)
            e2, g2 = eid[:, 2].rearrange("p a b -> p (a b)"), gw[:, 2].rearrange("p a b -> p (a b)")
            for dst, src in ((eid_s, e2), (gw_s, g2)):
                V.tensor_copy(dst[0:TS, :], src[0:TS, 0:64])
                last = V.tensor_copy(dst[TS:128, :], src[TS:128, 64:128])
            last.then_inc(s_eid, 1)
            dve.sem_inc(s_rowfree, HANDED)

            for ph, (kind, t) in enumerate(PHASES):
                base = BASE[ph]
                if kind == "u":
                    with dve.Fori(0, NROWS[t] // 16, 1) as it:
                        for s in range(16):
                            dve.wait_ge(s_row[s % 8], (it * 2 + base // 8 + s // 8) * 16 + 16)
                            V.tensor_tensor_reduce(out=rows_ring[:, s % 8, :], in0=rows_ring[:, s % 8, :], in1=H2[:, t, :], scale=1.0, scalar=0.0,
                                                   op0=ALU.mult, op1=ALU.add, accum_out=stage_a[:, s:s + 1]).then_inc(s_rowfree, 1)
                        dve.wait_ge(s_rowfree, it * 16 + (base + 16 + HANDED))
                        V.tensor_copy(dots[:, t, bass.ds(it * 16, 16)], stage_a).then_inc(s_stage, 1)
                        dve.wait_ge(s_stage, it + (base_copy(ph) + 2))
                    dve.sem_inc(s_dots, 1)
                else:
                    n = NROWS[t]
                    dve.wait_ge(s_gelu, t + 1)
                    g = gw[:, t].rearrange("p a b -> p (a b)") if t < 2 else gw_s
                    link(V.tensor_tensor(wgt[:, t, 0:n], dots[:, t, 0:n], g, ALU.mult))
                    wait(dve, s_yst, 16 * t)
                    link(V.memset(acc, 0.0))
                    with dve.Fori(0, n // 16, 1) as it:
                        V.tensor_copy(stage_w, wgt[:, t, bass.ds(it * 16, 16)]).then_inc(s_stage, 1)
                        dve.wait_ge(s_stage, it + (base_copy(ph) + 2))
                        for s in range(16):
                            dve.wait_ge(s_row[s % 8], (it * 2 + base // 8 + s // 8) * 16 + 16)
                            V.scalar_tensor_tensor(out=acc, in0=rows_ring[:, s % 8, :], scalar=stage_w[:, s:s + 1], in1=acc, op0=ALU.mult, op1=ALU.add).then_inc(s_rowfree, 1)
                            dve.wait_ge(s_rowfree, it * 16 + (base + s + 1 + HANDED))
                    if t == 2:
                        dve.sem_inc(s_facc, 1)
                        dve.wait_ge(s_fold, 1)
                        for n4 in range(4):
                            last = V.tensor_tensor(acc[0:TS, n4 * SECTION:(n4 + 1) * SECTION], PS[0:TS, n4, :], GB2[0:TS, 1, n4 * SECTION:(n4 + 1) * SECTION], ALU.mult)
                        link(last)
                        V.tensor_tensor(acc[0:TS, :], acc[0:TS, :], X1[0:TS, 2, :], ALU.add).then_inc(s_y, 1)
                    else:
                        link(V.tensor_tensor(acc, acc, GB2[:, 0, :], ALU.mult))
                        V.tensor_tensor(acc, acc, X1[:, t, :], ALU.add).then_inc(s_y, 1)


_INS = ["x_prompt", "x_sample", "cache_kv_cmp", "cache_kv_slc", "cache_kv_win", "state_pool", "page_table", "c_prompt", "c_sample",
        "w_ada", "b_ada", "g_norm1", "g_norm2", "w_in", "w_out", "g_qnorm", "g_knorm", "cmp_pe", "w_cmp", "w_pool", "pool_scale",
        "peer_wq", "peer_subkeys", "peer_u", "peer_v"]
_OUTS = [("y_prompt", (1, TP, D)), ("y_sample", (DB, DT, D)),
         ("cmp_prompt", (1, TP, 2, NKV, HD)), ("slc_prompt", (1, TP, 2, NKV, HD)), ("win_prompt", (1, TP, 2, NKV, HD)), ("pool_prompt", (1, POOL_BUF, POOL_W)),
         ("cmp_sample", (DB, DT, 2, NKV, HD)), ("slc_sample", (DB, DT, 2, NKV, HD)), ("win_sample", (DB, PAST, 2, NKV, HD)), ("pool_sample", (DB, POOL_BUF, POOL_W))]


def kernel(**inputs):
    import concourse.bacc as bacc
    from concourse.bass_utils import run_bass_kernel_spmd
    nc = bacc.Bacc("TRN2", target_bir_lowering=False, num_devices=1)
    arrays, ins, outs = {}, {}, {}
    for name, a in [(n, np.ascontiguousarray(inputs[n])) for n in _INS] + list(constants().items()):
        arrays[f"in_{name}"] = a
        ins[name] = nc.dram_tensor(f"in_{name}", a.shape, mybir.dt.from_np(a.dtype), kind="ExternalInput").ap()
    for name, shape in _OUTS:
        outs[name] = nc.dram_tensor(f"out_{name}", shape, F32, kind="ExternalOutput").ap()
    scratch = nc.dram_tensor("gates_scratch", (TS, 3 * NH), F32).ap()
    build(nc, ins, outs, scratch)
    r = run_bass_kernel_spmd(nc, [arrays], core_ids=[0])
    return tuple(r.results[0][f"out_{name}"] for name, _ in _OUTS)
```

```python
import numpy as np

import concourse.bass as bass
from concourse import mybir
from contextlib import ExitStack

F32 = mybir.dt.float32
I32 = mybir.dt.int32
U32 = mybir.dt.uint32
ALU = mybir.AluOpType
ACT = mybir.ActivationFunctionType
X_AXIS = mybir.AxisListType.X

D = 2048
NK = D // 128
TP = 256
DB, DT = 8, 8
TS = DB * DT
TOK = TP + TS
TILES = 3
PAST, PAGE = 256, 128
HD, NKV, GROUP = 64, 4, 4
NH = NKV * GROUP
NSA_W = NH * HD
KVW = NKV * HD
POOL_W = D - NSA_W
POOL_SIZES = (2, 4, 8, 16)
POOL_GW = POOL_W // 4
POOL_BUF = 15
CMP_BLOCK, CMP_STRIDE = 32, 16
NC_ = (TP - CMP_BLOCK) // CMP_STRIDE + 1
NS_C = DB * NC_
NSEQ = DB + 2
IN_COLS = NSA_W + 6 * KVW + 3 * NH + POOL_W
COL_C, COL_S, COL_W = NSA_W, NSA_W + 2 * KVW, NSA_W + 4 * KVW
COL_GL = NSA_W + 6 * KVW
COL_U = COL_GL + 3 * NH
PH, PK, TOPK = 8, 128, 16
HP = 2 * PH
EPS = 1e-6
SC_QK = HD ** -0.5
MASKED = -1e30
NSLOT = 8
N_PHYS = (DB * (PAST // PAGE) * 5) // 4
NROW = 6
GROUPS = [[0], [1, 2]]
WQ_PAUSE = 12
LOOP_ROW0 = 2 * 128 - NROW
SECTION = 512
KP = 4

C_ID, C_BLK, C_SELF, C_SELT, C_FOLD, C_IOTA, C_VALID, C_PAGE, C_ROW9 = 0, 128, 256, 280, 536, 600, 616, 618, 619
C_N = 620


def constants():
    c = np.zeros((128, C_N), np.float32)
    p = np.arange(128)
    c[p, C_ID + p] = 1.0
    c[:, C_BLK:C_BLK + 128] = (p[:, None] // 64 == p[None, :] // 64) / 64.0
    for j in range(4):
        for b in range(DB):
            c[32 * j + b, C_SELF + b] = c[32 * j + b, C_SELF + DB + b] = 1.0
        c[32 * j + DB, C_SELF + 2 * DB] = 1.0
        c[32 * j + DB, C_SELT:C_SELT + 128] = 1.0
        for m in range(128):
            c[32 * j + (m % TS) // DT, C_SELT + 128 + m] = 1.0
    c[DB + 1, C_SELF:C_SELF + 2 * DB + 1] = 1.0
    c[DB + 1, C_SELT:C_SELT + 256] = 1.0
    c[p, C_FOLD + p % 64] = 1.0
    c[:, C_IOTA:C_IOTA + 16] = np.arange(16)
    c[:, C_VALID] = p >= CMP_BLOCK - 1
    c[:, C_VALID + 1] = 1.0
    c[:, C_PAGE] = p
    c[DB + 1, C_ROW9] = 1.0
    slopes = (2.0 ** (-8.0 * np.arange(1, NH + 1) / NH)).astype(np.float32)
    inv = 1.0 / SC_QK
    q, k = np.arange(128), np.arange(256)
    dist = (128 + q[:, None] - k[None, :])
    bias = np.where(dist[:, None] >= 0, -inv * slopes[None, :, None] * dist[:, None], MASKED)
    pos_c = np.arange(NC_) * CMP_STRIDE + CMP_BLOCK - 1
    bc = np.zeros((128, 2, 2, 8, NC_), np.float32)
    for gi in range(2):
        for t in range(2):
            for gp in range(2):
                for r in range(GROUP):
                    dc = 128 * t + q[:, None] - pos_c[None, :]
                    s = slopes[(2 * gp + gi) * GROUP + r]
                    bc[:, gi, t, gp * 4 + r] = np.where(dc >= 0, -inv * s * dc, MASKED)
    rows = np.arange(128)
    s_row, t_row = slopes[rows // DT], rows % DT
    bs = np.full((128, DB, PAST + TS), MASKED, np.float64)
    bcs = np.full((128, DB, NS_C), MASKED, np.float64)
    for b in range(DB):
        bs[:, b, :PAST] = -inv * s_row[:, None] * (PAST + t_row[:, None] - np.arange(PAST)[None])
        dn = t_row[:, None] - np.arange(DT)[None]
        bs[:, b, PAST + b * DT:PAST + (b + 1) * DT] = np.where(dn >= 0, -inv * s_row[:, None] * dn, MASKED)
        bcs[:, b, b * NC_:(b + 1) * NC_] = -inv * s_row[:, None] * (PAST + t_row[:, None] - pos_c[None])
    pool = np.zeros((128, 4, 3 * 128 + 128), np.float32)
    for i, w in enumerate(POOL_SIZES):
        for t in range(TP):
            cnt = min(w, t + 1)
            for s in range(max(0, t - w + 1), t + 1):
                v = 1.0 / cnt - (s == t)
                if t < 128:
                    pool[s, i, t] = v
                elif s < 128:
                    pool[s, i, 128 + t - 128] = v
                else:
                    pool[s - 128, i, 256 + t - 128] = v
        for b in range(DB):
            for t in range(DT):
                for s in range(t - w + 1, t + 1):
                    v = 1.0 / w - (s == t)
                    if s < 0:
                        pool[b * POOL_BUF + POOL_BUF + s, i, 384 + b * DT + t] = v
                    else:
                        pool[b * DT + s, i, 448 + b * DT + t] = v
    f = lambda a: np.ascontiguousarray(a, dtype=np.float32)
    return {"k_const": c, "k_bias": f(bias.reshape(128, -1)), "k_bias_c": f(bc.reshape(128, -1)),
            "k_bias_s": f(bs.reshape(128, -1)), "k_bias_cs": f(bcs.reshape(128, -1)),
            "k_pool": f(pool.reshape(128, -1))}


def build(nc, I, O, scratch):
    ctx = ExitStack()
    with ctx:
        arena = ctx.enter_context(nc.sbuf_tensor("arena", [128, 53200], F32))
        PS = ctx.enter_context(nc.psum_tensor("PS", [128, 8, 512], F32))

        def sem(name):
            return ctx.enter_context(nc.semaphore(name))

        def view(at, *dims):
            n = int(np.prod(dims))
            v = arena[:, at:at + n]
            if len(dims) == 1:
                return v
            names = "abcde"[:len(dims)]
            return v.rearrange(f"p ({' '.join(names)}) -> p {' '.join(names)}",
                               **{k: d for k, d in zip(names[1:], dims[1:])})

        R_MOD, R_RING, R_H, R_Z, R_P = 0, 12288, 28672, 34816, 45712
        mod = view(R_MOD, 6 * D)
        ring = view(R_RING, NSLOT, KP, SECTION)
        hT = view(R_H, NK, 3 * 128)
        Z = view(R_Z, TILES, IN_COLS)
        X = view(R_Z, TILES, D)
        at = [R_P]

        def keep(*dims):
            v = view(at[0], *dims)
            at[0] += int(np.prod(dims))
            return v
        cst = keep(C_N)
        ident, blk = cst[:, C_ID:C_ID + 128], cst[:, C_BLK:C_BLK + 128]
        selF = cst[:, C_SELF:C_SELF + 17]
        selT = cst[:, C_SELT:C_SELT + 256].rearrange("p (a b) -> p a b", a=2)
        fold = cst[:, C_FOLD:C_FOLD + 64]
        iota = cst[:, C_IOTA:C_IOTA + 16]
        sumsq, rstd = keep(4), keep(4)
        early_at = at[0]
        A1T, B1T = keep(NK, 17), keep(NK, 17)
        g1T = keep(NK)
        gq, gk = keep(HD), keep(3, HD)
        gkc = keep(1)
        psT = keep(8)
        cT = keep(NK, 32)
        eid = view(early_at, TILES, PH, TOPK).bitcast(I32)
        gw = view(early_at + 384, TILES, PH, TOPK)
        dots = view(early_at + 768, TILES, 128)
        eid_s = view(early_at + 1152, 64).bitcast(I32)
        gw_s = view(early_at + 1216, 64)
        idxs = view(early_at + 1280, 2, 8).bitcast(I32)
        stage_a = view(early_at + 1296, 16)
        stage_w = view(early_at + 1312, 16)
        assert early_at + 1328 <= at[0]
        skT = keep(HP, PK)
        KC = keep(2, 9 * NC_)
        VCp = keep(256)
        stat = keep(128)
        qkr = keep(3, 24)
        mxv, nm, sm = keep(2, 4), keep(2, 4), keep(2, 4)
        gates_s = keep(DB, 3)
        pgf = keep(16)
        pgi = keep(16).bitcast(I32)
        pgx = keep(16).bitcast(I32)
        vg_at = at[0]
        VK = keep(TILES, 2, KVW)
        GK = keep(TILES, 3 * NH)
        biasC = keep(2, 16, NC_)
        PC = keep(2, 16, NC_)
        biasCS = view(vg_at + TILES * (2 * KVW + 3 * NH), DB, NS_C)
        acc = view(vg_at, D)
        assert at[0] <= 53200, at[0]
        cin = view(R_H, D)
        csig = view(R_H + D, D)
        sk_raw = view(R_H + 2 * D, HP, 128)
        sq_junk = view(R_Z + 3 * D, D)
        g1_raw = view(R_Z + 4 * D, 128)
        ps_raw = view(R_Z + 4 * D + 128, 128)
        QT = view(R_MOD, 8, TP)
        QTs = view(R_MOD + 8 * TP, 2, DB, 4 * DT)
        KT = view(R_MOD + 8 * TOK, 2, 2, TOK)
        VCs = view(R_MOD + 8 * TOK + 4 * TOK, 256)
        CT = view(R_RING, 4, NSEQ, 256)
        WC = [view(R_RING + 10240, 2, CMP_BLOCK, HD), view(R_H, 2, CMP_BLOCK, HD)]
        cpage = view(R_RING + 14336, 4, 512)
        sq_z = view(R_H + 4096, 24, HD)
        VCT = view(R_H + 4096, 2, 9 * NC_)
        kc_sq = view(R_H + 4096 + 300, 2 * 9 * NC_)
        pe_raw = view(R_H + 5632, 512)
        poolB = view(R_RING, 4, 512)
        past_u = view(R_RING + 2048, POOL_W)
        WP = view(R_RING + 3072, 4, 2, POOL_GW)
        DTt = view(R_RING + 5120, 8, TOK)
        g2b = view(R_RING + 7680, D)
        OT = view(R_H, NK, 3 * 128)
        biasP = view(R_Z, NH, 256)
        Pp = view(R_Z + 4096, 2, 2, 512)
        PTp = view(R_Z + 6144, 2, 1280)
        biasS = view(R_Z, DB, PAST + TS)
        kvpage = [view(R_Z + 2560, 2, 2, 512), view(R_MOD, 2, 2, 512)]
        KTb = view(R_Z + 4608, 2, 2, 2, 256)
        Ps = view(R_Z + 6656, 2, 760)
        PTs = view(R_Z + 8176, 2, 7 * 128)
        rows_ring = view(R_RING, NROW, D)
        loop_row = [view(R_Z, D), view(R_Z + D, D)] + [rows_ring[:, (LOOP_ROW0 + i) % NROW, :] for i in range(NROW)]
        X1_0, H2_0 = view(R_RING + NROW * D, D), view(R_RING + (NROW + 1) * D, D)
        H2T_0 = view(R_RING + 4 * D, NK, 128)
        QPT_0 = view(R_RING + 5 * D, NK, 128)
        GB_0, TMP_0 = view(R_RING + (NROW + 1) * D, 2, SECTION), view(R_RING + (NROW + 1) * D + 2 * SECTION, 1, SECTION)
        X1_12 = view(R_MOD, 2, D)
        ring2 = view(R_Z, 4, KP, SECTION)
        GB_12, TMP_12 = view(R_Z + 4 * D, 2, SECTION), view(R_Z + 4 * D + 2 * SECTION, 2, SECTION)
        H2_12 = view(R_H, 2, D)
        H2T_12 = view(R_MOD + 4096, NK, 256)
        QPT_12 = [view(R_MOD + 8192, 8, 256), view(R_H + 4096, 8, 256)]
        GB2 = view(R_MOD + 4096, 2, D)

        def x1(t):
            return X1_0 if t == 0 else X1_12[:, t - 1]

        def h2(t):
            return H2_0 if t == 0 else H2_12[:, t - 1]

        def scratch_of(group):
            base = R_RING if group == 0 else R_Z
            n = len(GROUPS[group])
            sc = view(base, n, HP, PK)
            o = base + n * 2048
            k = o + 4096
            return dict(sc=sc, cand=view(o, PH, TOPK, TOPK), onehot=view(o + 2048, PH, TOPK, TOPK),
                        val1=view(k, HP, TOPK), idx1=view(k + 256, HP, TOPK).bitcast(U32), idx1f=view(k + 512, HP, TOPK),
                        val2=view(k + 768, PH, TOPK), idx2=view(k + 896, PH, TOPK).bitcast(U32), ab_i=view(k + 1024, 2, PH, TOPK).bitcast(U32),
                        ab_f=view(k + 1280, 2, PH, TOPK), picked=view(k + 1536, 2, PH, TOPK))

        s_cst, s_cin, s_x, s_sk, s_gain = sem("consts_in"), sem("cond_in"), sem("x_in"), sem("subkeys_in"), sem("gains_in")
        s_piece = [sem(f"piece_in{i}") for i in range(NSLOT)]
        s_piece2 = [sem(f"second_piece_in{i}") for i in range(4)]
        s_free = sem("piece_used")
        s_sig, s_silu, s_cps, s_cT = sem("sigma_ready"), sem("silu_ready"), sem("cond_T_psum"), sem("cond_T_ready")
        s_adaC, s_bada = sem("ada_copied"), sem("bias_ada_in")
        s_sq, s_ms, s_rt, s_rs, s_xn = sem("squares"), sem("mean_sq"), sem("root"), sem("rstd"), sem("x_normed")
        s_gT, s_gTc = sem("gain_T_psum"), sem("gain_T")
        s_m1, s_m1c = sem("mod1_psum"), sem("mod1_ready")
        s_xt, s_hA, s_hD = sem("x_T_psum"), sem("h_prompt_ready"), sem("h_sample_ready")
        s_zA, s_zD = sem("z_tiles12_ready"), sem("z_tile0_ready")
        s_gexp, s_zms, s_zrt, s_norm = sem("gate_exp"), sem("z_mean_sq"), sem("z_root"), sem("qk_normed")
        s_wc, s_pe, s_ctz, s_pt_in, s_pgi, s_pgx = sem("w_cmp_in"), sem("cmp_pe_in"), sem("cmp_zeroed"), sem("page_table_in"), sem("page_rows_f"), sem("page_rows")
        s_cpage = [sem(f"cmp_page_in{i}") for i in range(4)]
        s_ct, s_ctc, s_cmp = sem("cmp_T_psum"), sem("cmp_T"), sem("cmp_psum")
        s_kc1, s_kcm, s_kc2, s_kc3, s_kc = sem("kc_squares"), sem("kc_mean"), sem("kc_meaned"), sem("kc_root"), sem("kc_ready")
        s_vct, s_vcp, s_vc = sem("vc_T"), sem("vc_psum"), sem("vc_ready")
        s_qt, s_qtA, s_qtD = sem("qk_T_psum"), sem("q_T"), sem("k_T")
        s_plin, s_dp, s_dt, s_yp, s_yo = sem("pool_in"), sem("pool_d_psum"), sem("pool_d"), sem("pool_y_psum"), sem("pool_y")
        s_bp, s_bc, s_bs = sem("bias_prompt_in"), sem("bias_cmp_in"), sem("bias_sample_in")
        s_csc, s_cmx, s_cex, s_pc = sem("cmp_scores"), sem("cmp_shifted"), sem("cmp_exp"), sem("cmp_probs")
        s_S, s_mx, s_exp, s_pn = sem("scores"), sem("row_max"), sem("exps"), sem("probs")
        s_T, s_TA, s_TD, s_o, s_oc = sem("probs_T_psum"), sem("probs_T_a"), sem("probs_T_d"), sem("out_psum"), sem("out_ready")
        s_kvp = [sem("kv_page_in0"), sem("kv_page_in1")]
        s_a2 = sem("scale2_with_gain")
        s_gso, s_gsi = sem("gates_out"), sem("gates_in")
        s_kt, s_ktA, s_ktD = sem("cache_kT_psum"), sem("cache_ksT"), sem("cache_kwT")
        q_S, q_mx, q_exp, q_pn = sem("smp_scores"), sem("smp_row_max"), sem("smp_exps"), sem("smp_probs")
        q_T, q_TA, q_TD, q_o, q_oc = sem("smp_T_psum"), sem("smp_T_a"), sem("smp_T_d"), sem("smp_out_psum"), sem("smp_out")
        s_out = sem("outputs_stored")
        s_zout = sem("z_outputs_stored")
        s_x1in, s_vk = sem("x_again_in"), sem("values_kept")
        s_gp, s_gb, s_x1 = sem("gate1_psum"), sem("gate1"), sem("x1_ready")
        s_sq2, s_ms2, s_rt2 = sem("squares2"), sem("mean_sq2"), sem("root2")
        s_g2in, s_m2, s_h2 = sem("g_norm2_in"), sem("mod2_psum"), sem("h2_ready")
        s_ht, s_htA, s_htD = sem("h2_T_psum"), sem("h2_T_a"), sem("h2_T_d")
        s_g2p, s_g2 = sem("gate2_psum"), sem("gate2")
        s_qA, s_qD = sem("peer_q_a"), sem("peer_q_d")
        s_skp, s_skc = sem("subkeys_T_psum"), sem("subkeys_T")
        s_scp, s_sc = sem("peer_scores_psum"), sem("peer_scores")
        s_e2, s_e2x, s_eid = sem("expert_logits"), sem("expert_exp"), sem("experts_ready")
        s_row = [sem(f"row_in{i}") for i in range(NROW)]
        s_lrow = [sem(f"loop_row_in{i}") for i in range(8)]
        s_idx, s_rowfree, s_pdma = sem("row_indices"), sem("row_used"), sem("pool_dma_go")
        s_stage, s_dots, s_gelu, s_wgt = sem("dots_staged"), sem("dots_ready"), sem("gelu_ready"), sem("weights_staged")
        s_facc, s_fold, s_y, s_yst = sem("acc_ready"), sem("folded"), sem("y_ready"), sem("y_stored")
        dve_chain = sem("dve_chain")
        n_link = [0]

        def link(ins):
            n_link[0] += 1
            ins.then_inc(dve_chain, 1)
            nc.vector.wait_ge(dve_chain, n_link[0])

        def wait(eng, s, n):
            if n > 0:
                eng.wait_ge(s, n)

        ADA_N = 6 * D // SECTION
        ADA_FIRST = 8
        w_ada_v = I["w_ada"].rearrange("(c p) n -> p c n", p=128)
        w_in_v = I["w_in"].rearrange("(c p) n -> p c n", p=128)
        w_wq_v = I["peer_wq"].rearrange("(c p) n -> p c n", p=128)
        w_out_nsa = I["w_out"][0:NSA_W, :].rearrange("(gp gi r d) n -> gp gi d r n", gp=2, gi=2, r=4)
        w_out_pool = I["w_out"][NSA_W:D, :].rearrange("(c p) n -> p c n", p=128)
        IN_SEC = [0, 512, COL_C, COL_S, COL_W, COL_U, COL_U + 512]
        NIN = len(IN_SEC)
        ADA_WITH = [3, 3] + [2] * 5
        pieces = [("ada", s, p) for s in range(ADA_FIRST) for p in range(4)]
        ada_next = ADA_FIRST
        for n in range(NIN):
            pieces += [("in", n, p) for p in range(4)]
            for _ in range(ADA_WITH[n]):
                pieces += [("ada", ada_next, p) for p in range(4)]
                ada_next += 1
        assert ada_next == ADA_N
        pieces += [("gl", 0, 0)]
        n_early = len(pieces)
        for group in range(2):
            pieces += [("out", n, p, group) for n in range(4) for p in range(4)]
            pieces += [("wq", n, p, group) for n in range(4) for p in range(4)]
        n_first = n_early + 32
        index = {p: i for i, p in enumerate(pieces)}

        def slot(i):
            if i < n_early:
                return ring[:, i % NSLOT], s_piece[i % NSLOT]
            if i < n_first:
                return ring[:, (i - n_early) % 4], s_piece[(i - n_early) % 4]
            return ring2[:, (i - n_first) % 4], s_piece2[(i - n_first) % 4]

        def slot_key(i):
            return i % NSLOT if i < n_early else (i - n_early) % 4 if i < n_first else NSLOT + (i - n_first) % 4
        count, arrived = [0] * (NSLOT + 4), []
        for i, p in enumerate(pieces):
            count[slot_key(i)] += 32 if p[0] == "out" and p[2] < 2 else 16
            arrived.append(count[slot_key(i)])

        def used(eng, kind, n, p=3, *group):
            eng.wait_ge(s_free, index[(kind, n, p, *group)] + 1)

        gl_w = view(R_RING + (index[("gl", 0, 0)] % NSLOT) * KP * SECTION, NK, 48)

        def load_piece(eng, i):
            kind, n, p = pieces[i][:3]
            dst, done = slot(i)
            wait(eng, s_free, i - (NSLOT if i < n_early else 4) + 1)
            cols = slice(n * SECTION, (n + 1) * SECTION)
            if kind == "ada":
                eng.dma_start(dst, w_ada_v[:, KP * p:KP * p + KP, cols]).then_inc(done, 16)
            elif kind == "in":
                eng.dma_start(dst, w_in_v[:, KP * p:KP * p + KP, IN_SEC[n]:IN_SEC[n] + SECTION]).then_inc(done, 16)
            elif kind == "wq":
                eng.dma_start(dst, w_wq_v[:, KP * p:KP * p + KP, cols]).then_inc(done, 16)
            elif kind == "gl":
                eng.dma_start(gl_w, w_in_v[:, :, COL_GL:COL_GL + 48]).then_inc(done, 16)
            elif p < 2:
                for gi in range(2):
                    eng.dma_start(dst[64 * gi:64 * gi + 64], w_out_nsa[p, gi, :, :, cols]).then_inc(done, 16)
            else:
                eng.dma_start(dst, w_out_pool[:, KP * (p - 2):KP * (p - 2) + KP, cols]).then_inc(done, 16)

        CBLK = [("page", m // 2, m % 2) for m in range(16)] + [("prompt", DB, 0), ("prompt", DB, 1), ("pe", DB + 1, 0)]
        b_ada = I["b_ada"].rearrange("(a n) -> a n", a=1)
        b_row = slice(DB + 1, DB + 2)
        N_ZOUT = 6 + 2 + 1 + 2 * DB
        UNITS = [(t, gp, r) for t in range(2) for gp in range(2) for r in range(4)]
        SPANS = [(0, 320), (320, 640), (640, 760)]
        PHASES = [("u", 0), ("v", 0), ("u", 1), ("u", 2), ("v", 1), ("v", 2)]
        NROWS = [128, 128, 64]
        BASE = [sum(NROWS[t] for _, t in PHASES[:i]) for i in range(len(PHASES))]
        N_INLINE = 2
        LOOP_BASE = BASE[N_INLINE]

        def z_half(n, half):
            cols = slice(256 * half, 256 * half + 256)
            z = Z[0:TS, 2, IN_SEC[n]:IN_SEC[n] + SECTION]
            p = PS[64 * half:64 * half + 64, 3 * (n % 2) + 2, cols]
            if n >= 2:
                return z[:, cols], p
            return z.rearrange("p (r gi d) -> p gi r d", r=4, gi=2)[:, half], p.rearrange("p (r d) -> p r d", r=4)

        def z_section(t, n):
            v = Z[:, t, IN_SEC[n]:IN_SEC[n] + SECTION]
            return v.rearrange("p (r gi d) -> p gi r d", r=4, gi=2) if n < 2 else v

        def in_bank(t, n):
            v = PS[:, 3 * (n % 2) + t, :]
            return v.rearrange("p (gi r d) -> p gi r d", gi=2, r=4) if n < 2 else v

        block = ctx.enter_context(nc.Block())

        @block.sync
        def _(sp):
            sp.dma_start(cin[0:DB, :], I["c_sample"]).then_inc(s_cin, 16)
            sp.dma_start(cin[DB:DB + 1, :], I["c_prompt"]).then_inc(s_cin, 16)
            sp.dma_start(cst, I["k_const"]).then_inc(s_cst, 16)
            for i in range(n_early):
                if i == index[("ada", ADA_FIRST, 0)]:
                    sp.wait_ge(s_adaC, ADA_FIRST)
                    sp.dma_start(mod[b_row, 0:2 * D], b_ada[:, 0:2 * D]).then_inc(s_bada, 16)
                load_piece(sp, i)
                if i == 8:
                    xs = I["x_sample"].rearrange("b t d -> (b t) d")
                    sp.dma_start(X[:, 0:2, :], I["x_prompt"][0].rearrange("(t p) d -> p t d", p=128)).then_inc(s_x, 16)
                    sp.dma_start(X[0:TS, 2, :], xs).then_inc(s_x, 16)
                    sp.dma_start(X[TS:128, 2, :], xs).then_inc(s_x, 16)
                    sp.dma_start(g1_raw[0:NK, :], I["g_norm1"].rearrange("(c p) -> c p", p=128)).then_inc(s_gain, 16)
                    sp.dma_start(ps_raw[0:8, :], I["pool_scale"].rearrange("(c p) -> c p", p=128)).then_inc(s_gain, 16)
                    sp.dma_start(gq, I["g_qnorm"].rearrange("(a d) -> a d", a=1).to_broadcast([128, HD])).then_inc(s_gain, 16)
                    sp.dma_start(gk.rearrange("p a b -> p (a b)"), I["g_knorm"].rearrange("(a k) d -> a (k d)", a=1).to_broadcast([128, 3 * HD])).then_inc(s_gain, 16)
                    for gi in range(2):
                        sp.dma_start(gkc[64 * gi:64 * gi + 64, :], I["g_knorm"][0].rearrange("(d a) -> d a", a=1)).then_inc(s_gain, 16)
                    sp.dma_start(sk_raw, I["peer_subkeys"].rearrange("p h k d -> k (p h) d")).then_inc(s_sk, 16)
                    sp.dma_start(biasC.rearrange("p a b c -> p (a b c)"), I["k_bias_c"]).then_inc(s_bc, 16)
            sp.wait_ge(s_adaC, ADA_N)
            sp.dma_start(mod[b_row, 2 * D:6 * D], b_ada[:, 2 * D:6 * D]).then_inc(s_bada, 16)
            sp.wait_ge(s_free, n_early)
            wc = I["w_cmp"].rearrange("c (gp gi) l d e -> c gi gp d l e", gi=2)
            for c in range(2):
                for gi in range(2):
                    for gp in range(2):
                        sp.dma_start(WC[c][64 * gi:64 * gi + 64, gp], wc[c, gi, gp]).then_inc(s_wc, 16)
            for c in range(2):
                sp.dma_start(pe_raw[0:CMP_BLOCK, c * 256:(c + 1) * 256], I["cmp_pe"][c].rearrange("l g d -> l (g d)")).then_inc(s_pe, 16)
            sp.wait_ge(s_cmp, 2)
            sp.dma_start(poolB.rearrange("p a b -> p (a b)"), I["k_pool"]).then_inc(s_plin, 16)
            sp.dma_start(past_u[0:DB * POOL_BUF, :], I["state_pool"].rearrange("b s c -> (b s) c")).then_inc(s_plin, 16)
            for i in range(4):
                sp.dma_start(WP[:, i], I["w_pool"][i].rearrange("(c p) e -> p c e", p=128)).then_inc(s_plin, 16)
            sp.dma_start(g2b, I["g_norm2"].rearrange("(a d) -> a d", a=1).to_broadcast([128, D])).then_inc(s_g2in, 16)
            sp.wait_ge(s_yp, 8)
            sp.wait_ge(s_zout, 16 * N_ZOUT)
            sp.dma_start(biasP.rearrange("p a b -> p (a b)"), I["k_bias"]).then_inc(s_bp, 16)
            sp.wait_ge(s_a2, 1)
            for i in range(n_early, n_early + 4):
                load_piece(sp, i)
            sp.dma_start(X1_0, I["x_prompt"][0, 0:128, :]).then_inc(s_x1in, 16)
            for i in range(n_early + 4, n_first):
                load_piece(sp, i)
            sp.wait_ge(s_oc, 16)
            sp.dma_start(biasS.rearrange("p a b -> p (a b)"), I["k_bias_s"]).then_inc(s_bs, 16)
            sp.dma_start(biasCS.rearrange("p a b -> p (a b)"), I["k_bias_cs"]).then_inc(s_bs, 16)
            slc_rows = I["cache_kv_slc"].rearrange("n s c g d -> (n s) (c g d)")
            win_rows = I["cache_kv_win"].rearrange("b (j s) c g d -> b s j (c g d)", j=2)
            sp.wait_ge(s_pt_in, 16)
            for b in range(DB):
                wait(sp, q_o, b - 1)
                for j in range(2):
                    page = sp.value_load(pgi[0:1, 2 * b + j:2 * b + j + 1], min_val=0, max_val=N_PHYS - 1)
                    sp.dma_start(kvpage[b % 2][:, 0, j, :], slc_rows[bass.ds(page * PAGE, PAGE), :]).then_inc(s_kvp[b % 2], 16)
                sp.dma_start(kvpage[b % 2][:, 1], win_rows[b]).then_inc(s_kvp[b % 2], 16)
            sp.wait_ge(q_oc, 2 * DB)
            for i in range(n_first, n_first + 4):
                load_piece(sp, i)
            sp.dma_start(X1_12[:, 0, :], I["x_prompt"][0, 128:256, :]).then_inc(s_x1in, 16)
            sp.dma_start(X1_12[0:TS, 1, :], xs).then_inc(s_x1in, 16)
            sp.dma_start(X1_12[TS:128, 1, :], xs).then_inc(s_x1in, 16)
            for i in range(n_first + 4, len(pieces)):
                load_piece(sp, i)
            for t in range(2):
                sp.wait_ge(s_y, t + 1)
                sp.dma_start(O["y_prompt"][0, t * 128:(t + 1) * 128, :], acc).then_inc(s_yst, 16)
            sp.wait_ge(s_y, 3)
            sp.dma_start(O["y_sample"].rearrange("b t d -> (b t) d"), acc[0:TS, :]).then_inc(s_yst, 16)
            sp.wait_ge(s_yst, 48)
            sp.wait_ge(s_out, 32)

        @block.gpsimd
        def _(pool):
            pool.dma_start(O["win_sample"][:, 0:PAST - DT].rearrange("b s c g d -> b (s c g d)"),
                           I["cache_kv_win"][:, DT:PAST].rearrange("b s c g d -> b (s c g d)")).then_inc(s_out, 16)
            pool.dma_start(O["pool_sample"][:, 0:POOL_BUF - DT, :], I["state_pool"][:, DT:POOL_BUF, :]).then_inc(s_out, 16)
            pool.dma_start(pgi, I["page_table"].rearrange("(a b) j -> a (b j)", a=1).to_broadcast([128, 16])).then_inc(s_pt_in, 16)
            pool.wait_ge(s_free, n_early)
            nc.gpsimd.memset(CT[:, :, DB + 1, :], 0.0).then_inc(s_ctz, 1)
            cmp_rows = I["cache_kv_cmp"].rearrange("n s c g d -> (n s) (c g d)")
            pool.wait_ge(s_pgx, 1)
            for m in range(16):
                wait(pool, s_ct, m - 3)
                pool.indirect_dma_start(out=cpage[:, m % 4, :], out_offset=None, in_=cmp_rows,
                                        in_offset=bass.IndirectOffsetOnAxis(ap=pgx[:, m:m + 1], axis=0)).then_inc(s_cpage[m % 4], 16)
            pool.wait_ge(s_norm, 1)
            for t in range(2):
                for name, col in (("cmp_prompt", COL_C), ("slc_prompt", COL_S), ("win_prompt", COL_W)):
                    pool.dma_start(O[name][0, t * 128:(t + 1) * 128].rearrange("s c g d -> s (c g d)"), Z[:, t, col:col + 512]).then_inc(s_zout, 16)
            for name, col in (("cmp_sample", COL_C), ("slc_sample", COL_S)):
                pool.dma_start(O[name].rearrange("b t c g d -> (b t) (c g d)"), Z[0:TS, 2, col:col + 512]).then_inc(s_zout, 16)
            pool.dma_start(O["pool_prompt"][0], Z[128 - POOL_BUF:128, 1, COL_U:COL_U + POOL_W]).then_inc(s_zout, 16)
            for b in range(DB):
                pool.dma_start(O["win_sample"][b, PAST - DT:PAST].rearrange("s c g d -> s (c g d)"), Z[b * DT:b * DT + DT, 2, COL_W:COL_W + 512]).then_inc(s_zout, 16)
            for b in range(DB):
                pool.dma_start(O["pool_sample"][b, POOL_BUF - DT:POOL_BUF, :], Z[b * DT:b * DT + DT, 2, COL_U:COL_U + POOL_W]).then_inc(s_zout, 16)
            pool.dma_start(scratch, GK[0:TS, 2, :]).then_inc(s_gso, 16)
            pool.wait_ge(s_gso, 16)
            sv = scratch.rearrange("(b t) (h x) -> h t b x", t=DT, x=3)
            for h in range(NH):
                pool.dma_start(gates_s[DT * h:DT * h + DT, :, :], sv[h]).then_inc(s_gsi, 16)
            tables = {"u": I["peer_u"], "v": I["peer_v"]}
            pool.wait_ge(s_eid, 1)
            for ph, (kind, t) in enumerate(PHASES[:N_INLINE]):
                ids = eid[:, t].rearrange("p a b -> p (a b)")
                for r in range(NROWS[t]):
                    k = BASE[ph] + r
                    wait(pool, s_rowfree, k - NROW + 1)
                    pool.indirect_dma_start(out=rows_ring[:, k % NROW, :], out_offset=None, in_=tables[kind],
                                            in_offset=bass.IndirectOffsetOnAxis(ap=ids[:, r:r + 1], axis=0)).then_inc(s_row[k % NROW], 16)
            for ph, (kind, t) in list(enumerate(PHASES))[N_INLINE:]:
                done = BASE[ph] - LOOP_BASE
                with pool.Fori(0, NROWS[t] // 16, 1) as it:
                    for half in range(2):
                        pool.wait_ge(s_idx, it * 2 + (done // 8 + half + 1))
                        for s in range(8):
                            pool.wait_ge(s_rowfree, it * 16 + (BASE[ph] + half * 8 + s - 7))
                            pool.sem_inc(s_pdma, 1)
                            pool.indirect_dma_start(out=loop_row[s], out_offset=None, in_=tables[kind],
                                                    in_offset=bass.IndirectOffsetOnAxis(ap=idxs[:, half, s:s + 1], axis=0)).then_inc(s_lrow[s], 16)

        @block.scalar
        def _(act):
            act.wait_ge(s_cin, 32)
            nc.scalar.activation(csig[0:9, :], cin[0:9, :], ACT.Exp, scale=-1.0).then_inc(s_sig, 1)
            ada_done = [0]

            def ada_out(n):
                for s in range(ada_done[0], ada_done[0] + n):
                    used(act, "ada", s)
                    nc.scalar.activation(mod[:, s * SECTION:(s + 1) * SECTION], PS[:, 6 + s % 2, :], ACT.Copy).then_inc(s_adaC, 1)
                ada_done[0] += n
            ada_out(3)
            act.wait_ge(s_x, 48)
            for t in range(TILES):
                wait(act, s_sq, t)
                nc.scalar.activation(sq_junk, X[:, t, :], ACT.Square, accum_out=sumsq[:, t:t + 1]).then_inc(s_sq, 1)
            ada_out(2)
            act.wait_ge(s_ms, 1)
            nc.scalar.activation(rstd[:, 0:3], sumsq[:, 0:3], ACT.Sqrt).then_inc(s_rt, 1)
            act.wait_ge(s_rs, 1)
            for t in range(TILES):
                nc.scalar.activation(X[:, t, :], X[:, t, :], ACT.Copy, scale=rstd[:, t:t + 1]).then_inc(s_xn, 1)
            ada_out(3)
            act.wait_ge(s_m1c, 1)
            for c in range(NK):
                act.wait_ge(s_xt, c + 1)
                nc.scalar.activation(hT[:, c, 0:TP], PS[:, c % 3, 0:TP], ACT.Identity, scale=A1T[:, c, 16:17], bias=B1T[:, c, 16:17]).then_inc(s_hA, 1)
            for n in range(NIN):
                used(act, "in", n)
                nc.scalar.activation(z_section(1, n), in_bank(1, n), ACT.Copy).then_inc(s_zA, 1)
                for half in range(2):
                    z, p = z_half(n, half)
                    nc.scalar.activation(z, p, ACT.Copy).then_inc(s_zA, 1)
                ada_out(ADA_WITH[n])
            used(act, "gl", 0, 0)
            for t in range(TILES):
                nc.scalar.activation(GK[:, t, :], PS[:, 3 + t, 0:48], ACT.Exp, scale=-1.0).then_inc(s_gexp, 1)

            def ct_out(m):
                kind, seq, j = CBLK[m]
                n = CMP_BLOCK if kind == "pe" else 128
                if m == 0 or kind == "pe":
                    act.wait_ge(s_ctz, 1)
                act.wait_ge(s_ct, m + 1)
                nc.scalar.activation(CT[:, :, seq, j * 128:j * 128 + n], PS[:, m % 4, :].rearrange("p (a b) -> p a b", a=4)[:, :, 0:n], ACT.Copy).then_inc(s_ctc, 1)
            for m in range(10):
                ct_out(m)
            act.wait_ge(s_zms, 1)
            nc.scalar.activation(qkr, qkr, ACT.Sqrt).then_inc(s_zrt, 1)
            for m in range(10, len(CBLK)):
                ct_out(m)
            act.wait_ge(s_kc2, 1)
            nc.scalar.activation(kc_sq, kc_sq, ACT.Sqrt).then_inc(s_kc3, 1)
            for t in range(TILES):
                n = 128 if t < 2 else TS
                act.wait_ge(s_qt, t + 1)
                for i in range(2):
                    src = PS[:, 3 * (t % 2) + i, :].rearrange("p (a b) -> p a b", a=4)[:, :, 0:n]
                    if t < 2:
                        nc.scalar.activation(QT[:, 4 * i:4 * i + 4, t * 128:(t + 1) * 128], src, ACT.Copy).then_inc(s_qtA, 1)
                    else:
                        nc.scalar.activation(QTs[:, i].rearrange("p b (r t) -> p r b t", r=4), src.rearrange("p r (b t) -> p r b t", t=DT), ACT.Copy).then_inc(s_qtA, 1)
            act.wait_ge(s_cmx, 1)
            nc.scalar.activation(PC, PC, ACT.Exp, scale=SC_QK).then_inc(s_cex, 1)
            act.wait_ge(s_kc, 1)
            for i in range(8):
                act.wait_ge(s_yp, i + 1)
                nc.scalar.activation(OT[:, 8 + i, 0:TOK], PS[:, 4 + i % 2, 0:TOK], ACT.Copy, scale=psT[:, i:i + 1]).then_inc(s_yo, 1)
                nc.scalar.activation(OT[:, 8 + i, TOK:384], PS[:, 4 + i % 2, TP:TOK], ACT.Copy, scale=psT[:, i:i + 1]).then_inc(s_yo, 1)

            def p_exp(u):
                t = UNITS[u][0]
                nk = 128 * (t + 1)
                act.wait_ge(s_mx, u + 1)
                for gi in range(2):
                    for br in range(2):
                        k = 2 * gi + br
                        v = Pp[:, u % 2, gi, br * nk:(br + 1) * nk]
                        nc.scalar.activation(v, v, ACT.Exp, bias=nm[:, u % 2, k:k + 1], scale=SC_QK, accum_out=sm[:, u % 2, k:k + 1]).then_inc(s_exp, 1)
            def p_unit(u):
                t, gp, r = UNITS[u]
                if u % 8 < 7:
                    p_exp(u + 1)
                act.wait_ge(s_T, u + 1)
                n = 256 * (t + 1)
                nc.scalar.activation(PTp[:, u % 2, 0:n], PS[:, 4, 0:n], ACT.Copy).then_inc(s_TA, 1)
                nc.scalar.activation(PTp[0:NC_, u % 2, 1024:1280], PS[0:NC_, 6, 0:256], ACT.Copy).then_inc(s_TA, 1)
                act.wait_ge(s_o, u + 1)
                nc.scalar.activation(OT[:, gp * 4 + r, t * 128:(t + 1) * 128], PS[:, 7, 0:128], ACT.Copy).then_inc(s_oc, 1)

            def gate1(group):
                buf, per = (GB_0, 1) if group == 0 else (GB_12, 2)
                for n in range(4):
                    act.wait_ge(s_gp, 4 * group + n + 1)
                    wait(act, s_x1, 4 * group + n)
                    for k in range(per):
                        nc.scalar.activation(buf[:, k], PS[:, 6 + k, :], ACT.Copy).then_inc(s_gb, 1)

            def norm2(group):
                act.wait_ge(s_x1, 4 * group + 4)
                tiles = GROUPS[group]
                for t in tiles:
                    nc.scalar.activation(h2(t), x1(t), ACT.Square, accum_out=sumsq[:, t:t + 1]).then_inc(s_sq2, 1)
                act.wait_ge(s_ms2, group + 1)
                nc.scalar.activation(rstd[:, tiles[0]:tiles[-1] + 1], sumsq[:, tiles[0]:tiles[-1] + 1], ACT.Sqrt).then_inc(s_rt2, 1)
                h2t, n = (H2T_0, 128) if group == 0 else (H2T_12, 192)
                for c in range(NK):
                    act.wait_ge(s_ht, 16 * group + c + 1)
                    nc.scalar.activation(h2t[:, c, 0:n], PS[:, c % 8, 0:n], ACT.Copy).then_inc(s_htA, 1)

            def queries(group):
                for i in range(HP):
                    used(act, "wq", i // 4, 3, group)
                    src = PS[:, i % 8, :]
                    if group == 0:
                        nc.scalar.activation(QPT_0[:, i, :], src[:, 0:128], ACT.Copy).then_inc(s_qA, 1)
                    else:
                        dst = QPT_12[i // 8][:, i % 8, :]
                        nc.scalar.activation(dst[:, 0:192], src[:, 0:192], ACT.Copy).then_inc(s_qA, 1)
                        nc.scalar.activation(dst[:, 192:256], src[:, 128:192], ACT.Copy).then_inc(s_qA, 1)
                sc = scratch_of(group)["sc"]
                for k in range(4 * len(GROUPS[group])):
                    act.wait_ge(s_scp, 4 * group + k + 1)
                    nc.scalar.activation(sc[:, k // 4, 4 * (k % 4):4 * (k % 4) + 4, :].rearrange("p a b -> p (a b)"), PS[:, k % 8, :], ACT.Copy).then_inc(s_sc, 1)

            def expert_exp(t):
                act.wait_ge(s_e2, t + 1)
                nc.scalar.activation(gw[:, t], gw[:, t], ACT.Exp).then_inc(s_e2x, 1)

            def gelu(t):
                act.wait_ge(s_dots, t + 1)
                nc.scalar.activation(dots[:, t, 0:NROWS[t]], dots[:, t, 0:NROWS[t]], ACT.Gelu).then_inc(s_gelu, 1)
            p_exp(0)
            for u in range(8):
                p_unit(u)
            gate1(0)
            norm2(0)
            queries(0)
            expert_exp(0)
            p_exp(8)
            for u in range(8, 16):
                p_unit(u)

            def kt_out(b):
                act.wait_ge(s_kt, b + 1)
                nc.scalar.activation(KTb[:, b % 2, 0], PS[:, 4, :].rearrange("p (a b) -> p a b", a=2), ACT.Copy).then_inc(s_ktA, 1)

            def s_exps(b):
                act.wait_ge(q_mx, b + 1)
                for k, (lo, hi) in enumerate(SPANS):
                    v = Ps[:, b % 2, lo:hi]
                    nc.scalar.activation(v, v, ACT.Exp, bias=nm[:, b % 2, k:k + 1], scale=SC_QK, accum_out=sm[:, b % 2, k:k + 1]).then_inc(q_exp, 1)
            kt_out(0)
            s_exps(0)
            for b in range(DB):
                if b + 1 < DB:
                    kt_out(b + 1)
                    s_exps(b + 1)
                act.wait_ge(q_T, b + 1)
                nc.scalar.activation(PTs[:, b % 2, 0:512], PS[:, 6, :], ACT.Copy).then_inc(q_TA, 1)
                act.wait_ge(q_o, b + 1)
                for dup in range(2):
                    o = TP + dup * TS + b * DT
                    nc.scalar.activation(OT[:, 0:8, o:o + DT], PS[:, 7, 448:512].rearrange("p (a b) -> p a b", a=8), ACT.Copy).then_inc(q_oc, 1)
            gate1(1)
            gelu(0)
            norm2(1)
            queries(1)
            for i in range(8):
                act.wait_ge(s_g2p, i + 1)
                nc.scalar.activation(GB2[:, i // 4, (i % 4) * SECTION:(i % 4 + 1) * SECTION], PS[:, i, :], ACT.Copy).then_inc(s_g2, 1)
            expert_exp(1)
            expert_exp(2)
            act.wait_ge(s_eid, 2)
            for ph, (kind, t) in list(enumerate(PHASES))[N_INLINE:]:
                if kind == "v":
                    gelu(t)
                src = eid[:, t].rearrange("p a b -> p (a b)") if t < 2 else eid_s
                with act.Fori(0, NROWS[t] // 16, 1) as it:
                    for half in range(2):
                        act.wait_ge(s_rowfree, it * 16 + (BASE[ph] + (half - 1) * 8))
                        nc.scalar.activation(idxs[:, half, :], src[:, bass.ds(it * 16 + half * 8, 8)], ACT.Copy).then_inc(s_idx, 1)

        @block.tensor
        def _(pe):
            def need(i):
                pe.wait_ge(slot(i)[1], arrived[i])

            def ada_section(s):
                wait(pe, s_adaC, s - 1)
                for p in range(4):
                    i = index[("ada", s, p)]
                    need(i)
                    for j in range(4):
                        last = nc.tensor.matmul(PS[32 * j:32 * j + 32, 6 + s % 2, :], cT[:, 4 * p + j, :], ring[:, i % NSLOT, j, :],
                                                start=(p == 0), stop=(p == 3), tile_position=(0, 32 * j))
                    last.then_inc(s_free, 1)

            pe.wait_ge(s_cst, 16)
            pe.wait_ge(s_silu, 1)
            for c in range(NK):
                last = nc.tensor.transpose(PS[:, 0, c * 9:c * 9 + 9], cin[0:9, c * 128:(c + 1) * 128], ident[0:9, 0:9])
            last.then_inc(s_cps, 1)
            pe.wait_ge(s_cT, 1)
            for s in range(ADA_FIRST):
                ada_section(s)
            pe.wait_ge(s_gain, 16 * 6)
            nc.tensor.transpose(PS[:, 0, 0:NK], g1_raw[0:NK, :], ident[0:NK, 0:NK])
            nc.tensor.transpose(PS[:, 0, 16:24], ps_raw[0:8, :], ident[0:8, 0:8]).then_inc(s_gT, 1)
            pe.wait_ge(s_sk, 16)
            for i in range(HP):
                last = nc.tensor.transpose(PS[:, 2 + i // 4, (i % 4) * 128:(i % 4 + 1) * 128], sk_raw[:, i, :], ident)
            last.then_inc(s_skp, 1)
            pe.wait_ge(s_bada, 16)
            pe.wait_ge(s_gTc, 1)
            for k in range(2):
                for c in range(NK):
                    last = nc.tensor.matmul(PS[:, k, c * 17:c * 17 + 17], mod[:, k * D + c * 128:k * D + (c + 1) * 128], selF, start=True, stop=True)
            last.then_inc(s_m1, 1)
            pe.wait_ge(s_m1c, 1)
            pe.wait_ge(s_skc, 1)
            pe.wait_ge(s_xn, 3)
            for c in range(NK):
                wait(pe, s_hA, c - 2)
                wait(pe, s_hD, c - 2)
                for t in range(TILES):
                    last = nc.tensor.transpose(PS[:, c % 3 + 3 * (t // 2), (t % 2) * 128:(t % 2 + 1) * 128], X[:, t, c * 128:(c + 1) * 128], ident)
                last.then_inc(s_xt, 1)
            pe.wait_ge(s_hA, NK)
            pe.wait_ge(s_hD, NK)
            ada_i = ADA_FIRST
            for n in range(NIN):
                wait(pe, s_zA, 3 * (n - 1))
                wait(pe, s_zD, n - 1)
                for p in range(4):
                    i = index[("in", n, p)]
                    need(i)
                    for t in range(2):
                        for j in range(KP):
                            c = KP * p + j
                            nc.tensor.matmul(PS[:, 3 * (n % 2) + t, :], hT[:, c, t * 128:(t + 1) * 128], ring[:, i % NSLOT, j, :],
                                             start=(c == 0), stop=(c == NK - 1))
                    for j in range(KP):
                        c = KP * p + j
                        for half in range(2):
                            cols = slice(256 * half, 256 * half + 256)
                            last = nc.tensor.matmul(PS[64 * half:64 * half + 64, 3 * (n % 2) + 2, cols], hT[:, c, TP:TOK], ring[:, i % NSLOT, j, cols],
                                                    start=(c == 0), stop=(c == NK - 1), tile_position=(0, 64 * half))
                    last.then_inc(s_free, 1)
                for _ in range(ADA_WITH[n]):
                    ada_section(ada_i)
                    ada_i += 1
            pe.wait_ge(s_zA, 3 * (NIN - 1))
            pe.wait_ge(s_zD, NIN - 1)
            need(index[("gl", 0, 0)])
            for t in range(TILES):
                for c in range(NK):
                    last = nc.tensor.matmul(PS[:, 3 + t, 0:48], hT[:, c, t * 128:(t + 1) * 128], gl_w[:, c, :], start=(c == 0), stop=(c == NK - 1))
            last.then_inc(s_free, 1)
            pe.wait_ge(s_zA, 3 * NIN)
            pe.wait_ge(s_zD, NIN)
            pe.wait_ge(s_gexp, 3)
            for m, (kind, seq, j) in enumerate(CBLK):
                wait(pe, s_ctc, m - 3)
                if kind == "page":
                    pe.wait_ge(s_cpage[m % 4], 16 * (m // 4 + 1))
                    src, n = cpage[:, m % 4, :], 128
                elif kind == "prompt":
                    src, n = Z[:, j, COL_C:COL_C + 512], 128
                else:
                    pe.wait_ge(s_pe, 32)
                    src, n = pe_raw[0:CMP_BLOCK, :], CMP_BLOCK
                for k in range(4):
                    last = nc.tensor.transpose(PS[:, m % 4, k * 128:k * 128 + n], src[:, k * 128:(k + 1) * 128], ident[0:n, 0:n])
                last.then_inc(s_ct, 1)
            pe.wait_ge(s_wc, 128)
            pe.wait_ge(s_ctc, len(CBLK))
            for c in range(2):
                for gp in range(2):
                    for l in range(CMP_BLOCK):
                        for gi in range(2):
                            h = slice(64 * gi, 64 * gi + 64)
                            last = nc.tensor.matmul(PS[h, 4 + c, gp * 150:gp * 150 + 150], WC[c][h, gp, l, :],
                                                    CT[h, 2 * c + gp, :, l:l + CMP_STRIDE * (NC_ - 1) + 1:CMP_STRIDE],
                                                    start=(l == 0), stop=(l == CMP_BLOCK - 1), tile_position=(64 * gi, 64 * gi))
                last.then_inc(s_cmp, 1)
            pe.wait_ge(s_kc1, 1)
            nc.tensor.matmul(PS[:, 6, 0:270], blk, kc_sq, start=True, stop=True).then_inc(s_kcm, 1)
            pe.wait_ge(s_vct, 1)
            for gp in range(2):
                nc.tensor.transpose(PS[0:NS_C, 7, gp * 128:(gp + 1) * 128], VCT[:, gp, 0:NS_C], ident)
            for gp in range(2):
                last = nc.tensor.transpose(PS[0:NC_, 7, 256 + gp * 128:256 + (gp + 1) * 128], VCT[:, gp, NS_C:NS_C + NC_], ident)
            last.then_inc(s_vcp, 1)
            pe.wait_ge(s_norm, 1)
            for t in range(TILES):
                n = 128 if t < 2 else TS
                wait(pe, s_qtA, 2 * (t - 1))
                wait(pe, s_qtD, t - 1)
                bank = 3 * (t % 2)
                for gp in range(2):
                    for r in range(4):
                        nc.tensor.transpose(PS[:, bank + gp, r * 128:r * 128 + n], Z[0:n, t, gp * 512 + r * 128:gp * 512 + (r + 1) * 128], ident[0:n, 0:n])
                for br, col in enumerate((COL_S, COL_W)):
                    for gp in range(2):
                        k = 2 * br + gp
                        last = nc.tensor.transpose(PS[:, bank + 2, k * 128:k * 128 + n], Z[0:n, t, col + gp * 128:col + (gp + 1) * 128], ident[0:n, 0:n])
                last.then_inc(s_qt, 1)
            pe.wait_ge(s_kc, 1)
            pe.wait_ge(s_vc, 1)
            pe.wait_ge(s_qtA, 6)
            pe.wait_ge(s_qtD, 3)
            for t in range(2):
                for k in range(8):
                    for gi in range(2):
                        h = slice(64 * gi, 64 * gi + 64)
                        last = nc.tensor.matmul(PS[:, 6 + gi, (t * 8 + k) * NC_:(t * 8 + k + 1) * NC_], QT[h, k, t * 128:(t + 1) * 128],
                                                KC[h, k // 4, NS_C:NS_C + NC_], start=True, stop=True, tile_position=(64 * gi, 0))
            last.then_inc(s_csc, 1)
            pe.wait_ge(s_plin, 16 * 6)
            for c in range(8):
                w = c // 2
                wait(pe, s_dt, c - 3)
                u = [Z[:, t, COL_U + c * 128:COL_U + (c + 1) * 128] for t in range(TILES)]
                bank = PS[:, c % 4, :]
                nc.tensor.matmul(bank[:, 0:128], u[0], poolB[:, w, 0:128], start=True, stop=True)
                nc.tensor.matmul(bank[:, 128:256], u[0], poolB[:, w, 128:256], start=True, stop=False)
                nc.tensor.matmul(bank[:, 128:256], u[1], poolB[:, w, 256:384], start=False, stop=True)
                n = DB * POOL_BUF
                nc.tensor.matmul(bank[:, 256:320], past_u[0:n, c * 128:(c + 1) * 128], poolB[0:n, w, 384:448], start=True, stop=False)
                nc.tensor.matmul(bank[:, 256:320], u[2][0:TS, :], poolB[0:TS, w, 448:512], start=False, stop=True).then_inc(s_dp, 1)
            pe.wait_ge(s_dt, 8)
            for i in range(8):
                w, eh = i // 2, i % 2
                wait(pe, s_yo, 2 * (i - 1))
                for ch in range(2):
                    last = nc.tensor.matmul(PS[:, 4 + i % 2, 0:TOK], WP[:, w, ch, eh * 128:(eh + 1) * 128], DTt[:, 2 * w + ch, :], start=(ch == 0), stop=(ch == 1))
                last.then_inc(s_yp, 1)
            pe.wait_ge(s_yo, 16)
            pe.wait_ge(s_cmx, 1)

            def p_scores(u):
                t, gp, r = UNITS[u]
                nk = 128 * (t + 1)
                wait(pe, s_mx, u - 1)
                for br in range(2):
                    for gi in range(2):
                        h = slice(64 * gi, 64 * gi + 64)
                        last = nc.tensor.matmul(PS[:, 2 * (u % 2) + gi, br * nk:(br + 1) * nk], QT[h, gp * 4 + r, t * 128:(t + 1) * 128],
                                                KT[h, br, gp, 0:nk], start=True, stop=True, tile_position=(64 * gi, 0))
                last.then_inc(s_S, 1)

            def p_unit(u):
                t, gp, r = UNITS[u]
                if u % 8 < 7:
                    p_scores(u + 1)
                pe.wait_ge(s_pn, u + 1)
                wait(pe, s_TA, 2 * u)
                wait(pe, s_TD, u)
                for gi in range(2):
                    for k in range(2 * (t + 1)):
                        nc.tensor.transpose(PS[:, 4 + gi, k * 128:(k + 1) * 128], Pp[:, u % 2, gi, k * 128:(k + 1) * 128], ident)
                    last = nc.tensor.transpose(PS[0:NC_, 6, gi * 128:(gi + 1) * 128], PC[:, gi, t * 8 + gp * 4 + r, :], ident)
                last.then_inc(s_T, 1)
                pe.wait_ge(s_TA, 2 * u + 2)
                pe.wait_ge(s_TD, u + 1)
                wait(pe, s_oc, u)
                for gi in range(2):
                    g = 2 * gp + gi
                    o = PS[64 * gi:64 * gi + 64, 7, 0:128]
                    nc.tensor.matmul(o, VCp[0:NC_, g * 64:(g + 1) * 64], PTp[0:NC_, u % 2, 1024 + gi * 128:1024 + (gi + 1) * 128], start=True, stop=False, tile_position=(0, 64 * gi))
                    for br in range(2):
                        for k in range(t + 1):
                            c = br * (t + 1) + k
                            last = nc.tensor.matmul(o, VK[:, k, br, g * 64:(g + 1) * 64], PTp[:, u % 2, gi * 512 + c * 128:gi * 512 + (c + 1) * 128],
                                                    start=False, stop=(br == 1 and k == t), tile_position=(0, 64 * gi))
                last.then_inc(s_o, 1)

            def project(group):
                tiles = GROUPS[group]
                for n in range(4):
                    wait(pe, s_gb, n if group == 0 else 4 + 2 * n)
                    for k in range(len(tiles)):
                        last = nc.tensor.matmul(PS[:, 6 + k, :], selT[:, k, :], mod[:, 2 * D + n * SECTION:2 * D + (n + 1) * SECTION], start=True, stop=True)
                    last.then_inc(s_gp, 1)
                    wait(pe, s_x1, 4 * group + n - 1)
                    for p in range(4):
                        i = index[("out", n, p, group)]
                        need(i)
                        for k, t in enumerate(tiles):
                            for j in range(KP):
                                c = KP * p + j
                                last = nc.tensor.matmul(PS[:, 3 * (n % 2) + k, :], OT[:, c, t * 128:(t + 1) * 128], slot(i)[0][:, j, :],
                                                        start=(c == 0), stop=(c == NK - 1))
                        last.then_inc(s_free, 1)

            def norm2(group):
                tiles = GROUPS[group]
                for n in range(4):
                    pe.wait_ge(s_x1, 4 * group + 4)
                    wait(pe, s_h2, 4 * group + n - 1)
                    for m, chunk in enumerate((4, 3)):
                        for k in range(len(tiles)):
                            last = nc.tensor.matmul(PS[:, 4 * (n % 2) + 2 * m + k, :], selT[:, k, :], mod[:, chunk * D + n * SECTION:chunk * D + (n + 1) * SECTION], start=True, stop=True)
                    last.then_inc(s_m2, 1)
                pe.wait_ge(s_h2, 4 * group + 4)
                for c in range(NK):
                    wait(pe, s_htA, 16 * group + c - 7 if c >= 8 else 0)
                    for k, t in enumerate(tiles):
                        n = 128 if t < 2 else TS
                        last = nc.tensor.transpose(PS[:, c % 8, k * 128:k * 128 + n], h2(t)[0:n, c * 128:(c + 1) * 128], ident[0:n, 0:n])
                    last.then_inc(s_ht, 1)
                pe.wait_ge(s_htA, 16 * group + 16)

            def queries(group):
                tiles = GROUPS[group]
                h2t, w = (H2T_0, 128) if group == 0 else (H2T_12, 192)
                for n in range(4):
                    wait(pe, s_qA, 0 if n < 2 else 4 * (n - 1) if group == 0 else 16 + 8 * (n - 1))
                    for p in range(4):
                        i = index[("wq", n, p, group)]
                        need(i)
                        for m in range(4):
                            for j in range(KP):
                                c = KP * p + j
                                last = nc.tensor.matmul(PS[:, 4 * (n % 2) + m, 0:w], slot(i)[0][:, j, m * 128:(m + 1) * 128], h2t[:, c, 0:w],
                                                        start=(c == 0), stop=(c == NK - 1))
                        last.then_inc(s_free, 1)
                pe.wait_ge(s_qA, 16 + 32 * group)
                for k in range(4 * len(tiles)):
                    for i in range(4):
                        hp = 4 * (k % 4) + i
                        h, p = hp // 2, hp % 2
                        q = QPT_0[:, hp, :] if group == 0 else QPT_12[hp // 8][:, hp % 8, k // 4 * 128:(k // 4 + 1) * 128]
                        last = nc.tensor.matmul(PS[:, k % 8, i * 128:(i + 1) * 128], q, skT[:, p * PH + h, :], start=True, stop=True)
                    last.then_inc(s_scp, 1)
                pe.wait_ge(s_sc, 4 + 8 * group)
            pe.wait_ge(s_pc, 1)
            p_scores(0)
            for u in range(8):
                p_unit(u)
            pe.wait_ge(s_oc, 8)
            pe.wait_ge(s_a2, 1)
            project(0)
            norm2(0)
            queries(0)
            p_scores(8)
            for u in range(8, 16):
                p_unit(u)
            pe.wait_ge(s_oc, 16)

            def s_keys(b):
                pe.wait_ge(s_kvp[b % 2], 48 * (b // 2 + 1))
                wait(pe, s_ktA, b)
                wait(pe, s_ktD, b)
                for br in range(2):
                    for gp in range(2):
                        for j in range(2):
                            last = nc.tensor.transpose(PS[:, 4 + br, gp * 256 + j * 128:gp * 256 + (j + 1) * 128], kvpage[b % 2][:, br, j, gp * 128:(gp + 1) * 128], ident)
                last.then_inc(s_kt, 1)

            def s_scores(b):
                pe.wait_ge(s_ktA, b + 1)
                pe.wait_ge(s_ktD, b + 1)
                wait(pe, q_mx, b - 1)
                for g in range(4):
                    gp, gi = g // 2, g % 2
                    h, o = slice(64 * gi, 64 * gi + 64), slice(32 * g, 32 * g + 32)
                    q = QTs[h, gp, b, :]
                    kw = dict(start=True, stop=True, tile_position=(64 * gi, 32 * g))
                    for br in range(2):
                        bank = PS[o, 2 * (b % 2) + br, :]
                        nc.tensor.matmul(bank[:, 0:PAST], q, KTb[h, b % 2, br, gp, :], **kw)
                        nc.tensor.matmul(bank[:, PAST:PAST + TS], q, KT[h, br, gp, TP:TOK], **kw)
                    last = nc.tensor.matmul(bank[:, 320:440], q, KC[h, gp, 0:NS_C], **kw)
                last.then_inc(q_S, 1)
            s_keys(0)
            s_scores(0)
            for b in range(DB):
                if b + 1 < DB:
                    s_keys(b + 1)
                    s_scores(b + 1)
                pe.wait_ge(q_pn, b + 1)
                wait(pe, q_TA, b)
                wait(pe, q_TD, b)
                wait(pe, q_oc, 2 * b)
                P = Ps[:, b % 2, :]
                for k, at_ in enumerate((0, 128, 320, 448)):
                    nc.tensor.transpose(PS[:, 6, k * 128:(k + 1) * 128], P[:, at_:at_ + 128], ident)
                for k, at_ in enumerate((256, 576)):
                    nc.tensor.transpose(PS[0:TS, 7, k * 128:(k + 1) * 128], P[:, at_:at_ + TS], ident)
                nc.tensor.transpose(PS[0:NS_C, 7, 256:384], P[:, 640:760], ident).then_inc(q_T, 1)
                pe.wait_ge(q_TA, b + 1)
                pe.wait_ge(q_TD, 2 * b + 2)
                for g in range(4):
                    gp, gi = g // 2, g % 2
                    o = PS[64 * gi:64 * gi + 64, 7, 448 + gp * 32:448 + gp * 32 + 32]
                    pt = PTs[:, b % 2, :].rearrange("p (a b) -> p a b", a=7)[:, :, 32 * g:32 * g + 32]
                    v = slice(256 + g * 64, 256 + (g + 1) * 64)
                    steps = [(kvpage[b % 2][:, br, j, v], pt[:, 2 * br + j]) for br in range(2) for j in range(2)]
                    steps += [(VK[0:TS, 2, br, g * 64:(g + 1) * 64], pt[0:TS, 4 + br]) for br in range(2)]
                    steps += [(VCs[0:NS_C, g * 64:(g + 1) * 64], pt[0:NS_C, 6])]
                    for i, (lhs, rhs) in enumerate(steps):
                        last = nc.tensor.matmul(o, lhs, rhs, start=(i == 0), stop=(i == len(steps) - 1), tile_position=(0, 64 * gi))
                last.then_inc(q_o, 1)
            pe.wait_ge(q_oc, 2 * DB)
            project(1)
            norm2(1)
            queries(1)
            for i in range(8):
                nc.tensor.matmul(PS[:, i, :], selT[:, i // 4, :], mod[:, 5 * D + (i % 4) * SECTION:5 * D + (i % 4 + 1) * SECTION], start=True, stop=True).then_inc(s_g2p, 1)
            pe.wait_ge(s_g2, 8)
            pe.wait_ge(s_facc, 1)
            for n in range(4):
                last = nc.tensor.matmul(PS[0:TS, n, :], fold, acc[:, n * SECTION:(n + 1) * SECTION], start=True, stop=True)
            last.then_inc(s_fold, 1)

        @block.vector
        def _(dve):
            V = nc.vector
            V.memset(cT, 0.0).then_inc(s_stage, 1)
            dve.wait_ge(s_cst, 16)
            dve.wait_ge(s_pt_in, 16)
            link(V.tensor_scalar(pgf, pgi, float(PAGE), cst[:, C_PAGE:C_PAGE + 1], ALU.mult, ALU.add))
            V.tensor_copy(pgx, pgf).then_inc(s_pgx, 1)
            dve.wait_ge(s_cin, 32)
            dve.wait_ge(s_sig, 1)
            link(V.tensor_scalar(csig[0:9, :], csig[0:9, :], 1.0, None, ALU.add))
            link(V.reciprocal(csig[0:9, :], csig[0:9, :]))
            V.tensor_tensor(cin[0:9, :], cin[0:9, :], csig[0:9, :], ALU.mult).then_inc(s_silu, 1)
            dve.wait_ge(s_cps, 1)
            dve.wait_ge(s_stage, 1)
            V.tensor_copy(cT[:, :, 0:9], PS[:, 0, 0:144].rearrange("p (a b) -> p a b", b=9)).then_inc(s_cT, 1)
            dve.wait_ge(s_sq, 3)
            V.tensor_scalar(sumsq[:, 0:3], sumsq[:, 0:3], 1.0 / D, EPS, ALU.mult, ALU.add).then_inc(s_ms, 1)
            dve.wait_ge(s_rt, 1)
            V.reciprocal(rstd[:, 0:3], rstd[:, 0:3]).then_inc(s_rs, 1)
            dve.wait_ge(s_gT, 1)
            V.tensor_copy(psT, PS[:, 0, 16:24])
            link(V.tensor_copy(g1T, PS[:, 0, 0:16]))
            V.tensor_copy(stat[:, 0:1], g1T[:, 0:1]).then_inc(s_gTc, 1)
            dve.wait_ge(s_skp, 1)
            for i in range(4):
                last = V.tensor_copy(skT[:, 4 * i:4 * i + 4, :].rearrange("p a b -> p (a b)"), PS[:, 2 + i, :])
            last.then_inc(s_skc, 1)
            dve.wait_ge(s_m1, 1)
            bank = [PS[:, k, 0:272].rearrange("p (a b) -> p a b", b=17) for k in range(2)]
            V.tensor_copy(B1T, bank[0])
            V.scalar_tensor_tensor(out=A1T, in0=bank[1], scalar=1.0, in1=g1T.unsqueeze(2).to_broadcast([128, NK, 17]), op0=ALU.add, op1=ALU.mult).then_inc(s_m1c, 1)
            dve.wait_ge(s_m1c, 1)
            for c in range(NK):
                dve.wait_ge(s_xt, c + 1)
                o = hT[:, c, TP:384].rearrange("p (b t) -> p b t", t=DT)
                link(V.tensor_tensor(o, PS[:, 3 + c % 3, 0:128].rearrange("p (b t) -> p b t", t=DT), A1T[:, c, 0:16].unsqueeze(2).to_broadcast([128, 16, DT]), ALU.mult))
                V.tensor_tensor(o, o, B1T[:, c, 0:16].unsqueeze(2).to_broadcast([128, 16, DT]), ALU.add).then_inc(s_hD, 1)
            for n in range(NIN):
                used(dve, "in", n)
                V.tensor_copy(z_section(0, n), in_bank(0, n)).then_inc(s_zD, 1)
            dve.wait_ge(s_gexp, 3)
            dve.wait_ge(s_zA, 3 * NIN)
            link(V.tensor_scalar(GK, GK, 1.0, None, ALU.add))
            V.reciprocal(GK, GK)
            for t in range(TILES):
                n = 128 if t < 2 else TS
                for br, col in enumerate((COL_S, COL_W)):
                    V.tensor_copy(VK[0:n, t, br, :], Z[0:n, t, col + KVW:col + 2 * KVW])
            parts = [(0, 0, NH), (COL_S, NH, NKV), (COL_W, NH + NKV, NKV)]
            V.memset(qkr[:, 2, :], float(HD))
            for t in range(TILES):
                m = 128 if t < 2 else TS
                for col, h0, n in parts:
                    v = Z[0:m, t, col:col + n * HD].rearrange("p (h d) -> p h d", d=HD)
                    last = V.tensor_tensor(sq_z[0:m, h0:h0 + n, :], v, v, ALU.mult)
                link(last)
                link(V.tensor_reduce(qkr[0:m, t, :], sq_z[0:m], X_AXIS, ALU.add))
            V.tensor_scalar(qkr, qkr, 1.0 / HD, EPS, ALU.mult, ALU.add).then_inc(s_zms, 1)
            dve.wait_ge(s_zrt, 1)
            link(V.reciprocal(qkr, qkr))
            for t in range(TILES):
                m = 128 if t < 2 else TS
                for col, h0, n in parts:
                    v = Z[0:m, t, col:col + n * HD].rearrange("p (h d) -> p h d", d=HD)
                    last = V.tensor_tensor(v, v, qkr[0:m, t, h0:h0 + n].unsqueeze(2).to_broadcast([m, n, HD]), ALU.mult)
            link(last)
            for t in range(TILES):
                m = 128 if t < 2 else TS
                for k, (col, h0, n) in enumerate(parts):
                    v = Z[0:m, t, col:col + n * HD].rearrange("p (h d) -> p h d", d=HD)
                    g = gq if k == 0 else gk[:, k, :]
                    last = V.tensor_tensor(v, v, g[0:m].unsqueeze(1).to_broadcast([m, n, HD]), ALU.mult)
            last.then_inc(s_norm, 1)
            dve.wait_ge(s_cmp, 2)
            for c, to in ((0, KC), (1, VCT)):
                for gp in range(2):
                    last = V.tensor_scalar(to[:, gp, :], PS[:, 4 + c, gp * 150:gp * 150 + 135], PS[:, 4 + c, gp * 150 + 135:gp * 150 + 136], None, ALU.add)
            last.then_inc(s_vct, 1)
            dve.wait_ge(s_vct, 1)
            kcf = KC.rearrange("p a b -> p (a b)")
            V.tensor_tensor(kc_sq, kcf, kcf, ALU.mult).then_inc(s_kc1, 1)
            dve.wait_ge(s_kcm, 1)
            V.tensor_scalar(kc_sq, PS[:, 6, 0:270], EPS, None, ALU.add).then_inc(s_kc2, 1)
            dve.wait_ge(s_kc3, 1)
            link(V.reciprocal(kc_sq, kc_sq))
            link(V.tensor_tensor(kcf, kcf, kc_sq, ALU.mult))
            V.tensor_scalar(kcf, kcf, gkc[:, 0:1], None, ALU.mult).then_inc(s_kc, 1)
            dve.wait_ge(s_vcp, 1)
            V.tensor_copy(VCs[0:NS_C, :], PS[0:NS_C, 7, 0:256])
            V.tensor_copy(VCp[0:NC_, :], PS[0:NC_, 7, 256:512]).then_inc(s_vc, 1)
            for t in range(TILES):
                n = 128 if t < 2 else TS
                dve.wait_ge(s_qt, t + 1)
                V.tensor_copy(KT[:, :, :, t * 128:t * 128 + n].rearrange("p a b c -> p (a b) c"),
                              PS[:, 3 * (t % 2) + 2, :].rearrange("p (a b) -> p a b", a=4)[:, :, 0:n]).then_inc(s_qtD, 1)
            dve.wait_ge(s_csc, 1)
            dve.wait_ge(s_bc, 16)
            for gi in range(2):
                last = V.tensor_tensor(PC[:, gi], PS[:, 6 + gi, 0:16 * NC_].rearrange("p (a b) -> p a b", a=16), biasC[:, gi], ALU.add)
            link(last)
            cmax = stat[:, 0:32].rearrange("p (a b) -> p a b", a=2)
            link(V.tensor_reduce(cmax, PC, X_AXIS, ALU.max))
            V.tensor_tensor(PC.rearrange("p a b c -> p (a b) c"), PC.rearrange("p a b c -> p (a b) c"), stat[:, 0:32].unsqueeze(2).to_broadcast([128, 32, NC_]), ALU.subtract).then_inc(s_cmx, 1)
            dve.wait_ge(s_cex, 1)
            link(V.tensor_reduce(cmax, PC, X_AXIS, ALU.add))
            link(V.reciprocal(stat[:, 0:32], stat[:, 0:32]))
            for gi in range(2):
                for t in range(2):
                    gate = GK[:, t, :].rearrange("p (gp gi r x) -> p gp gi r x", gp=2, gi=2, r=4)[:, :, gi, :, 0]
                    c = cmax[:, gi, t * 8:t * 8 + 8].rearrange("p (a b) -> p a b", a=2)
                    last = V.scalar_tensor_tensor(out=c, in0=gate, scalar=cst[:, C_VALID + t:C_VALID + t + 1], in1=c, op0=ALU.mult, op1=ALU.mult)
            link(last)
            V.tensor_tensor(PC.rearrange("p a b c -> p (a b) c"), PC.rearrange("p a b c -> p (a b) c"), stat[:, 0:32].unsqueeze(2).to_broadcast([128, 32, NC_]), ALU.mult).then_inc(s_pc, 1)
            for c in range(8):
                dve.wait_ge(s_dp, c + 1)
                V.tensor_copy(DTt[:, c, :], PS[:, c % 4, 0:TOK]).then_inc(s_dt, 1)

            dve.wait_ge(s_bada, 32)
            dve.wait_ge(s_g2in, 16)
            V.scalar_tensor_tensor(out=mod[:, 4 * D:5 * D], in0=mod[:, 4 * D:5 * D], scalar=cst[:, C_ROW9:C_ROW9 + 1], in1=g2b, op0=ALU.add, op1=ALU.mult).then_inc(s_a2, 1)

            dve.wait_ge(s_bp, 16)

            def p_max(u):
                t, gp, r = UNITS[u]
                nk = 128 * (t + 1)
                dve.wait_ge(s_S, u + 1)
                wait(dve, s_T, u - 1)
                for gi in range(2):
                    h = (2 * gp + gi) * GROUP + r
                    for br in range(2):
                        k = 2 * gi + br
                        last = V.tensor_tensor_reduce(out=Pp[:, u % 2, gi, br * nk:(br + 1) * nk], in0=PS[:, 2 * (u % 2) + gi, br * nk:(br + 1) * nk],
                                                      in1=biasP[:, h, 256 - nk:256], scale=1.0, scalar=-3.0e38, op0=ALU.add, op1=ALU.max, accum_out=mxv[:, u % 2, k:k + 1])
                link(last)
                V.tensor_scalar(nm[:, u % 2, 0:4], mxv[:, u % 2, 0:4], -SC_QK, None, ALU.mult).then_inc(s_mx, 1)

            def p_unit(u):
                t, gp, r = UNITS[u]
                nk = 128 * (t + 1)
                if u % 8 < 7:
                    p_max(u + 1)
                dve.wait_ge(s_exp, 4 * u + 4)
                link(V.reciprocal(sm[:, u % 2, 0:4], sm[:, u % 2, 0:4]))
                gate = GK[:, t, :].rearrange("p (gp gi r x) -> p gp gi r x", gp=2, gi=2, r=4)[:, gp, :, r, 1:3]
                s4 = sm[:, u % 2, 0:4].rearrange("p (a b) -> p a b", a=2)
                link(V.tensor_tensor(s4, s4, gate, ALU.mult))
                for k in range(4):
                    v = Pp[:, u % 2, k // 2, (k % 2) * nk:(k % 2 + 1) * nk]
                    last = V.tensor_scalar(v, v, sm[:, u % 2, k:k + 1], None, ALU.mult)
                last.then_inc(s_pn, 1)
                dve.wait_ge(s_T, u + 1)
                n = 256 * (t + 1)
                V.tensor_copy(PTp[:, u % 2, 512:512 + n], PS[:, 5, 0:n]).then_inc(s_TD, 1)


            def kt_out(b):
                dve.wait_ge(s_kt, b + 1)
                V.tensor_copy(KTb[:, b % 2, 1], PS[:, 5, :].rearrange("p (a b) -> p a b", a=2)).then_inc(s_ktD, 1)

            def s_max(b):
                dve.wait_ge(q_S, b + 1)
                wait(dve, q_T, b - 1)
                src = [PS[:, 2 * (b % 2), 0:320], PS[:, 2 * (b % 2) + 1, 0:320], PS[:, 2 * (b % 2) + 1, 320:440]]
                bias = [biasS[:, b], biasS[:, b], biasCS[:, b]]
                for k, (lo, hi) in enumerate(SPANS):
                    last = V.tensor_tensor_reduce(out=Ps[:, b % 2, lo:hi], in0=src[k], in1=bias[k], scale=1.0, scalar=-3.0e38, op0=ALU.add, op1=ALU.max, accum_out=mxv[:, b % 2, k:k + 1])
                link(last)
                V.tensor_scalar(nm[:, b % 2, 0:3], mxv[:, b % 2, 0:3], -SC_QK, None, ALU.mult).then_inc(q_mx, 1)

            def s_unit(b):
                if b + 1 < DB:
                    kt_out(b + 1)
                    s_max(b + 1)
                dve.wait_ge(q_exp, 3 * b + 3)
                link(V.reciprocal(sm[:, b % 2, 0:3], sm[:, b % 2, 0:3]))
                for k, x in enumerate((1, 2, 0)):
                    last = V.tensor_tensor(sm[:, b % 2, k:k + 1], sm[:, b % 2, k:k + 1], gates_s[:, b, x:x + 1], ALU.mult)
                link(last)
                for k, (lo, hi) in enumerate(SPANS):
                    last = V.tensor_scalar(Ps[:, b % 2, lo:hi], Ps[:, b % 2, lo:hi], sm[:, b % 2, k:k + 1], None, ALU.mult)
                last.then_inc(q_pn, 1)
                dve.wait_ge(q_T, b + 1)
                V.tensor_copy(PTs[0:TS, b % 2, 512:768], PS[0:TS, 7, 0:256]).then_inc(q_TD, 1)
                V.tensor_copy(PTs[0:NS_C, b % 2, 768:896], PS[0:NS_C, 7, 256:384]).then_inc(q_TD, 1)

            def add1(group, n):
                tiles = GROUPS[group]
                gb, tmp = (GB_0, TMP_0) if group == 0 else (GB_12, TMP_12)
                if n == 0:
                    dve.wait_ge(s_x1in, 16 + 48 * group)
                used(dve, "out", n, 3, group)
                dve.wait_ge(s_gb, n + 1 if group == 0 else 4 + 2 * n + 2)
                for k in range(len(tiles)):
                    last = V.tensor_tensor(tmp[:, k], PS[:, 3 * (n % 2) + k, :], gb[:, k], ALU.mult)
                link(last)
                for k, t in enumerate(tiles):
                    v = x1(t)[:, n * SECTION:(n + 1) * SECTION]
                    last = V.tensor_tensor(v, v, tmp[:, k], ALU.add)
                last.then_inc(s_x1, 1)
                dve.wait_ge(s_x1, 4 * group + n + 1)

            def rms2(group):
                lo, hi = GROUPS[group][0], GROUPS[group][-1] + 1
                dve.wait_ge(s_sq2, hi)
                V.tensor_scalar(sumsq[:, lo:hi], sumsq[:, lo:hi], 1.0 / D, EPS, ALU.mult, ALU.add).then_inc(s_ms2, 1)
                dve.wait_ge(s_rt2, group + 1)
                link(V.reciprocal(rstd[:, lo:hi], rstd[:, lo:hi]))

            def modulate2(group, n):
                cols = slice(n * SECTION, (n + 1) * SECTION)
                bank = 4 * (n % 2)
                dve.wait_ge(s_m2, 4 * group + n + 1)
                for k, t in enumerate(GROUPS[group]):
                    last = V.scalar_tensor_tensor(out=h2(t)[:, cols], in0=x1(t)[:, cols], scalar=rstd[:, t:t + 1], in1=PS[:, bank + k, :], op0=ALU.mult, op1=ALU.mult)
                link(last)
                for k, t in enumerate(GROUPS[group]):
                    last = V.tensor_tensor(h2(t)[:, cols], h2(t)[:, cols], PS[:, bank + 2 + k, :], ALU.add)
                last.then_inc(s_h2, 1)

            def top16(vals, val, idx, n):
                for lo in (0, 8):
                    for i in range(n):
                        last = V.max(val[:, i, lo:lo + 8], vals[i])
                    link(last)
                    yield
                    for i in range(n):
                        last = V.max_index(idx[:, i, lo:lo + 8], val[:, i, lo:lo + 8], vals[i])
                    link(last)
                    yield
                    if lo == 0:
                        for i in range(n):
                            last = V.match_replace(vals[i], val[:, i, 0:8], vals[i], -3.0e38)
                        link(last)
                        yield

            def experts(t):
                group = 0 if t == 0 else 1
                b = scratch_of(group)
                sc, cand, onehot, picked, ab_i, ab_f = b["sc"][:, GROUPS[group].index(t)], b["cand"], b["onehot"], b["picked"], b["ab_i"], b["ab_f"]
                val1, idx1, idx1f, val2, idx2, smax = b["val1"], b["idx1"], b["idx1f"], b["val2"], b["idx2"], stat[:, 0:PH]
                dve.wait_ge(s_sc, 4 + 8 * group)
                yield from top16([sc[:, i, :] for i in range(HP)], val1, idx1, HP)
                link(V.tensor_copy(idx1f, idx1))
                v1 = val1.rearrange("p (h two) k -> p h two k", two=2)
                i1 = idx1f.rearrange("p (h two) k -> p h two k", two=2)
                shape = [128, PH, TOPK, TOPK]
                link(V.tensor_tensor(cand, v1[:, :, 0, :].unsqueeze(3).to_broadcast(shape), v1[:, :, 1, :].unsqueeze(2).to_broadcast(shape), ALU.add))
                yield
                yield from top16([cand[:, h].rearrange("p a b -> p (a b)") for h in range(PH)], val2, idx2, PH)
                V.tensor_scalar(ab_i[:, 0], idx2, 4, None, ALU.logical_shift_right)
                link(V.tensor_scalar(ab_i[:, 1], idx2, 15, None, ALU.bitwise_and))
                link(V.tensor_copy(ab_f, ab_i))
                V.tensor_tensor(gw[:, t], val2, val2[:, :, 0:1].to_broadcast([128, PH, TOPK]), ALU.subtract).then_inc(s_e2, 1)
                for half in range(2):
                    link(V.tensor_tensor(onehot, iota.unsqueeze(1).unsqueeze(1).to_broadcast(shape), ab_f[:, half].unsqueeze(3).to_broadcast(shape), ALU.is_equal))
                    yield
                    link(V.tensor_tensor(onehot, onehot, i1[:, :, half, :].unsqueeze(2).to_broadcast(shape), ALU.mult))
                    yield
                    link(V.tensor_reduce(picked[:, half], onehot, X_AXIS, ALU.add))
                    yield
                link(V.scalar_tensor_tensor(out=eid[:, t], in0=picked[:, 0], scalar=float(PK), in1=picked[:, 1], op0=ALU.mult, op1=ALU.add))
                if t == 0:
                    dve.sem_inc(s_eid, 1)
                dve.wait_ge(s_e2x, t + 1)
                link(V.tensor_reduce(smax, gw[:, t], X_AXIS, ALU.add))
                link(V.reciprocal(smax, smax))
                link(V.tensor_tensor(gw[:, t], gw[:, t], smax.unsqueeze(2).to_broadcast([128, PH, TOPK]), ALU.mult))

            def sample_experts():
                e2, g2 = eid[:, 2].rearrange("p a b -> p (a b)"), gw[:, 2].rearrange("p a b -> p (a b)")
                for dst, src in ((eid_s, e2), (gw_s, g2)):
                    V.tensor_copy(dst[0:TS, :], src[0:TS, 0:64])
                    last = V.tensor_copy(dst[TS:128, :], src[TS:128, 64:128])
                last.then_inc(s_eid, 1)

            p_max(0)
            for u in range(8):
                p_unit(u)
            for n in range(4):
                add1(0, n)
            rms2(0)
            for n in range(4):
                modulate2(0, n)
            for _ in experts(0):
                pass

            def attention_step(i):
                if i == 0:
                    p_max(8)
                elif i <= 8:
                    p_unit(7 + i)
                elif i == 9:
                    dve.wait_ge(s_bs, 32)
                    dve.wait_ge(s_gsi, 16 * NH)
                    kt_out(0)
                    s_max(0)
                elif i <= 17:
                    s_unit(i - 10)
                elif i <= 21:
                    add1(1, i - 18)

            for r in range(128):
                dve.wait_ge(s_row[r % NROW], 16 * (r // NROW + 1))
                buf = rows_ring[:, r % NROW, :]
                V.tensor_tensor_reduce(out=buf, in0=buf, in1=H2_0, scale=1.0, scalar=0.0, op0=ALU.mult, op1=ALU.add, accum_out=dots[:, 0, r:r + 1]).then_inc(s_rowfree, 1)
                if r % 5 == 4:
                    attention_step(r // 5)
            dve.wait_ge(s_rowfree, 128)
            dve.sem_inc(s_dots, 1)

            def weights(t):
                n = NROWS[t]
                dve.wait_ge(s_gelu, t + 1)
                g = gw[:, t].rearrange("p a b -> p (a b)") if t < 2 else gw_s
                V.tensor_tensor(dots[:, t, 0:n], dots[:, t, 0:n], g, ALU.mult)
                wait(dve, s_yst, 16 * t)
                link(V.memset(acc, 0.0))

            def finish(t):
                link(V.tensor_tensor(acc, acc, GB2[:, 0, :], ALU.mult))
                V.tensor_tensor(acc, acc, x1(t), ALU.add).then_inc(s_y, 1)

            def second_pass():
                rms2(1)
                yield
                for n in range(4):
                    modulate2(1, n)
                    yield
                for _ in range(WQ_PAUSE):
                    yield
                for t in (1, 2):
                    yield from experts(t)
                sample_experts()

            weights(0)
            beside = second_pass()
            for r in range(128):
                k = 128 + r
                dve.wait_ge(s_row[k % NROW], 16 * (k // NROW + 1))
                V.scalar_tensor_tensor(out=acc, in0=rows_ring[:, k % NROW, :], scalar=dots[:, 0, r:r + 1], in1=acc, op0=ALU.mult, op1=ALU.add).then_inc(s_rowfree, 1)
                if r % 2 == 1:
                    next(beside, None)
                dve.wait_ge(s_rowfree, k + 1)
            for _ in beside:
                pass
            dve.wait_ge(s_g2, 8)
            finish(0)

            for ph, (kind, t) in list(enumerate(PHASES))[N_INLINE:]:
                base = BASE[ph]
                turn = (base - LOOP_BASE) // 8
                copies = (base - LOOP_BASE) // 16
                n = NROWS[t]
                if kind == "v":
                    weights(t)
                with dve.Fori(0, n // 16, 1) as it:
                    if kind == "v":
                        V.tensor_copy(stage_w, dots[:, t, bass.ds(it * 16, 16)]).then_inc(s_stage, 1)
                        dve.wait_ge(s_stage, it + (copies + 2))
                    for s in range(16):
                        dve.wait_ge(s_lrow[s % 8], (it * 2 + (turn + s // 8)) * 16 + 16)
                        buf = loop_row[s % 8]
                        if kind == "u":
                            V.tensor_tensor_reduce(out=buf, in0=buf, in1=h2(t), scale=1.0, scalar=0.0, op0=ALU.mult, op1=ALU.add,
                                                   accum_out=stage_a[:, s:s + 1]).then_inc(s_rowfree, 1)
                        else:
                            V.scalar_tensor_tensor(out=acc, in0=buf, scalar=stage_w[:, s:s + 1], in1=acc, op0=ALU.mult, op1=ALU.add).then_inc(s_rowfree, 1)
                            dve.wait_ge(s_rowfree, it * 16 + (base + s + 1))
                    if kind == "u":
                        dve.wait_ge(s_rowfree, it * 16 + (base + 16))
                        V.tensor_copy(dots[:, t, bass.ds(it * 16, 16)], stage_a).then_inc(s_stage, 1)
                        dve.wait_ge(s_stage, it + (copies + 2))
                if kind == "u":
                    dve.sem_inc(s_dots, 1)
                elif t == 1:
                    finish(t)
                else:
                    dve.sem_inc(s_facc, 1)
                    dve.wait_ge(s_fold, 1)
                    for i in range(4):
                        cols = slice(i * SECTION, (i + 1) * SECTION)
                        last = V.tensor_tensor(acc[0:TS, cols], PS[0:TS, i, :], GB2[0:TS, 1, cols], ALU.mult)
                    link(last)
                    V.tensor_tensor(acc[0:TS, :], acc[0:TS, :], x1(2)[0:TS, :], ALU.add).then_inc(s_y, 1)


_INS = ["x_prompt", "x_sample", "cache_kv_cmp", "cache_kv_slc", "cache_kv_win", "state_pool", "page_table", "c_prompt", "c_sample",
        "w_ada", "b_ada", "g_norm1", "g_norm2", "w_in", "w_out", "g_qnorm", "g_knorm", "cmp_pe", "w_cmp", "w_pool", "pool_scale",
        "peer_wq", "peer_subkeys", "peer_u", "peer_v"]
_OUTS = [("y_prompt", (1, TP, D)), ("y_sample", (DB, DT, D)),
         ("cmp_prompt", (1, TP, 2, NKV, HD)), ("slc_prompt", (1, TP, 2, NKV, HD)), ("win_prompt", (1, TP, 2, NKV, HD)), ("pool_prompt", (1, POOL_BUF, POOL_W)),
         ("cmp_sample", (DB, DT, 2, NKV, HD)), ("slc_sample", (DB, DT, 2, NKV, HD)), ("win_sample", (DB, PAST, 2, NKV, HD)), ("pool_sample", (DB, POOL_BUF, POOL_W))]


def kernel(**inputs):
    import concourse.bacc as bacc
    from concourse.bass_utils import run_bass_kernel_spmd
    nc = bacc.Bacc("TRN2", target_bir_lowering=False, num_devices=1)
    arrays, ins, outs = {}, {}, {}
    for name, a in [(n, np.ascontiguousarray(inputs[n])) for n in _INS] + list(constants().items()):
        arrays[f"in_{name}"] = a
        ins[name] = nc.dram_tensor(f"in_{name}", a.shape, mybir.dt.from_np(a.dtype), kind="ExternalInput").ap()
    for name, shape in _OUTS:
        outs[name] = nc.dram_tensor(f"out_{name}", shape, F32, kind="ExternalOutput").ap()
    scratch = nc.dram_tensor("gates_scratch", (TS, 3 * NH), F32).ap()
    build(nc, ins, outs, scratch)
    r = run_bass_kernel_spmd(nc, [arrays], core_ids=[0])
    return tuple(r.results[0][f"out_{name}"] for name, _ in _OUTS)
```

```python
import numpy as np

import concourse.bass as bass
from concourse import mybir
from contextlib import ExitStack

F32 = mybir.dt.float32
I32 = mybir.dt.int32
U32 = mybir.dt.uint32
ALU = mybir.AluOpType
ACT = mybir.ActivationFunctionType
X_AXIS = mybir.AxisListType.X

D = 2048
NK = D // 128
TP = 256
DB, DT = 8, 8
TS = DB * DT
TOK = TP + TS
TILES = 3
PAST, PAGE = 256, 128
HD, NKV, GROUP = 64, 4, 4
NH = NKV * GROUP
NSA_W = NH * HD
KVW = NKV * HD
POOL_W = D - NSA_W
POOL_SIZES = (2, 4, 8, 16)
POOL_GW = POOL_W // 4
POOL_BUF = 15
CMP_BLOCK, CMP_STRIDE = 32, 16
NC_ = (TP - CMP_BLOCK) // CMP_STRIDE + 1
NS_C = DB * NC_
NSEQ = DB + 2
IN_COLS = NSA_W + 6 * KVW + 3 * NH + POOL_W
COL_C, COL_S, COL_W = NSA_W, NSA_W + 2 * KVW, NSA_W + 4 * KVW
COL_GL = NSA_W + 6 * KVW
COL_U = COL_GL + 3 * NH
PH, PK, TOPK = 8, 128, 16
HP = 2 * PH
HH = PH // 2
EPS = 1e-6
SC_QK = HD ** -0.5
MASKED = -1e30
NSLOT = 8
N_LOW, NSLOT_LOW = 9, 5
N_PHYS = (DB * (PAST // PAGE) * 5) // 4
WORDS = 53208
NROW = 6
PE_ROWS = range(20, 118, 3)
GROUPS = [[0], [1, 2]]
GELU_AT = 8
KV_PAUSE, OUT_PAUSE, WQ_PAUSE = 1, 7, 16
LOOP_ROW0 = 2 * 128 - NROW
SECTION = 512
KP = 4

C_ID, C_BLK, C_SELF, C_SELT, C_FOLD, C_IOTA, C_VALID, C_ROW9 = 0, 128, 256, 280, 536, 600, 616, 618
C_N = 620


def constants():
    c = np.zeros((128, C_N), np.float32)
    p = np.arange(128)
    c[p, C_ID + p] = 1.0
    c[:, C_BLK:C_BLK + 128] = (p[:, None] // 64 == p[None, :] // 64) / 64.0
    for j in range(4):
        for b in range(DB):
            c[32 * j + b, C_SELF + b] = c[32 * j + b, C_SELF + DB + b] = 1.0
        c[32 * j + DB, C_SELF + 2 * DB] = 1.0
        c[32 * j + DB, C_SELT:C_SELT + 128] = 1.0
        for m in range(128):
            c[32 * j + (m % TS) // DT, C_SELT + 128 + m] = 1.0
    c[DB + 1, C_SELT:C_SELT + 256] = 1.0
    c[p, C_FOLD + p % 64] = 1.0
    c[:, C_IOTA:C_IOTA + 16] = np.arange(16)
    c[:, C_VALID] = p >= CMP_BLOCK - 1
    c[:, C_VALID + 1] = 1.0
    c[DB + 1, C_ROW9] = 1.0
    slopes = (2.0 ** (-8.0 * np.arange(1, NH + 1) / NH)).astype(np.float32)
    inv = 1.0 / SC_QK
    q, k = np.arange(128), np.arange(256)
    dist = (128 + q[:, None] - k[None, :])
    bias = np.where(dist[:, None] >= 0, -inv * slopes[None, :, None] * dist[:, None], MASKED)
    pos_c = np.arange(NC_) * CMP_STRIDE + CMP_BLOCK - 1
    bc = np.zeros((128, 2, 2, 8, NC_), np.float32)
    for gi in range(2):
        for t in range(2):
            for gp in range(2):
                for r in range(GROUP):
                    dc = 128 * t + q[:, None] - pos_c[None, :]
                    s = slopes[(2 * gp + gi) * GROUP + r]
                    bc[:, gi, t, gp * 4 + r] = np.where(dc >= 0, -inv * s * dc, MASKED)
    rows = np.arange(128)
    s_row, t_row = slopes[rows // DT], rows % DT
    bs = np.full((128, DB, PAST + TS), MASKED, np.float64)
    bcs = np.full((128, DB, NS_C), MASKED, np.float64)
    for b in range(DB):
        bs[:, b, :PAST] = -inv * s_row[:, None] * (PAST + t_row[:, None] - np.arange(PAST)[None])
        dn = t_row[:, None] - np.arange(DT)[None]
        bs[:, b, PAST + b * DT:PAST + (b + 1) * DT] = np.where(dn >= 0, -inv * s_row[:, None] * dn, MASKED)
        bcs[:, b, b * NC_:(b + 1) * NC_] = -inv * s_row[:, None] * (PAST + t_row[:, None] - pos_c[None])
    pool = np.zeros((128, 4, 3 * 128 + 128), np.float32)
    for i, w in enumerate(POOL_SIZES):
        for t in range(TP):
            cnt = min(w, t + 1)
            for s in range(max(0, t - w + 1), t + 1):
                v = 1.0 / cnt - (s == t)
                if t < 128:
                    pool[s, i, t] = v
                elif s < 128:
                    pool[s, i, 128 + t - 128] = v
                else:
                    pool[s - 128, i, 256 + t - 128] = v
        for b in range(DB):
            for t in range(DT):
                for s in range(t - w + 1, t + 1):
                    v = 1.0 / w - (s == t)
                    if s < 0:
                        pool[b * POOL_BUF + POOL_BUF + s, i, 384 + b * DT + t] = v
                    else:
                        pool[b * DT + s, i, 448 + b * DT + t] = v
    f = lambda a: np.ascontiguousarray(a, dtype=np.float32)
    return {"k_const": c, "k_bias": f(bias.reshape(128, -1)), "k_bias_c": f(bc.reshape(128, -1)),
            "k_bias_s": f(bs.reshape(128, -1)), "k_bias_cs": f(bcs.reshape(128, -1)),
            "k_pool": f(pool.reshape(128, -1))}


def build(nc, I, O, scratch):
    ctx = ExitStack()
    with ctx:
        arena = ctx.enter_context(nc.sbuf_tensor("arena", [128, WORDS], F32))
        PS = ctx.enter_context(nc.psum_tensor("PS", [128, 8, 512], F32))

        def sem(name):
            return ctx.enter_context(nc.semaphore(name))

        def view(at, *dims):
            n = int(np.prod(dims))
            v = arena[:, at:at + n]
            if len(dims) == 1:
                return v
            names = "abcde"[:len(dims)]
            return v.rearrange(f"p ({' '.join(names)}) -> p {' '.join(names)}",
                               **{k: d for k, d in zip(names[1:], dims[1:])})

        R_MOD, R_RING, R_H, R_Z, R_P = 0, 12288, 28672, 34816, 45816
        mod = view(R_MOD, 6 * D)
        ring = view(R_RING, NSLOT, KP, SECTION)
        hT = view(R_H, NK, 3 * 128)
        Z = view(R_Z, TILES, IN_COLS)
        X = view(R_Z, TILES, D)
        at = [R_P]

        def keep(*dims):
            v = view(at[0], *dims)
            at[0] += int(np.prod(dims))
            return v
        cst = keep(C_N)
        ident, blk = cst[:, C_ID:C_ID + 128], cst[:, C_BLK:C_BLK + 128]
        selF = cst[:, C_SELF:C_SELF + 17]
        selT = cst[:, C_SELT:C_SELT + 256].rearrange("p (a b) -> p a b", a=2)
        fold = cst[:, C_FOLD:C_FOLD + 64]
        iota = cst[:, C_IOTA:C_IOTA + 16]
        sumsq, rstd = keep(4), keep(4)
        early_at = at[0]
        A1T, B1T = keep(NK, 17), keep(NK, 17)
        g1T = keep(NK)
        gq, gk = keep(HD), keep(3, HD)
        gkc = keep(1)
        psT = keep(8)
        cT = keep(NK, 32)
        eid = view(early_at, TILES, PH, TOPK).bitcast(I32)
        gw = view(early_at + 384, TILES, PH, TOPK)
        dots = view(early_at + 768, TILES, 128)
        eid_s = view(early_at + 1152, 64).bitcast(I32)
        gw_s = view(early_at + 1216, 64)
        idxs = view(early_at + 1280, 2, 8).bitcast(I32)
        stage_a = view(early_at + 1296, 16)
        stage_w = view(early_at + 1312, 16)
        assert early_at + 1328 <= at[0]
        skT = keep(HP, PK)
        KC = keep(2, 9 * NC_)
        VCp = keep(256)
        stat = keep(40)
        b1T = stat[:, 0:2 * NK]
        qkr = keep(3, 24)
        mxv, nm, sm = keep(2, 4), keep(2, 4), keep(2, 4)
        gates_s = keep(DB, 3)
        pgi = keep(16).bitcast(I32)
        vg_at = at[0]
        VK = keep(TILES, 2, KVW)
        GK = keep(TILES, 3 * NH)
        biasC = keep(2, 16, NC_)
        PC = keep(2, 16, NC_)
        biasCS = view(vg_at + TILES * (2 * KVW + 3 * NH), DB, NS_C)
        acc = view(vg_at, D)
        assert at[0] <= WORDS, at[0]
        cin = view(R_H, D)
        sigT = view(R_H + D, NK * 9)
        sk_raw = view(R_H + 2 * D, HP, 128)
        sq_junk = view(R_Z + 3 * D, D)
        g1_raw = view(R_Z + 4 * D, 128)
        b1_raw = view(R_Z + 4 * D + 256, 128)
        ps_raw = view(R_Z + 4 * D + 128, 128)
        QT = view(R_MOD, 8, TP)
        QTs = view(R_MOD + 8 * TP, 2, DB, 4 * DT)
        KT = view(R_MOD + 8 * TOK, 2, 2, TOK)
        VCs = view(R_MOD + 8 * TOK + 4 * TOK, 256)
        CT = view(R_RING, 4, NSEQ, 256)
        WC = [view(R_RING + 10240, 2, CMP_BLOCK, HD), view(R_H, 2, CMP_BLOCK, HD)]
        cpage = view(R_RING + 14336, 4, 512)
        sq_z = view(R_H + 4096, 24, HD)
        VCT = view(R_H + 4096, 2, 9 * NC_)
        kc_sq = view(R_H + 4096 + 300, 2 * 9 * NC_)
        pe_raw = view(R_H + 5632, 512)
        poolB = view(R_RING + 14336, 4, 512)
        past_u = view(R_RING + 10240, POOL_W)
        WP = view(R_RING + 11264, 4, 2, POOL_GW)
        DTt = view(R_RING + 5120, 8, TOK)
        g2b = view(R_RING + 7680, D)
        OT = view(R_H, NK, 3 * 128)
        biasP = view(R_Z, NH, 256)
        biasP0 = view(R_RING, NH, 128)
        Pp = view(R_Z + 4096, 2, 2, 512)
        PTp = view(R_Z + 6144, 2, 1280)
        biasS = view(R_Z, DB, PAST + TS)
        kpage = [view(o, 2, 2, KVW) for o in (R_Z + 2560, R_Z + 3584, R_Z + 9968)]
        vpage = [view(o, 2, 2, KVW) for o in (R_MOD, R_MOD + 1024)]
        KTb = view(R_Z + 4608, 2, 2, 2, 256)
        Ps = view(R_Z + 6656, 2, 760)
        PTs = view(R_Z + 8176, 2, 7 * 128)
        rows_ring = view(R_RING, NROW, D)
        loop_row = [view(R_Z, D), view(R_Z + D, D)] + [rows_ring[:, (LOOP_ROW0 + i) % NROW, :] for i in range(NROW)]
        X1_0, H2_0 = view(R_RING + NROW * D, D), view(R_RING + (NROW + 1) * D, D)
        H2T_0 = view(R_RING + 4 * D, NK, 128)
        QPT_0 = view(R_RING + 5 * D, NK, 128)
        GB_0, TMP_0 = view(R_RING + (NROW + 1) * D, 2, SECTION), view(R_RING + (NROW + 1) * D + 2 * SECTION, 1, SECTION)
        X1_12 = view(R_MOD, 2, D)
        ring2 = view(R_Z, 4, KP, SECTION)
        GB_12, TMP_12 = view(R_Z + 4 * D, 2, SECTION), view(R_Z + 4 * D + 2 * SECTION, 2, SECTION)
        H2_12 = view(R_H, 2, D)
        H2T_12 = view(R_MOD + 4096, NK, 256)
        QPT_12 = [view(R_MOD + 8192, 8, 256), view(R_H + 4096, 8, 256)]
        GB2 = view(R_MOD + 4096, 2, D)
        diag = view(R_MOD + 8192, 2, 128)

        def x1(t):
            return X1_0 if t == 0 else X1_12[:, t - 1]

        def h2(t):
            return H2_0 if t == 0 else H2_12[:, t - 1]

        def scratch_of(group):
            base = R_Z + 4096 if group == 0 else R_Z
            n = len(GROUPS[group])
            sc = view(base, n, HP, PK)
            o = base + n * 2048
            k = o + 2048
            return dict(sc=sc, cand=view(o, HH, TOPK, TOPK), onehot=view(o + 1024, HH, TOPK, TOPK),
                        val1=view(k, 2 * HH, TOPK), idx1=view(k + 128, 2 * HH, TOPK).bitcast(U32), idx1f=view(k + 256, 2 * HH, TOPK),
                        val2=view(k + 384, HH, TOPK), idx2=view(k + 448, HH, TOPK).bitcast(U32), ab_i=view(k + 512, 2, HH, TOPK).bitcast(U32),
                        ab_f=view(k + 640, 2, HH, TOPK), picked=view(k + 768, 2, HH, TOPK))

        s_cst, s_cin, s_x, s_sk, s_gain = sem("consts_in"), sem("cond_in"), sem("x_in"), sem("subkeys_in"), sem("gains_in")
        s_piece = [sem(f"piece_in{i}") for i in range(NSLOT)]
        s_piece2 = [sem(f"second_piece_in{i}") for i in range(4)]
        s_free = sem("piece_used")
        s_sig, s_cps, s_cT = sem("cond_exp"), sem("cond_T_psum"), sem("cond_T_ready")
        s_adaC, s_bada = sem("ada_copied"), sem("bias_ada_in")
        s_sq, s_ms, s_rt, s_rs, s_xn = sem("squares"), sem("mean_sq"), sem("root"), sem("rstd"), sem("x_normed")
        s_gT, s_gTc = sem("gain_T_psum"), sem("gain_T")
        s_m1, s_m1c = sem("mod1_psum"), sem("mod1_ready")
        s_xt, s_hA, s_hD = sem("x_T_psum"), sem("h_prompt_ready"), sem("h_sample_ready")
        s_zA, s_zD = sem("z_tiles12_ready"), sem("z_tile0_ready")
        s_gexp, s_zms, s_zrt, s_norm = sem("gate_exp"), sem("z_mean_sq"), sem("z_root"), sem("qk_normed")
        s_wc, s_pe, s_ctz, s_pt_in = sem("w_cmp_in"), sem("cmp_pe_in"), sem("cmp_zeroed"), sem("page_table_in")
        s_cpage = [sem(f"cmp_page_in{i}") for i in range(4)]
        s_ct, s_ctc, s_cmp = sem("cmp_T_psum"), sem("cmp_T"), sem("cmp_psum")
        s_kc1, s_kcm, s_kc2, s_kc3, s_kc = sem("kc_squares"), sem("kc_mean"), sem("kc_meaned"), sem("kc_root"), sem("kc_ready")
        s_vct, s_vcp, s_vc = sem("vc_T"), sem("vc_psum"), sem("vc_ready")
        s_qt, s_qtA, s_qtD = sem("qk_T_psum"), sem("q_T"), sem("k_T")
        s_plin, s_dp, s_dt, s_yp, s_yo = sem("pool_in"), sem("pool_d_psum"), sem("pool_d"), sem("pool_y_psum"), sem("pool_y")
        s_bp0, s_bp, s_bc, s_bs = sem("bias_tile0_in"), sem("bias_prompt_in"), sem("bias_cmp_in"), sem("bias_sample_in")
        s_csc, s_cmx, s_cex, s_pc = sem("cmp_scores"), sem("cmp_shifted"), sem("cmp_exp"), sem("cmp_probs")
        s_S, s_mx, s_exp, s_pn = sem("scores"), sem("row_max"), sem("exps"), sem("probs")
        s_T, s_TA, s_TD, s_o, s_oc = sem("probs_T_psum"), sem("probs_T_a"), sem("probs_T_d"), sem("out_psum"), sem("out_ready")
        s_kpage = [sem(f"key_pages_in{i}") for i in range(3)]
        s_vpage = [sem(f"value_pages_in{i}") for i in range(2)]
        s_a2 = sem("scale2_with_gain")
        s_gso, s_gsi = sem("gates_out"), sem("gates_in")
        s_kt, s_ktA = sem("cache_kT_psum"), sem("cache_kT")
        q_S, q_mx, q_exp, q_pn = sem("smp_scores"), sem("smp_row_max"), sem("smp_exps"), sem("smp_probs")
        q_T, q_TA, q_o, q_oc = sem("smp_T_psum"), sem("smp_T"), sem("smp_out_psum"), sem("smp_out")
        s_out = sem("outputs_stored")
        s_zout = sem("z_outputs_stored")
        s_x1in = sem("x_again_in")
        s_gp, s_gb, s_x1 = sem("gate1_psum"), sem("gate1"), sem("x1_ready")
        s_sq2, s_ms2, s_rt2 = sem("squares2"), sem("mean_sq2"), sem("root2")
        s_g2in, s_m2, s_h2 = sem("g_norm2_in"), sem("mod2_psum"), sem("h2_ready")
        s_ht, s_htA = sem("h2_T_psum"), sem("h2_T")
        s_g2p, s_g2 = sem("gate2_psum"), sem("gate2")
        s_qA = sem("peer_q")
        s_skp, s_skc = sem("subkeys_T_psum"), sem("subkeys_T")
        s_scp, s_sc = sem("peer_scores_psum"), sem("peer_scores")
        s_e2, s_e2x, s_eid = sem("expert_logits"), sem("expert_exp"), sem("experts_ready")
        s_row = [sem(f"row_in{i}") for i in range(NROW)]
        s_lrow = [sem(f"loop_row_in{i}") for i in range(8)]
        s_idx, s_rowfree, s_pdma = sem("row_indices"), sem("row_used"), sem("pool_dma_go")
        s_stage, s_dots, s_gelu = sem("dots_staged"), sem("dots_ready"), sem("gelu_ready")
        s_w0, s_diag, s_prow = sem("tile0_weights"), sem("diagonal"), sem("row_added")
        s_facc, s_fold, s_y, s_yst = sem("acc_ready"), sem("folded"), sem("y_ready"), sem("y_stored")
        dve_chain = sem("dve_chain")
        n_link = [0]

        def link(ins):
            n_link[0] += 1
            ins.then_inc(dve_chain, 1)
            nc.vector.wait_ge(dve_chain, n_link[0])

        def wait(eng, s, n):
            if n > 0:
                eng.wait_ge(s, n)

        ADA_N = 6 * D // SECTION
        ADA_FIRST = 8
        w_ada_v = I["w_ada"].rearrange("(c p) n -> p c n", p=128)
        w_in_v = I["w_in"].rearrange("(c p) n -> p c n", p=128)
        w_wq_v = I["peer_wq"].rearrange("(c p) n -> p c n", p=128)
        w_out_nsa = I["w_out"][0:NSA_W, :].rearrange("(gp gi r d) n -> gp gi d r n", gp=2, gi=2, r=4)
        w_out_pool = I["w_out"][NSA_W:D, :].rearrange("(c p) n -> p c n", p=128)
        IN_SEC = [0, 512, COL_C, COL_S, COL_W, COL_U, COL_U + 512]
        NIN = len(IN_SEC)
        ADA_WITH = [2, 2, 2, 3, 3, 3, 1]
        pieces = [("ada", s, p) for s in range(ADA_FIRST) for p in range(4)]
        ada_next = ADA_FIRST
        for n in range(NIN):
            pieces += [("in", n, p) for p in range(4)]
            for _ in range(ADA_WITH[n]):
                pieces += [("ada", ada_next, p) for p in range(4)]
                ada_next += 1
        assert ada_next == ADA_N
        pieces += [("gl", 0, 0)]
        n_early = len(pieces)
        for group in range(2):
            pieces += [("out", n, p, group) for n in range(4) for p in range(4)]
            pieces += [("wq", n, p, group) for n in range(4) for p in range(4)]
        n_first = n_early + 32
        index = {p: i for i, p in enumerate(pieces)}

        slot_no = [i % NSLOT if i < n_early - N_LOW else (i - n_early + N_LOW) % NSLOT_LOW if i < n_early
                   else (i - n_early + 1) % 4 if i < n_first else NSLOT + (i - n_first) % 4 for i in range(len(pieces))]
        count, arrived, former, last_in = [0] * (NSLOT + 4), [], [], [-1] * (NSLOT + 4)
        for i, p in enumerate(pieces):
            k = slot_no[i]
            count[k] += 32 if p[0] == "out" and p[2] < 2 else 16
            arrived.append(count[k])
            former.append(last_in[k])
            last_in[k] = i
            if i == n_early - 1:
                last_early = list(last_in)

        def slot(i):
            k = slot_no[i]
            return (ring[:, k], s_piece[k]) if k < NSLOT else (ring2[:, k - NSLOT], s_piece2[k - NSLOT])

        def used(eng, kind, n, p=3, *group):
            eng.wait_ge(s_free, index[(kind, n, p, *group)] + 1)

        gl_w = view(R_RING + slot_no[index[("gl", 0, 0)]] * KP * SECTION, NK, 48)

        def load_piece(eng, i):
            kind, n, p = pieces[i][:3]
            dst, done = slot(i)
            wait(eng, s_free, former[i] + 1)
            cols = slice(n * SECTION, (n + 1) * SECTION)
            if kind == "ada":
                eng.dma_start(dst, w_ada_v[:, KP * p:KP * p + KP, cols]).then_inc(done, 16)
            elif kind == "in":
                eng.dma_start(dst, w_in_v[:, KP * p:KP * p + KP, IN_SEC[n]:IN_SEC[n] + SECTION]).then_inc(done, 16)
            elif kind == "wq":
                eng.dma_start(dst, w_wq_v[:, KP * p:KP * p + KP, cols]).then_inc(done, 16)
            elif kind == "gl":
                eng.dma_start(gl_w, w_in_v[:, :, COL_GL:COL_GL + 48]).then_inc(done, 16)
            elif p < 2:
                for gi in range(2):
                    eng.dma_start(dst[64 * gi:64 * gi + 64], w_out_nsa[p, gi, :, :, cols]).then_inc(done, 16)
            else:
                eng.dma_start(dst, w_out_pool[:, KP * (p - 2):KP * (p - 2) + KP, cols]).then_inc(done, 16)

        CBLK = [("page", m // 2, m % 2) for m in range(16)]
        CBLK[4:4] = [("prompt", DB, 0), ("prompt", DB, 1), ("pe", DB + 1, 0)]
        b_ada = I["b_ada"].rearrange("(a n) -> a n", a=1)
        b_row = slice(DB + 1, DB + 2)
        N_ZOUT = 6 + 2 + 1 + 2 * DB
        UNITS = [(t, gp, r) for t in range(2) for gp in range(2) for r in range(4)]
        SPANS = [(0, 320), (320, 640), (640, 760)]
        PHASES = [("u", 0), ("v", 0), ("u", 1), ("u", 2), ("v", 1), ("v", 2)]
        NROWS = [128, 128, 64]
        BASE = [sum(NROWS[t] for _, t in PHASES[:i]) for i in range(len(PHASES))]
        N_INLINE = 2
        LOOP_BASE = BASE[N_INLINE]

        def z_half(n, half):
            cols = slice(256 * half, 256 * half + 256)
            z = Z[0:TS, 2, IN_SEC[n]:IN_SEC[n] + SECTION]
            p = PS[64 * half:64 * half + 64, 3 * (n % 2) + 2, cols]
            if n >= 2:
                return z[:, cols], p
            return z.rearrange("p (r gi d) -> p gi r d", r=4, gi=2)[:, half], p.rearrange("p (r d) -> p r d", r=4)

        def z_section(t, n):
            v = Z[:, t, IN_SEC[n]:IN_SEC[n] + SECTION]
            return v.rearrange("p (r gi d) -> p gi r d", r=4, gi=2) if n < 2 else v

        def in_bank(t, n):
            v = PS[:, 3 * (n % 2) + t, :]
            return v.rearrange("p (gi r d) -> p gi r d", gi=2, r=4) if n < 2 else v

        block = ctx.enter_context(nc.Block())

        @block.sync
        def _(sp):
            sp.dma_start(cin[0:DB, :], I["c_sample"]).then_inc(s_cin, 16)
            sp.dma_start(cin[DB:DB + 1, :], I["c_prompt"]).then_inc(s_cin, 16)
            sp.dma_start(cst, I["k_const"]).then_inc(s_cst, 16)
            for i in range(n_early):
                load_piece(sp, i)
                if i == 4:
                    xs = I["x_sample"].rearrange("b t d -> (b t) d")
                    sp.dma_start(X[:, 0:2, :], I["x_prompt"][0].rearrange("(t p) d -> p t d", p=128)).then_inc(s_x, 16)
                    sp.dma_start(X[0:TS, 2, :], xs).then_inc(s_x, 16)
                    sp.dma_start(X[TS:128, 2, :], xs).then_inc(s_x, 16)
                    sp.dma_start(g1_raw[0:NK, :], I["g_norm1"].rearrange("(c p) -> c p", p=128)).then_inc(s_gain, 16)
                    sp.dma_start(b1_raw[0:2 * NK, :], I["b_ada"][0:2 * D].rearrange("(c p) -> c p", p=128)).then_inc(s_gain, 16)
                    sp.dma_start(ps_raw[0:8, :], I["pool_scale"].rearrange("(c p) -> c p", p=128)).then_inc(s_gain, 16)
                    sp.dma_start(gq, I["g_qnorm"].rearrange("(a d) -> a d", a=1).to_broadcast([128, HD])).then_inc(s_gain, 16)
                    sp.dma_start(gk.rearrange("p a b -> p (a b)"), I["g_knorm"].rearrange("(a k) d -> a (k d)", a=1).to_broadcast([128, 3 * HD])).then_inc(s_gain, 16)
                    for gi in range(2):
                        sp.dma_start(gkc[64 * gi:64 * gi + 64, :], I["g_knorm"][0].rearrange("(d a) -> d a", a=1)).then_inc(s_gain, 16)
                    sp.dma_start(sk_raw, I["peer_subkeys"].rearrange("p h k d -> k (p h) d")).then_inc(s_sk, 16)
                    sp.dma_start(biasC.rearrange("p a b c -> p (a b c)"), I["k_bias_c"]).then_inc(s_bc, 16)
            sp.wait_ge(s_adaC, ADA_N)
            sp.dma_start(mod[b_row, 2 * D:6 * D], b_ada[:, 2 * D:6 * D]).then_inc(s_bada, 16)
            wc = I["w_cmp"].rearrange("c (gp gi) l d e -> c gi gp d l e", gi=2)
            cmp_rows = I["cache_kv_cmp"].rearrange("n s c g d -> (n s) (c g d)")

            def cmp_weights(c):
                for gi in range(2):
                    for gp in range(2):
                        sp.dma_start(WC[c][64 * gi:64 * gi + 64, gp], wc[c, gi, gp]).then_inc(s_wc, 16)
            sp.wait_ge(s_pt_in, 16)
            sp.wait_ge(s_free, last_early[7] + 1)
            for m in range(16):
                if m >= 4:
                    sp.wait_ge(s_ct, CBLK.index(("page", (m - 4) // 2, m % 2)) + 1)
                page = sp.value_load(pgi[0:1, m:m + 1], min_val=0, max_val=N_PHYS - 1)
                sp.dma_start(cpage[:, m % 4, :], cmp_rows[bass.ds(page * PAGE, PAGE), :]).then_inc(s_cpage[m % 4], 16)
                if m == 3:
                    sp.wait_ge(s_free, max(last_early[5:7]) + 1)
                    cmp_weights(0)
                    sp.wait_ge(s_free, n_early)
                    for c in range(2):
                        sp.dma_start(pe_raw[0:CMP_BLOCK, c * 256:(c + 1) * 256], I["cmp_pe"][c].rearrange("l g d -> l (g d)")).then_inc(s_pe, 16)
                    cmp_weights(1)
            sp.wait_ge(s_ct, len(CBLK))
            sp.dma_start(poolB.rearrange("p a b -> p (a b)"), I["k_pool"]).then_inc(s_plin, 16)
            sp.wait_ge(s_cmp, 1)
            sp.dma_start(past_u[0:DB * POOL_BUF, :], I["state_pool"].rearrange("b s c -> (b s) c")).then_inc(s_plin, 16)
            for i in range(4):
                sp.dma_start(WP[:, i], I["w_pool"][i].rearrange("(c p) e -> p c e", p=128)).then_inc(s_plin, 16)
            sp.wait_ge(s_cmp, 2)
            sp.dma_start(g2b, I["g_norm2"].rearrange("(a d) -> a d", a=1).to_broadcast([128, D])).then_inc(s_g2in, 16)
            sp.dma_start(biasP0, I["k_bias"].rearrange("p (h k) -> p h k", k=256)[:, :, 128:256]).then_inc(s_bp0, 16)
            sp.wait_ge(s_yp, 8)
            sp.wait_ge(s_zout, 16 * N_ZOUT)
            sp.dma_start(biasP.rearrange("p a b -> p (a b)"), I["k_bias"]).then_inc(s_bp, 16)
            sp.wait_ge(s_a2, 1)
            for i in range(n_early, n_early + 3):
                load_piece(sp, i)
            sp.dma_start(X1_0, I["x_prompt"][0, 0:128, :]).then_inc(s_x1in, 16)
            sp.wait_ge(s_mx, 8)
            for i in range(n_early + 3, n_first):
                load_piece(sp, i)
            sp.wait_ge(s_oc, 16)
            sp.dma_start(biasS.rearrange("p a b -> p (a b)"), I["k_bias_s"]).then_inc(s_bs, 16)
            sp.dma_start(biasCS.rearrange("p a b -> p (a b)"), I["k_bias_cs"]).then_inc(s_bs, 16)
            slc_rows = I["cache_kv_slc"].rearrange("n s c g d -> (n s) c (g d)")
            win_rows = I["cache_kv_win"].rearrange("b (j s) c g d -> b s j c (g d)", j=2)
            sp.wait_ge(s_pt_in, 16)

            def cached(b, c, dst, done):
                for j in range(2):
                    page = sp.value_load(pgi[0:1, 2 * b + j:2 * b + j + 1], min_val=0, max_val=N_PHYS - 1)
                    sp.dma_start(dst[:, 0, j, :], slc_rows[bass.ds(page * PAGE, PAGE), c, :]).then_inc(done, 16)
                sp.dma_start(dst[:, 1], win_rows[b, :, :, c, :]).then_inc(done, 16)
            cached(0, 0, kpage[0], s_kpage[0])
            for b in range(DB):
                if b + 1 < DB:
                    wait(sp, s_kt, b - 1)
                    cached(b + 1, 0, kpage[(b + 1) % 3], s_kpage[(b + 1) % 3])
                wait(sp, q_o, b - 1)
                cached(b, 1, vpage[b % 2], s_vpage[b % 2])
            sp.wait_ge(q_oc, 2 * DB)
            for i in range(n_first, n_first + 4):
                load_piece(sp, i)
            sp.dma_start(X1_12[:, 0, :], I["x_prompt"][0, 128:256, :]).then_inc(s_x1in, 16)
            sp.dma_start(X1_12[0:TS, 1, :], xs).then_inc(s_x1in, 16)
            sp.dma_start(X1_12[TS:128, 1, :], xs).then_inc(s_x1in, 16)
            for i in range(n_first + 4, len(pieces)):
                load_piece(sp, i)
            for t in range(2):
                sp.wait_ge(s_y, t + 1)
                sp.dma_start(O["y_prompt"][0, t * 128:(t + 1) * 128, :], acc).then_inc(s_yst, 16)
            sp.wait_ge(s_y, 3)
            sp.dma_start(O["y_sample"].rearrange("b t d -> (b t) d"), acc[0:TS, :]).then_inc(s_yst, 16)
            sp.wait_ge(s_yst, 48)
            sp.wait_ge(s_out, 32)

        @block.gpsimd
        def _(pool):
            pool.dma_start(pgi, I["page_table"].rearrange("(a b) j -> a (b j)", a=1).to_broadcast([128, 16])).then_inc(s_pt_in, 16)
            used(pool, "in", 0, 0)
            pool.dma_start(O["win_sample"][:, 0:PAST - DT].rearrange("b s c g d -> b (s c g d)"),
                           I["cache_kv_win"][:, DT:PAST].rearrange("b s c g d -> b (s c g d)")).then_inc(s_out, 16)
            pool.dma_start(O["pool_sample"][:, 0:POOL_BUF - DT, :], I["state_pool"][:, DT:POOL_BUF, :]).then_inc(s_out, 16)
            pool.wait_ge(s_free, n_early)
            nc.gpsimd.memset(CT[:, :, DB + 1, :], 0.0).then_inc(s_ctz, 1)
            pool.wait_ge(s_norm, 1)
            for t in range(2):
                for name, col in (("cmp_prompt", COL_C), ("slc_prompt", COL_S), ("win_prompt", COL_W)):
                    pool.dma_start(O[name][0, t * 128:(t + 1) * 128].rearrange("s c g d -> s (c g d)"), Z[:, t, col:col + 512]).then_inc(s_zout, 16)
            for name, col in (("cmp_sample", COL_C), ("slc_sample", COL_S)):
                pool.dma_start(O[name].rearrange("b t c g d -> (b t) (c g d)"), Z[0:TS, 2, col:col + 512]).then_inc(s_zout, 16)
            pool.dma_start(O["pool_prompt"][0], Z[128 - POOL_BUF:128, 1, COL_U:COL_U + POOL_W]).then_inc(s_zout, 16)
            for b in range(DB):
                pool.dma_start(O["win_sample"][b, PAST - DT:PAST].rearrange("s c g d -> s (c g d)"), Z[b * DT:b * DT + DT, 2, COL_W:COL_W + 512]).then_inc(s_zout, 16)
            for b in range(DB):
                pool.dma_start(O["pool_sample"][b, POOL_BUF - DT:POOL_BUF, :], Z[b * DT:b * DT + DT, 2, COL_U:COL_U + POOL_W]).then_inc(s_zout, 16)
            pool.dma_start(scratch, GK[0:TS, 2, :]).then_inc(s_gso, 16)
            pool.wait_ge(s_gso, 16)
            sv = scratch.rearrange("(b t) (h x) -> h t b x", t=DT, x=3)
            for h in range(NH):
                pool.dma_start(gates_s[DT * h:DT * h + DT, :, :], sv[h]).then_inc(s_gsi, 16)
            tables = {"u": I["peer_u"], "v": I["peer_v"]}
            pool.wait_ge(s_eid, 1)
            for ph, (kind, t) in enumerate(PHASES[:N_INLINE]):
                ids = eid[:, t].rearrange("p a b -> p (a b)")
                for r in range(NROWS[t]):
                    k = BASE[ph] + r
                    if k == 64:
                        pool.wait_ge(s_eid, 2)
                    wait(pool, s_rowfree, k - NROW + 1)
                    if kind == "v" and r - NROW in PE_ROWS:
                        pool.wait_ge(s_prow, PE_ROWS.index(r - NROW) + 1)
                    if kind == "v" and r in PE_ROWS:
                        i = PE_ROWS.index(r)
                        if i == 0:
                            pool.wait_ge(s_w0, 1)
                            pool.wait_ge(s_scp, 12)
                        wait(pool, s_prow, i - 1)
                        nc.gpsimd.tensor_scalar(diag[:, i % 2], ident, dots[:, 0, r:r + 1], None, ALU.mult).then_inc(s_diag, 1)
                    pool.indirect_dma_start(out=rows_ring[:, k % NROW, :], out_offset=None, in_=tables[kind],
                                            in_offset=bass.IndirectOffsetOnAxis(ap=ids[:, r:r + 1], axis=0)).then_inc(s_row[k % NROW], 16)
            for ph, (kind, t) in list(enumerate(PHASES))[N_INLINE:]:
                done = BASE[ph] - LOOP_BASE
                with pool.Fori(0, NROWS[t] // 16, 1) as it:
                    for half in range(2):
                        pool.wait_ge(s_idx, it * 2 + (done // 8 + half + 1))
                        for s in range(8):
                            pool.wait_ge(s_rowfree, it * 16 + (BASE[ph] + half * 8 + s - 7))
                            pool.sem_inc(s_pdma, 1)
                            pool.indirect_dma_start(out=loop_row[s], out_offset=None, in_=tables[kind],
                                                    in_offset=bass.IndirectOffsetOnAxis(ap=idxs[:, half, s:s + 1], axis=0)).then_inc(s_lrow[s], 16)

        @block.scalar
        def _(act):
            act.wait_ge(s_cps, 1)
            nc.scalar.activation(sigT, PS[:, 0, 0:NK * 9], ACT.Exp, scale=-1.0).then_inc(s_sig, 1)
            ada_done = [0]

            def ada_out(n):
                for s in range(ada_done[0], ada_done[0] + n):
                    used(act, "ada", s)
                    nc.scalar.activation(mod[:, s * SECTION:(s + 1) * SECTION], PS[:, 6 + s % 2, :], ACT.Copy).then_inc(s_adaC, 1)
                ada_done[0] += n
            ada_out(2)
            act.wait_ge(s_x, 48)
            for t in range(TILES):
                wait(act, s_sq, t)
                nc.scalar.activation(sq_junk, X[:, t, :], ACT.Square, accum_out=sumsq[:, t:t + 1]).then_inc(s_sq, 1)
            ada_out(2)
            act.wait_ge(s_ms, 1)
            nc.scalar.activation(rstd[:, 0:3], sumsq[:, 0:3], ACT.Sqrt).then_inc(s_rt, 1)
            act.wait_ge(s_rs, 1)
            for t in range(TILES):
                nc.scalar.activation(X[:, t, :], X[:, t, :], ACT.Copy, scale=rstd[:, t:t + 1]).then_inc(s_xn, 1)
            ada_out(1)
            for c in range(NK):
                act.wait_ge(s_xt, c + 1)
                nc.scalar.activation(hT[:, c, 0:TP], PS[:, c % 2, 0:TP], ACT.Copy).then_inc(s_hA, 1)
            ada_out(3)
            act.wait_ge(s_m1c, 1)
            for c in range(NK):
                act.wait_ge(s_hA, c + 1)
                nc.scalar.activation(hT[:, c, 0:TP], hT[:, c, 0:TP], ACT.Identity, scale=A1T[:, c, 16:17], bias=B1T[:, c, 16:17]).then_inc(s_hA, 1)
            for n in range(NIN):
                used(act, "in", n)
                nc.scalar.activation(z_section(1, n), in_bank(1, n), ACT.Copy).then_inc(s_zA, 1)
                for half in range(2):
                    z, p = z_half(n, half)
                    nc.scalar.activation(z, p, ACT.Copy).then_inc(s_zA, 1)
                ada_out(ADA_WITH[n])
            used(act, "gl", 0, 0)
            for t in range(TILES):
                nc.scalar.activation(GK[:, t, :], PS[:, 3 + t, 0:48], ACT.Exp, scale=-1.0).then_inc(s_gexp, 1)

            def ct_out(m):
                kind, seq, j = CBLK[m]
                n = CMP_BLOCK if kind == "pe" else 128
                if kind == "pe":
                    act.wait_ge(s_ctz, 1)
                act.wait_ge(s_ct, m + 1)
                nc.scalar.activation(CT[:, :, seq, j * 128:j * 128 + n], PS[:, m % 4, :].rearrange("p (a b) -> p a b", a=4)[:, :, 0:n], ACT.Copy).then_inc(s_ctc, 1)
            for m in range(10):
                ct_out(m)
            act.wait_ge(s_zms, 1)
            nc.scalar.activation(qkr, qkr, ACT.Sqrt).then_inc(s_zrt, 1)
            for m in range(10, len(CBLK)):
                ct_out(m)
            act.wait_ge(s_kc2, 1)
            nc.scalar.activation(kc_sq, kc_sq, ACT.Sqrt).then_inc(s_kc3, 1)
            for t in range(TILES):
                n = 128 if t < 2 else TS
                act.wait_ge(s_qt, t + 1)
                for i in range(2):
                    src = PS[:, 3 * (t % 2) + i, :].rearrange("p (a b) -> p a b", a=4)[:, :, 0:n]
                    if t < 2:
                        nc.scalar.activation(QT[:, 4 * i:4 * i + 4, t * 128:(t + 1) * 128], src, ACT.Copy).then_inc(s_qtA, 1)
                    else:
                        nc.scalar.activation(QTs[:, i].rearrange("p b (r t) -> p r b t", r=4), src.rearrange("p r (b t) -> p r b t", t=DT), ACT.Copy).then_inc(s_qtA, 1)
            act.wait_ge(s_cmx, 1)
            nc.scalar.activation(PC, PC, ACT.Exp, scale=SC_QK).then_inc(s_cex, 1)
            act.wait_ge(s_kc, 1)
            for i in range(8):
                act.wait_ge(s_yp, i + 1)
                nc.scalar.activation(OT[:, 8 + i, 0:TOK], PS[:, 4 + i % 2, 0:TOK], ACT.Copy, scale=psT[:, i:i + 1]).then_inc(s_yo, 1)
                nc.scalar.activation(OT[:, 8 + i, TOK:384], PS[:, 4 + i % 2, TP:TOK], ACT.Copy, scale=psT[:, i:i + 1]).then_inc(s_yo, 1)

            def p_exp(u):
                t = UNITS[u][0]
                nk = 128 * (t + 1)
                act.wait_ge(s_mx, u + 1)
                for gi in range(2):
                    for br in range(2):
                        k = 2 * gi + br
                        v = Pp[:, u % 2, gi, br * nk:(br + 1) * nk]
                        nc.scalar.activation(v, v, ACT.Exp, bias=nm[:, u % 2, k:k + 1], scale=SC_QK, accum_out=sm[:, u % 2, k:k + 1]).then_inc(s_exp, 1)
            def p_unit(u):
                t, gp, r = UNITS[u]
                if u % 8 < 7:
                    p_exp(u + 1)
                act.wait_ge(s_T, u + 1)
                n = 256 * (t + 1)
                nc.scalar.activation(PTp[:, u % 2, 0:n], PS[:, 4, 0:n], ACT.Copy).then_inc(s_TA, 1)
                nc.scalar.activation(PTp[0:NC_, u % 2, 1024:1280], PS[0:NC_, 6, 0:256], ACT.Copy).then_inc(s_TA, 1)
                if t == 1:
                    nc.scalar.activation(PTp[:, u % 2, 512:512 + n], PS[:, 5, 0:n], ACT.Copy).then_inc(s_TD, 1)
                act.wait_ge(s_o, u + 1)
                nc.scalar.activation(OT[:, gp * 4 + r, t * 128:(t + 1) * 128], PS[:, 7, 0:128], ACT.Copy).then_inc(s_oc, 1)

            def gate1(group):
                buf, per = (GB_0, 1) if group == 0 else (GB_12, 2)
                for n in range(4):
                    act.wait_ge(s_gp, 4 * group + n + 1)
                    wait(act, s_x1, 4 * group + n)
                    for k in range(per):
                        nc.scalar.activation(buf[:, k], PS[:, 6 + k, :], ACT.Copy).then_inc(s_gb, 1)

            def norm2(group):
                act.wait_ge(s_x1, 4 * group + 4)
                tiles = GROUPS[group]
                for t in tiles:
                    nc.scalar.activation(h2(t), x1(t), ACT.Square, accum_out=sumsq[:, t:t + 1]).then_inc(s_sq2, 1)
                act.wait_ge(s_ms2, group + 1)
                nc.scalar.activation(rstd[:, tiles[0]:tiles[-1] + 1], sumsq[:, tiles[0]:tiles[-1] + 1], ACT.Sqrt).then_inc(s_rt2, 1)
                h2t, n = (H2T_0, 128) if group == 0 else (H2T_12, 192)
                for c in range(NK):
                    act.wait_ge(s_ht, 16 * group + c + 1)
                    nc.scalar.activation(h2t[:, c, 0:n], PS[:, c % 8, 0:n], ACT.Copy).then_inc(s_htA, 1)

            def queries(group):
                for i in range(HP):
                    if group == 1 and i == GELU_AT:
                        gelu(0)
                    used(act, "wq", i // 4, 3, group)
                    src = PS[:, i % 8, :]
                    if group == 0:
                        nc.scalar.activation(QPT_0[:, i, :], src[:, 0:128], ACT.Copy).then_inc(s_qA, 1)
                    else:
                        dst = QPT_12[i // 8][:, i % 8, :]
                        nc.scalar.activation(dst[:, 0:192], src[:, 0:192], ACT.Copy).then_inc(s_qA, 1)
                        nc.scalar.activation(dst[:, 192:256], src[:, 128:192], ACT.Copy).then_inc(s_qA, 1)
                sc = scratch_of(group)["sc"]
                for k in range(4 * len(GROUPS[group])):
                    act.wait_ge(s_scp, 4 * group + k + 1)
                    nc.scalar.activation(sc[:, k // 4, 4 * (k % 4):4 * (k % 4) + 4, :].rearrange("p a b -> p (a b)"), PS[:, k % 8, :], ACT.Copy).then_inc(s_sc, 1)

            def expert_exp(t):
                for half in range(2):
                    w = gw[:, t, half * HH:(half + 1) * HH]
                    act.wait_ge(s_e2, 2 * t + half + 1)
                    nc.scalar.activation(w, w, ACT.Exp).then_inc(s_e2x, 1)

            def gelu(t):
                act.wait_ge(s_dots, t + 1)
                nc.scalar.activation(dots[:, t, 0:NROWS[t]], dots[:, t, 0:NROWS[t]], ACT.Gelu).then_inc(s_gelu, 1)
            p_exp(0)
            for u in range(8):
                p_unit(u)
            gate1(0)
            norm2(0)
            queries(0)
            expert_exp(0)
            p_exp(8)
            for u in range(8, 16):
                p_unit(u)

            def kt_out(b):
                act.wait_ge(s_kt, b + 1)
                nc.scalar.activation(KTb[:, b % 2, 0], PS[:, 4, :].rearrange("p (a b) -> p a b", a=2), ACT.Copy).then_inc(s_ktA, 1)
                nc.scalar.activation(KTb[:, b % 2, 1], PS[:, 5, :].rearrange("p (a b) -> p a b", a=2), ACT.Copy).then_inc(s_ktA, 1)

            def s_exps(b):
                act.wait_ge(q_mx, b + 1)
                for k, (lo, hi) in enumerate(SPANS):
                    v = Ps[:, b % 2, lo:hi]
                    nc.scalar.activation(v, v, ACT.Exp, bias=nm[:, b % 2, k:k + 1], scale=SC_QK, accum_out=sm[:, b % 2, k:k + 1]).then_inc(q_exp, 1)
            kt_out(0)
            s_exps(0)
            for b in range(DB):
                if b + 1 < DB:
                    kt_out(b + 1)
                    s_exps(b + 1)
                act.wait_ge(q_T, b + 1)
                nc.scalar.activation(PTs[:, b % 2, 0:512], PS[:, 6, :], ACT.Copy).then_inc(q_TA, 1)
                nc.scalar.activation(PTs[0:TS, b % 2, 512:768], PS[0:TS, 7, 0:256], ACT.Copy).then_inc(q_TA, 1)
                nc.scalar.activation(PTs[0:NS_C, b % 2, 768:896], PS[0:NS_C, 7, 256:384], ACT.Copy).then_inc(q_TA, 1)
                act.wait_ge(q_o, b + 1)
                for dup in range(2):
                    o = TP + dup * TS + b * DT
                    nc.scalar.activation(OT[:, 0:8, o:o + DT], PS[:, 7, 448:512].rearrange("p (a b) -> p a b", a=8), ACT.Copy).then_inc(q_oc, 1)
            gate1(1)
            norm2(1)
            queries(1)
            for i in range(8):
                act.wait_ge(s_g2p, i + 1)
                nc.scalar.activation(GB2[:, i // 4, (i % 4) * SECTION:(i % 4 + 1) * SECTION], PS[:, i, :], ACT.Copy).then_inc(s_g2, 1)
            expert_exp(1)
            expert_exp(2)
            act.wait_ge(s_eid, 3)
            for ph, (kind, t) in list(enumerate(PHASES))[N_INLINE:]:
                if kind == "v":
                    gelu(t)
                src = eid[:, t].rearrange("p a b -> p (a b)") if t < 2 else eid_s
                with act.Fori(0, NROWS[t] // 16, 1) as it:
                    for half in range(2):
                        act.wait_ge(s_rowfree, it * 16 + (BASE[ph] + (half - 1) * 8))
                        nc.scalar.activation(idxs[:, half, :], src[:, bass.ds(it * 16 + half * 8, 8)], ACT.Copy).then_inc(s_idx, 1)

        @block.tensor
        def _(pe):
            def need(i):
                pe.wait_ge(slot(i)[1], arrived[i])

            def ada_section(s):
                wait(pe, s_adaC, s - 1)
                for p in range(4):
                    i = index[("ada", s, p)]
                    need(i)
                    for j in range(4):
                        last = nc.tensor.matmul(PS[32 * j:32 * j + 32, 6 + s % 2, :], cT[:, 4 * p + j, :], slot(i)[0][:, j, :],
                                                start=(p == 0), stop=(p == 3), tile_position=(0, 32 * j))
                    last.then_inc(s_free, 1)

            def warm_up(bank):
                for _ in range(4):
                    nc.tensor.matmul(PS[:, bank, :], ident, cst[:, 0:512], start=True, stop=True)

            pe.wait_ge(s_cst, 16)
            pe.wait_ge(s_cin, 32)
            for c in range(NK):
                last = nc.tensor.transpose(PS[:, 0, c * 9:c * 9 + 9], cin[0:9, c * 128:(c + 1) * 128], ident[0:9, 0:9])
            last.then_inc(s_cps, 1)
            pe.wait_ge(s_cT, 1)
            for s in range(4):
                ada_section(s)
            pe.wait_ge(s_gain, 16 * 7)
            nc.tensor.transpose(PS[:, 0, 0:NK], g1_raw[0:NK, :], ident[0:NK, 0:NK])
            nc.tensor.transpose(PS[:, 0, 24:24 + 2 * NK], b1_raw[0:2 * NK, :], ident[0:2 * NK, 0:2 * NK])
            nc.tensor.transpose(PS[:, 0, 16:24], ps_raw[0:8, :], ident[0:8, 0:8]).then_inc(s_gT, 1)
            pe.wait_ge(s_sk, 16)
            for i in range(HP):
                last = nc.tensor.transpose(PS[:, 2 + i // 4, (i % 4) * 128:(i % 4 + 1) * 128], sk_raw[:, i, :], ident)
            last.then_inc(s_skp, 1)
            ada_section(4)

            def mod1(s):
                pe.wait_ge(s_adaC, s + 1)
                for c in range(4 * (s % 4), 4 * (s % 4) + 4):
                    k = s // 4
                    last = nc.tensor.matmul(PS[:, 2 + 3 * k, c * 17:c * 17 + 17], mod[:, k * D + c * 128:k * D + (c + 1) * 128], selF, start=True, stop=True)
                return last
            pe.wait_ge(s_gTc, 1)
            pe.wait_ge(s_skc, 1)
            for s in range(4):
                mod1(s)
            pe.wait_ge(s_xn, 3)
            for c in range(NK):
                wait(pe, s_hA, c - 1)
                wait(pe, s_hD, c - 1)
                for t in range(TILES):
                    last = nc.tensor.transpose(PS[:, c % 2 + 3 * (t // 2), (t % 2) * 128:(t % 2 + 1) * 128], X[:, t, c * 128:(c + 1) * 128], ident)
                last.then_inc(s_xt, 1)
            for s in range(5, ADA_FIRST):
                ada_section(s)
                mod1(s - 1)
            mod1(ADA_FIRST - 1).then_inc(s_m1, 1)
            pe.wait_ge(s_hA, NK)
            pe.wait_ge(s_hD, NK)
            pe.wait_ge(s_m1c, 1)
            ada_i = ADA_FIRST
            for n in range(NIN):
                wait(pe, s_zA, 3 * (n - 1))
                wait(pe, s_zD, n - 1)
                for p in range(4):
                    i = index[("in", n, p)]
                    need(i)
                    if n == 0:
                        pe.wait_ge(s_hA, NK + KP * (p + 1))
                        pe.wait_ge(s_hD, NK + KP * (p + 1))
                    for t in range(2):
                        for j in range(KP):
                            c = KP * p + j
                            nc.tensor.matmul(PS[:, 3 * (n % 2) + t, :], hT[:, c, t * 128:(t + 1) * 128], slot(i)[0][:, j, :],
                                             start=(c == 0), stop=(c == NK - 1))
                    for j in range(KP):
                        c = KP * p + j
                        for half in range(2):
                            cols = slice(256 * half, 256 * half + 256)
                            last = nc.tensor.matmul(PS[64 * half:64 * half + 64, 3 * (n % 2) + 2, cols], hT[:, c, TP:TOK], slot(i)[0][:, j, cols],
                                                    start=(c == 0), stop=(c == NK - 1), tile_position=(0, 64 * half))
                    last.then_inc(s_free, 1)
                for _ in range(ADA_WITH[n]):
                    ada_section(ada_i)
                    ada_i += 1
            pe.wait_ge(s_zA, 3 * (NIN - 1))
            pe.wait_ge(s_zD, NIN - 1)
            need(index[("gl", 0, 0)])
            for t in range(TILES):
                for c in range(NK):
                    last = nc.tensor.matmul(PS[:, 3 + t, 0:48], hT[:, c, t * 128:(t + 1) * 128], gl_w[:, c, :], start=(c == 0), stop=(c == NK - 1))
            last.then_inc(s_free, 1)
            pe.wait_ge(s_zA, 3 * NIN)
            pe.wait_ge(s_zD, NIN)
            pe.wait_ge(s_gexp, 3)
            for m, (kind, seq, j) in enumerate(CBLK):
                wait(pe, s_ctc, m - 3)
                if kind == "page":
                    page = 2 * seq + j
                    pe.wait_ge(s_cpage[page % 4], 16 * (page // 4 + 1))
                    src, n = cpage[:, page % 4, :], 128
                elif kind == "prompt":
                    src, n = Z[:, j, COL_C:COL_C + 512], 128
                else:
                    pe.wait_ge(s_pe, 32)
                    src, n = pe_raw[0:CMP_BLOCK, :], CMP_BLOCK
                for k in range(4):
                    last = nc.tensor.transpose(PS[:, m % 4, k * 128:k * 128 + n], src[:, k * 128:(k + 1) * 128], ident[0:n, 0:n])
                last.then_inc(s_ct, 1)
            pe.wait_ge(s_wc, 128)
            pe.wait_ge(s_ctc, len(CBLK))
            warm_up(6)
            for c in range(2):
                for gp in range(2):
                    for l in range(CMP_BLOCK):
                        for gi in range(2):
                            h = slice(64 * gi, 64 * gi + 64)
                            last = nc.tensor.matmul(PS[h, 4 + c, gp * 150:gp * 150 + 150], WC[c][h, gp, l, :],
                                                    CT[h, 2 * c + gp, :, l:l + CMP_STRIDE * (NC_ - 1) + 1:CMP_STRIDE],
                                                    start=(l == 0), stop=(l == CMP_BLOCK - 1), tile_position=(64 * gi, 64 * gi))
                last.then_inc(s_cmp, 1)

            def turn_qk(t):
                n = 128 if t < 2 else TS
                wait(pe, s_qtA, 2 * (t - 1))
                wait(pe, s_qtD, t - 1)
                bank = 3 * (t % 2)
                for gp in range(2):
                    for r in range(4):
                        nc.tensor.transpose(PS[:, bank + gp, r * 128:r * 128 + n], Z[0:n, t, gp * 512 + r * 128:gp * 512 + (r + 1) * 128], ident[0:n, 0:n])
                for br, col in enumerate((COL_S, COL_W)):
                    for gp in range(2):
                        k = 2 * br + gp
                        last = nc.tensor.transpose(PS[:, bank + 2, k * 128:k * 128 + n], Z[0:n, t, col + gp * 128:col + (gp + 1) * 128], ident[0:n, 0:n])
                last.then_inc(s_qt, 1)
            pe.wait_ge(s_norm, 1)
            turn_qk(0)
            pe.wait_ge(s_kc1, 1)
            nc.tensor.matmul(PS[:, 6, 0:270], blk, kc_sq, start=True, stop=True).then_inc(s_kcm, 1)
            turn_qk(1)
            for gp in range(2):
                nc.tensor.transpose(PS[0:NS_C, 7, gp * 128:(gp + 1) * 128], VCT[:, gp, 0:NS_C], ident)
            for gp in range(2):
                last = nc.tensor.transpose(PS[0:NC_, 7, 256 + gp * 128:256 + (gp + 1) * 128], VCT[:, gp, NS_C:NS_C + NC_], ident)
            last.then_inc(s_vcp, 1)
            turn_qk(2)
            pe.wait_ge(s_kc, 1)
            pe.wait_ge(s_vc, 1)
            pe.wait_ge(s_qtA, 6)
            pe.wait_ge(s_qtD, 3)
            for t in range(2):
                for k in range(8):
                    for gi in range(2):
                        h = slice(64 * gi, 64 * gi + 64)
                        last = nc.tensor.matmul(PS[:, 6 + gi, (t * 8 + k) * NC_:(t * 8 + k + 1) * NC_], QT[h, k, t * 128:(t + 1) * 128],
                                                KC[h, k // 4, NS_C:NS_C + NC_], start=True, stop=True, tile_position=(64 * gi, 0))
            last.then_inc(s_csc, 1)
            pe.wait_ge(s_plin, 16 * 6)
            for c in range(8):
                w = c // 2
                wait(pe, s_dt, c - 3)
                u = [Z[:, t, COL_U + c * 128:COL_U + (c + 1) * 128] for t in range(TILES)]
                bank = PS[:, c % 4, :]
                nc.tensor.matmul(bank[:, 0:128], u[0], poolB[:, w, 0:128], start=True, stop=True)
                nc.tensor.matmul(bank[:, 128:256], u[0], poolB[:, w, 128:256], start=True, stop=False)
                nc.tensor.matmul(bank[:, 128:256], u[1], poolB[:, w, 256:384], start=False, stop=True)
                n = DB * POOL_BUF
                nc.tensor.matmul(bank[:, 256:320], past_u[0:n, c * 128:(c + 1) * 128], poolB[0:n, w, 384:448], start=True, stop=False)
                nc.tensor.matmul(bank[:, 256:320], u[2][0:TS, :], poolB[0:TS, w, 448:512], start=False, stop=True).then_inc(s_dp, 1)
            pe.wait_ge(s_dt, 8)
            for i in range(8):
                w, eh = i // 2, i % 2
                wait(pe, s_yo, 2 * (i - 1))
                for ch in range(2):
                    last = nc.tensor.matmul(PS[:, 4 + i % 2, 0:TOK], WP[:, w, ch, eh * 128:(eh + 1) * 128], DTt[:, 2 * w + ch, :], start=(ch == 0), stop=(ch == 1))
                last.then_inc(s_yp, 1)
            pe.wait_ge(s_yo, 16)
            pe.wait_ge(s_cmx, 1)

            def p_scores(u):
                t, gp, r = UNITS[u]
                nk = 128 * (t + 1)
                wait(pe, s_mx, u - 1)
                for br in range(2):
                    for gi in range(2):
                        h = slice(64 * gi, 64 * gi + 64)
                        last = nc.tensor.matmul(PS[:, 2 * (u % 2) + gi, br * nk:(br + 1) * nk], QT[h, gp * 4 + r, t * 128:(t + 1) * 128],
                                                KT[h, br, gp, 0:nk], start=True, stop=True, tile_position=(64 * gi, 0))
                last.then_inc(s_S, 1)

            def p_unit(u):
                t, gp, r = UNITS[u]
                pe.wait_ge(s_pn, u + 1)
                wait(pe, s_TA, 2 * u)
                wait(pe, s_TD, u)
                for gi in range(2):
                    for k in range(2 * (t + 1)):
                        nc.tensor.transpose(PS[:, 4 + gi, k * 128:(k + 1) * 128], Pp[:, u % 2, gi, k * 128:(k + 1) * 128], ident)
                    last = nc.tensor.transpose(PS[0:NC_, 6, gi * 128:(gi + 1) * 128], PC[:, gi, t * 8 + gp * 4 + r, :], ident)
                last.then_inc(s_T, 1)
                if u % 8 < 6:
                    p_scores(u + 2)
                pe.wait_ge(s_TA, 2 * u + 2)
                pe.wait_ge(s_TD, u + 1)
                wait(pe, s_oc, u)
                for gi in range(2):
                    g = 2 * gp + gi
                    o = PS[64 * gi:64 * gi + 64, 7, 0:128]
                    nc.tensor.matmul(o, VCp[0:NC_, g * 64:(g + 1) * 64], PTp[0:NC_, u % 2, 1024 + gi * 128:1024 + (gi + 1) * 128], start=True, stop=False, tile_position=(0, 64 * gi))
                    for br in range(2):
                        for k in range(t + 1):
                            c = br * (t + 1) + k
                            last = nc.tensor.matmul(o, VK[:, k, br, g * 64:(g + 1) * 64], PTp[:, u % 2, gi * 512 + c * 128:gi * 512 + (c + 1) * 128],
                                                    start=False, stop=(br == 1 and k == t), tile_position=(0, 64 * gi))
                last.then_inc(s_o, 1)

            def project(group):
                tiles = GROUPS[group]
                for n in range(4):
                    wait(pe, s_gb, n if group == 0 else 4 + 2 * n)
                    for k in range(len(tiles)):
                        last = nc.tensor.matmul(PS[:, 6 + k, :], selT[:, k, :], mod[:, 2 * D + n * SECTION:2 * D + (n + 1) * SECTION], start=True, stop=True)
                    last.then_inc(s_gp, 1)
                    wait(pe, s_x1, 4 * group + n - 1)
                    for p in range(4):
                        i = index[("out", n, p, group)]
                        need(i)
                        for k, t in enumerate(tiles):
                            for j in range(KP):
                                c = KP * p + j
                                last = nc.tensor.matmul(PS[:, 3 * (n % 2) + k, :], OT[:, c, t * 128:(t + 1) * 128], slot(i)[0][:, j, :],
                                                        start=(c == 0), stop=(c == NK - 1))
                        last.then_inc(s_free, 1)

            def norm2(group):
                tiles = GROUPS[group]
                for n in range(4):
                    pe.wait_ge(s_x1, 4 * group + 4)
                    wait(pe, s_h2, 4 * group + n - 1)
                    for m, chunk in enumerate((4, 3)):
                        for k in range(len(tiles)):
                            last = nc.tensor.matmul(PS[:, 4 * (n % 2) + 2 * m + k, :], selT[:, k, :], mod[:, chunk * D + n * SECTION:chunk * D + (n + 1) * SECTION], start=True, stop=True)
                    last.then_inc(s_m2, 1)
                pe.wait_ge(s_h2, 4 * group + 4)
                for c in range(NK):
                    wait(pe, s_htA, 16 * group + c - 7 if c >= 8 else 0)
                    for k, t in enumerate(tiles):
                        n = 128 if t < 2 else TS
                        last = nc.tensor.transpose(PS[:, c % 8, k * 128:k * 128 + n], h2(t)[0:n, c * 128:(c + 1) * 128], ident[0:n, 0:n])
                    last.then_inc(s_ht, 1)
                pe.wait_ge(s_htA, 16 * group + 16)

            def queries(group):
                tiles = GROUPS[group]
                h2t, w = (H2T_0, 128) if group == 0 else (H2T_12, 192)
                for n in range(4):
                    wait(pe, s_qA, 0 if n < 2 else 4 * (n - 1) if group == 0 else 16 + 8 * (n - 1))
                    for p in range(4):
                        i = index[("wq", n, p, group)]
                        need(i)
                        for m in range(4):
                            for j in range(KP):
                                c = KP * p + j
                                last = nc.tensor.matmul(PS[:, 4 * (n % 2) + m, 0:w], slot(i)[0][:, j, m * 128:(m + 1) * 128], h2t[:, c, 0:w],
                                                        start=(c == 0), stop=(c == NK - 1))
                        last.then_inc(s_free, 1)
                pe.wait_ge(s_qA, 16 + 32 * group)
                for k in range(4 * len(tiles)):
                    for i in range(4):
                        hp = 4 * (k % 4) + i
                        h, p = hp // 2, hp % 2
                        q = QPT_0[:, hp, :] if group == 0 else QPT_12[hp // 8][:, hp % 8, k // 4 * 128:(k // 4 + 1) * 128]
                        last = nc.tensor.matmul(PS[:, k % 8, i * 128:(i + 1) * 128], q, skT[:, p * PH + h, :], start=True, stop=True)
                    last.then_inc(s_scp, 1)
                pe.wait_ge(s_sc, 4 + 8 * group)
            pe.wait_ge(s_pc, 1)
            p_scores(0)
            p_scores(1)
            for u in range(8):
                p_unit(u)
            pe.wait_ge(s_oc, 8)
            pe.wait_ge(s_a2, 1)
            project(0)
            norm2(0)
            queries(0)
            p_scores(8)
            p_scores(9)
            for u in range(8, 16):
                p_unit(u)
            pe.wait_ge(s_oc, 16)

            def s_keys(b):
                pe.wait_ge(s_kpage[b % 3], 48 * (b // 3 + 1))
                wait(pe, s_ktA, 2 * b)
                for br in range(2):
                    for gp in range(2):
                        for j in range(2):
                            last = nc.tensor.transpose(PS[:, 4 + br, gp * 256 + j * 128:gp * 256 + (j + 1) * 128], kpage[b % 3][:, br, j, gp * 128:(gp + 1) * 128], ident)
                last.then_inc(s_kt, 1)

            def s_scores(b):
                pe.wait_ge(s_ktA, 2 * b + 2)
                wait(pe, q_mx, b - 1)
                for g in range(4):
                    gp, gi = g // 2, g % 2
                    h, o = slice(64 * gi, 64 * gi + 64), slice(32 * g, 32 * g + 32)
                    q = QTs[h, gp, b, :]
                    kw = dict(start=True, stop=True, tile_position=(64 * gi, 32 * g))
                    for br in range(2):
                        bank = PS[o, 2 * (b % 2) + br, :]
                        nc.tensor.matmul(bank[:, 0:PAST], q, KTb[h, b % 2, br, gp, :], **kw)
                        nc.tensor.matmul(bank[:, PAST:PAST + TS], q, KT[h, br, gp, TP:TOK], **kw)
                    last = nc.tensor.matmul(bank[:, 320:440], q, KC[h, gp, 0:NS_C], **kw)
                last.then_inc(q_S, 1)
            s_keys(0)
            s_scores(0)
            for b in range(DB):
                if b + 1 < DB:
                    s_keys(b + 1)
                    s_scores(b + 1)
                pe.wait_ge(q_pn, b + 1)
                wait(pe, q_TA, 3 * b)
                wait(pe, q_oc, 2 * b)
                P = Ps[:, b % 2, :]
                for k, at_ in enumerate((0, 128, 320, 448)):
                    nc.tensor.transpose(PS[:, 6, k * 128:(k + 1) * 128], P[:, at_:at_ + 128], ident)
                for k, at_ in enumerate((256, 576)):
                    nc.tensor.transpose(PS[0:TS, 7, k * 128:(k + 1) * 128], P[:, at_:at_ + TS], ident)
                nc.tensor.transpose(PS[0:NS_C, 7, 256:384], P[:, 640:760], ident).then_inc(q_T, 1)
                pe.wait_ge(q_TA, 3 * b + 3)
                pe.wait_ge(s_vpage[b % 2], 48 * (b // 2 + 1))
                for g in range(4):
                    gp, gi = g // 2, g % 2
                    o = PS[64 * gi:64 * gi + 64, 7, 448 + gp * 32:448 + gp * 32 + 32]
                    pt = PTs[:, b % 2, :].rearrange("p (a b) -> p a b", a=7)[:, :, 32 * g:32 * g + 32]
                    v = slice(g * 64, (g + 1) * 64)
                    steps = [(vpage[b % 2][:, br, j, v], pt[:, 2 * br + j]) for br in range(2) for j in range(2)]
                    steps += [(VK[0:TS, 2, br, g * 64:(g + 1) * 64], pt[0:TS, 4 + br]) for br in range(2)]
                    steps += [(VCs[0:NS_C, g * 64:(g + 1) * 64], pt[0:NS_C, 6])]
                    for i, (lhs, rhs) in enumerate(steps):
                        last = nc.tensor.matmul(o, lhs, rhs, start=(i == 0), stop=(i == len(steps) - 1), tile_position=(0, 64 * gi))
                last.then_inc(q_o, 1)
            pe.wait_ge(q_oc, 2 * DB)
            project(1)
            norm2(1)
            queries(1)
            for i in range(8):
                nc.tensor.matmul(PS[:, i, :], selT[:, i // 4, :], mod[:, 5 * D + (i % 4) * SECTION:5 * D + (i % 4 + 1) * SECTION], start=True, stop=True).then_inc(s_g2p, 1)
            pe.wait_ge(s_g2, 8)
            for i, r in enumerate(PE_ROWS):
                k = 128 + r
                pe.wait_ge(s_row[k % NROW], 16 * (k // NROW + 1))
                pe.wait_ge(s_diag, i + 1)
                for n in range(4):
                    last = nc.tensor.matmul(PS[:, n, :], diag[:, i % 2], rows_ring[:, k % NROW, n * SECTION:(n + 1) * SECTION],
                                            start=(i == 0), stop=(i == len(PE_ROWS) - 1))
                last.then_inc(s_prow, 1)
            pe.wait_ge(s_facc, 1)
            for n in range(4):
                last = nc.tensor.matmul(PS[0:TS, n, :], fold, acc[:, n * SECTION:(n + 1) * SECTION], start=True, stop=True)
            last.then_inc(s_fold, 1)

        @block.vector
        def _(dve):
            V = nc.vector
            V.memset(cT, 0.0).then_inc(s_stage, 1)
            dve.wait_ge(s_sig, 1)
            link(V.tensor_scalar(sigT, sigT, 1.0, None, ALU.add))
            link(V.reciprocal(sigT, sigT))
            dve.wait_ge(s_stage, 1)
            V.tensor_tensor(cT[:, :, 0:9], PS[:, 0, 0:NK * 9].rearrange("p (a b) -> p a b", b=9), sigT.rearrange("p (a b) -> p a b", b=9), ALU.mult).then_inc(s_cT, 1)
            dve.wait_ge(s_sq, 3)
            V.tensor_scalar(sumsq[:, 0:3], sumsq[:, 0:3], 1.0 / D, EPS, ALU.mult, ALU.add).then_inc(s_ms, 1)
            dve.wait_ge(s_rt, 1)
            V.reciprocal(rstd[:, 0:3], rstd[:, 0:3]).then_inc(s_rs, 1)
            dve.wait_ge(s_gT, 1)
            V.tensor_copy(psT, PS[:, 0, 16:24])
            V.tensor_copy(b1T, PS[:, 0, 24:24 + 2 * NK])
            V.tensor_copy(g1T, PS[:, 0, 0:16]).then_inc(s_gTc, 1)
            dve.wait_ge(s_skp, 1)
            for i in range(4):
                last = V.tensor_copy(skT[:, 4 * i:4 * i + 4, :].rearrange("p a b -> p (a b)"), PS[:, 2 + i, :])
            last.then_inc(s_skc, 1)
            for c in range(NK):
                dve.wait_ge(s_xt, c + 1)
                V.tensor_copy(hT[:, c, TP:TOK], PS[:, 3 + c % 2, 0:TS]).then_inc(s_hD, 1)
            dve.wait_ge(s_m1, 1)
            dve.wait_ge(s_gTc, 1)
            bank = [PS[:, 2 + 3 * k, 0:272].rearrange("p (a b) -> p a b", b=17) for k in range(2)]
            b1 = b1T.rearrange("p (k c) -> p k c", k=2)
            for k, to in enumerate((B1T, A1T)):
                last = V.tensor_tensor(to, bank[k], b1[:, k].unsqueeze(2).to_broadcast([128, NK, 17]), ALU.add)
            link(last)
            V.scalar_tensor_tensor(out=A1T, in0=A1T, scalar=1.0, in1=g1T.unsqueeze(2).to_broadcast([128, NK, 17]), op0=ALU.add, op1=ALU.mult).then_inc(s_m1c, 1)
            dve.wait_ge(s_m1c, 1)
            for c in range(NK):
                o = hT[:, c, TP:TOK].rearrange("p (b t) -> p b t", t=DT)
                twice = hT[:, c, TOK:384].rearrange("p (b t) -> p b t", t=DT)
                A, B = [v[:, c, 0:DB].unsqueeze(2).to_broadcast([128, DB, DT]) for v in (A1T, B1T)]
                dve.wait_ge(s_hD, c + 1)
                link(V.tensor_tensor(o, o, A, ALU.mult))
                V.tensor_tensor(twice, o, B, ALU.add)
                V.tensor_tensor(o, o, B, ALU.add).then_inc(s_hD, 1)
            for n in range(NIN):
                used(dve, "in", n)
                V.tensor_copy(z_section(0, n), in_bank(0, n)).then_inc(s_zD, 1)
            dve.wait_ge(s_gexp, 3)
            dve.wait_ge(s_zA, 3 * NIN)
            link(V.tensor_scalar(GK, GK, 1.0, None, ALU.add))
            V.reciprocal(GK, GK)
            for t in range(TILES):
                n = 128 if t < 2 else TS
                for br, col in enumerate((COL_S, COL_W)):
                    V.tensor_copy(VK[0:n, t, br, :], Z[0:n, t, col + KVW:col + 2 * KVW])
            parts = [(0, 0, NH), (COL_S, NH, NKV), (COL_W, NH + NKV, NKV)]
            V.memset(qkr[:, 2, :], float(HD))
            for t in range(TILES):
                m = 128 if t < 2 else TS
                for col, h0, n in parts:
                    v = Z[0:m, t, col:col + n * HD].rearrange("p (h d) -> p h d", d=HD)
                    last = V.tensor_tensor(sq_z[0:m, h0:h0 + n, :], v, v, ALU.mult)
                link(last)
                link(V.tensor_reduce(qkr[0:m, t, :], sq_z[0:m], X_AXIS, ALU.add))
            V.tensor_scalar(qkr, qkr, 1.0 / HD, EPS, ALU.mult, ALU.add).then_inc(s_zms, 1)
            dve.wait_ge(s_zrt, 1)
            link(V.reciprocal(qkr, qkr))
            for t in range(TILES):
                m = 128 if t < 2 else TS
                for col, h0, n in parts:
                    v = Z[0:m, t, col:col + n * HD].rearrange("p (h d) -> p h d", d=HD)
                    last = V.tensor_tensor(v, v, qkr[0:m, t, h0:h0 + n].unsqueeze(2).to_broadcast([m, n, HD]), ALU.mult)
            link(last)
            for t in range(TILES):
                m = 128 if t < 2 else TS
                for k, (col, h0, n) in enumerate(parts):
                    v = Z[0:m, t, col:col + n * HD].rearrange("p (h d) -> p h d", d=HD)
                    g = gq if k == 0 else gk[:, k, :]
                    last = V.tensor_tensor(v, v, g[0:m].unsqueeze(1).to_broadcast([m, n, HD]), ALU.mult)
            last.then_inc(s_norm, 1)
            dve.wait_ge(s_cmp, 2)
            for c, to in ((0, KC), (1, VCT)):
                for gp in range(2):
                    last = V.tensor_scalar(to[:, gp, :], PS[:, 4 + c, gp * 150:gp * 150 + 135], PS[:, 4 + c, gp * 150 + 135:gp * 150 + 136], None, ALU.add)
            last.then_inc(s_vct, 1)
            dve.wait_ge(s_vct, 1)
            kcf = KC.rearrange("p a b -> p (a b)")
            V.tensor_tensor(kc_sq, kcf, kcf, ALU.mult).then_inc(s_kc1, 1)
            dve.wait_ge(s_kcm, 1)
            V.tensor_scalar(kc_sq, PS[:, 6, 0:270], EPS, None, ALU.add).then_inc(s_kc2, 1)
            dve.wait_ge(s_kc3, 1)
            link(V.reciprocal(kc_sq, kc_sq))
            link(V.tensor_tensor(kcf, kcf, kc_sq, ALU.mult))
            V.tensor_scalar(kcf, kcf, gkc[:, 0:1], None, ALU.mult).then_inc(s_kc, 1)
            dve.wait_ge(s_vcp, 1)
            V.tensor_copy(VCs[0:NS_C, :], PS[0:NS_C, 7, 0:256])
            V.tensor_copy(VCp[0:NC_, :], PS[0:NC_, 7, 256:512]).then_inc(s_vc, 1)
            for t in range(TILES):
                n = 128 if t < 2 else TS
                dve.wait_ge(s_qt, t + 1)
                V.tensor_copy(KT[:, :, :, t * 128:t * 128 + n].rearrange("p a b c -> p (a b) c"),
                              PS[:, 3 * (t % 2) + 2, :].rearrange("p (a b) -> p a b", a=4)[:, :, 0:n]).then_inc(s_qtD, 1)
            dve.wait_ge(s_csc, 1)
            dve.wait_ge(s_bc, 16)
            for gi in range(2):
                last = V.tensor_tensor(PC[:, gi], PS[:, 6 + gi, 0:16 * NC_].rearrange("p (a b) -> p a b", a=16), biasC[:, gi], ALU.add)
            link(last)
            cmax = stat[:, 0:32].rearrange("p (a b) -> p a b", a=2)
            link(V.tensor_reduce(cmax, PC, X_AXIS, ALU.max))
            V.tensor_tensor(PC.rearrange("p a b c -> p (a b) c"), PC.rearrange("p a b c -> p (a b) c"), stat[:, 0:32].unsqueeze(2).to_broadcast([128, 32, NC_]), ALU.subtract).then_inc(s_cmx, 1)
            dve.wait_ge(s_cex, 1)
            link(V.tensor_reduce(cmax, PC, X_AXIS, ALU.add))
            link(V.reciprocal(stat[:, 0:32], stat[:, 0:32]))
            for gi in range(2):
                for t in range(2):
                    gate = GK[:, t, :].rearrange("p (gp gi r x) -> p gp gi r x", gp=2, gi=2, r=4)[:, :, gi, :, 0]
                    c = cmax[:, gi, t * 8:t * 8 + 8].rearrange("p (a b) -> p a b", a=2)
                    last = V.scalar_tensor_tensor(out=c, in0=gate, scalar=cst[:, C_VALID + t:C_VALID + t + 1], in1=c, op0=ALU.mult, op1=ALU.mult)
            link(last)
            V.tensor_tensor(PC.rearrange("p a b c -> p (a b) c"), PC.rearrange("p a b c -> p (a b) c"), stat[:, 0:32].unsqueeze(2).to_broadcast([128, 32, NC_]), ALU.mult).then_inc(s_pc, 1)
            for c in range(8):
                dve.wait_ge(s_dp, c + 1)
                V.tensor_copy(DTt[:, c, :], PS[:, c % 4, 0:TOK]).then_inc(s_dt, 1)

            dve.wait_ge(s_bada, 16)
            dve.wait_ge(s_g2in, 16)
            V.scalar_tensor_tensor(out=mod[:, 4 * D:5 * D], in0=mod[:, 4 * D:5 * D], scalar=cst[:, C_ROW9:C_ROW9 + 1], in1=g2b, op0=ALU.add, op1=ALU.mult).then_inc(s_a2, 1)


            def p_max(u):
                t, gp, r = UNITS[u]
                nk = 128 * (t + 1)
                if u % 8 == 0:
                    dve.wait_ge(s_bp if t else s_bp0, 16)
                dve.wait_ge(s_S, u + 1)
                wait(dve, s_T, u - 1)
                for gi in range(2):
                    h = (2 * gp + gi) * GROUP + r
                    for br in range(2):
                        k = 2 * gi + br
                        last = V.tensor_tensor_reduce(out=Pp[:, u % 2, gi, br * nk:(br + 1) * nk], in0=PS[:, 2 * (u % 2) + gi, br * nk:(br + 1) * nk],
                                                      in1=biasP[:, h, :] if t else biasP0[:, h, :], scale=1.0, scalar=-3.0e38, op0=ALU.add, op1=ALU.max, accum_out=mxv[:, u % 2, k:k + 1])
                link(last)
                V.tensor_scalar(nm[:, u % 2, 0:4], mxv[:, u % 2, 0:4], -SC_QK, None, ALU.mult).then_inc(s_mx, 1)

            def p_norm(u):
                t, gp, r = UNITS[u]
                nk = 128 * (t + 1)
                dve.wait_ge(s_exp, 4 * u + 4)
                link(V.reciprocal(sm[:, u % 2, 0:4], sm[:, u % 2, 0:4]))
                gate = GK[:, t, :].rearrange("p (gp gi r x) -> p gp gi r x", gp=2, gi=2, r=4)[:, gp, :, r, 1:3]
                s4 = sm[:, u % 2, 0:4].rearrange("p (a b) -> p a b", a=2)
                link(V.tensor_tensor(s4, s4, gate, ALU.mult))
                for k in range(4):
                    v = Pp[:, u % 2, k // 2, (k % 2) * nk:(k % 2 + 1) * nk]
                    last = V.tensor_scalar(v, v, sm[:, u % 2, k:k + 1], None, ALU.mult)
                last.then_inc(s_pn, 1)

            def p_turn(u):
                dve.wait_ge(s_T, u + 1)
                n = 256 * (UNITS[u][0] + 1)
                V.tensor_copy(PTp[:, u % 2, 512:512 + n], PS[:, 5, 0:n]).then_inc(s_TD, 1)


            def s_max(b):
                dve.wait_ge(q_S, b + 1)
                wait(dve, q_T, b - 1)
                src = [PS[:, 2 * (b % 2), 0:320], PS[:, 2 * (b % 2) + 1, 0:320], PS[:, 2 * (b % 2) + 1, 320:440]]
                bias = [biasS[:, b], biasS[:, b], biasCS[:, b]]
                for k, (lo, hi) in enumerate(SPANS):
                    last = V.tensor_tensor_reduce(out=Ps[:, b % 2, lo:hi], in0=src[k], in1=bias[k], scale=1.0, scalar=-3.0e38, op0=ALU.add, op1=ALU.max, accum_out=mxv[:, b % 2, k:k + 1])
                link(last)
                V.tensor_scalar(nm[:, b % 2, 0:3], mxv[:, b % 2, 0:3], -SC_QK, None, ALU.mult).then_inc(q_mx, 1)

            def smp_norm(b):
                dve.wait_ge(q_exp, 3 * b + 3)
                link(V.reciprocal(sm[:, b % 2, 0:3], sm[:, b % 2, 0:3]))
                for k, x in enumerate((1, 2, 0)):
                    last = V.tensor_tensor(sm[:, b % 2, k:k + 1], sm[:, b % 2, k:k + 1], gates_s[:, b, x:x + 1], ALU.mult)
                link(last)
                for k, (lo, hi) in enumerate(SPANS):
                    last = V.tensor_scalar(Ps[:, b % 2, lo:hi], Ps[:, b % 2, lo:hi], sm[:, b % 2, k:k + 1], None, ALU.mult)
                last.then_inc(q_pn, 1)

            def add1(group, n):
                tiles = GROUPS[group]
                gb, tmp = (GB_0, TMP_0) if group == 0 else (GB_12, TMP_12)
                if n == 0:
                    dve.wait_ge(s_x1in, 16 + 48 * group)
                used(dve, "out", n, 3, group)
                dve.wait_ge(s_gb, n + 1 if group == 0 else 4 + 2 * n + 2)
                for k in range(len(tiles)):
                    last = V.tensor_tensor(tmp[:, k], PS[:, 3 * (n % 2) + k, :], gb[:, k], ALU.mult)
                link(last)
                for k, t in enumerate(tiles):
                    v = x1(t)[:, n * SECTION:(n + 1) * SECTION]
                    last = V.tensor_tensor(v, v, tmp[:, k], ALU.add)
                last.then_inc(s_x1, 1)
                dve.wait_ge(s_x1, 4 * group + n + 1)

            def rms2(group):
                lo, hi = GROUPS[group][0], GROUPS[group][-1] + 1
                dve.wait_ge(s_sq2, hi)
                V.tensor_scalar(sumsq[:, lo:hi], sumsq[:, lo:hi], 1.0 / D, EPS, ALU.mult, ALU.add).then_inc(s_ms2, 1)
                dve.wait_ge(s_rt2, group + 1)
                link(V.reciprocal(rstd[:, lo:hi], rstd[:, lo:hi]))

            def modulate2(group, n):
                cols = slice(n * SECTION, (n + 1) * SECTION)
                bank = 4 * (n % 2)
                dve.wait_ge(s_m2, 4 * group + n + 1)
                for k, t in enumerate(GROUPS[group]):
                    last = V.scalar_tensor_tensor(out=h2(t)[:, cols], in0=x1(t)[:, cols], scalar=rstd[:, t:t + 1], in1=PS[:, bank + k, :], op0=ALU.mult, op1=ALU.mult)
                link(last)
                for k, t in enumerate(GROUPS[group]):
                    last = V.tensor_tensor(h2(t)[:, cols], h2(t)[:, cols], PS[:, bank + 2 + k, :], ALU.add)
                last.then_inc(s_h2, 1)

            def top16(vals, val, idx, n):
                for lo in (0, 8):
                    for i in range(n):
                        last = V.max(val[:, i, lo:lo + 8], vals[i])
                        if i % 4 == 3:
                            yield
                    link(last)
                    for i in range(n):
                        last = V.max_index(idx[:, i, lo:lo + 8], val[:, i, lo:lo + 8], vals[i])
                        if i % 4 == 3:
                            yield
                    link(last)
                    if lo == 0:
                        for i in range(n):
                            last = V.match_replace(vals[i], val[:, i, 0:8], vals[i], -3.0e38)
                            if i % 4 == 3:
                                yield
                        link(last)

            def experts(t, half):
                group = 0 if t == 0 else 1
                heads = slice(half * HH, (half + 1) * HH)
                b = scratch_of(group)
                sc, cand, onehot, picked, ab_i, ab_f = b["sc"][:, GROUPS[group].index(t)], b["cand"], b["onehot"], b["picked"], b["ab_i"], b["ab_f"]
                val1, idx1, idx1f, val2, idx2, smax = b["val1"], b["idx1"], b["idx1f"], b["val2"], b["idx2"], stat[:, 0:HH]
                dve.wait_ge(s_sc, 4 + 8 * group)
                yield from top16([sc[:, 2 * HH * half + i, :] for i in range(2 * HH)], val1, idx1, 2 * HH)
                link(V.tensor_copy(idx1f, idx1))
                v1 = val1.rearrange("p (h two) k -> p h two k", two=2)
                i1 = idx1f.rearrange("p (h two) k -> p h two k", two=2)
                shape = [128, HH, TOPK, TOPK]
                link(V.tensor_tensor(cand, v1[:, :, 0, :].unsqueeze(3).to_broadcast(shape), v1[:, :, 1, :].unsqueeze(2).to_broadcast(shape), ALU.add))
                yield
                yield from top16([cand[:, h].rearrange("p a b -> p (a b)") for h in range(HH)], val2, idx2, HH)
                V.tensor_scalar(ab_i[:, 0], idx2, 4, None, ALU.logical_shift_right)
                link(V.tensor_scalar(ab_i[:, 1], idx2, 15, None, ALU.bitwise_and))
                link(V.tensor_copy(ab_f, ab_i))
                w = gw[:, t, heads]
                V.tensor_tensor(w, val2, val2[:, :, 0:1].to_broadcast([128, HH, TOPK]), ALU.subtract).then_inc(s_e2, 1)
                for key in range(2):
                    link(V.tensor_tensor(onehot, iota.unsqueeze(1).unsqueeze(1).to_broadcast(shape), ab_f[:, key].unsqueeze(3).to_broadcast(shape), ALU.is_equal))
                    yield
                    link(V.tensor_tensor(onehot, onehot, i1[:, :, key, :].unsqueeze(2).to_broadcast(shape), ALU.mult))
                    yield
                    link(V.tensor_reduce(picked[:, key], onehot, X_AXIS, ALU.add))
                    yield
                link(V.scalar_tensor_tensor(out=eid[:, t, heads], in0=picked[:, 0], scalar=float(PK), in1=picked[:, 1], op0=ALU.mult, op1=ALU.add))
                if t == 0:
                    dve.sem_inc(s_eid, 1)
                dve.wait_ge(s_e2x, 2 * t + half + 1)
                link(V.tensor_reduce(smax, w, X_AXIS, ALU.add))
                link(V.reciprocal(smax, smax))
                link(V.tensor_tensor(w, w, smax.unsqueeze(2).to_broadcast([128, HH, TOPK]), ALU.mult))

            def sample_experts():
                e2, g2 = eid[:, 2].rearrange("p a b -> p (a b)"), gw[:, 2].rearrange("p a b -> p (a b)")
                for dst, src in ((eid_s, e2), (gw_s, g2)):
                    V.tensor_copy(dst[0:TS, :], src[0:TS, 0:64])
                    last = V.tensor_copy(dst[TS:128, :], src[TS:128, 64:128])
                last.then_inc(s_eid, 1)

            def prompt_attention(t):
                p_max(8 * t)
                for u in range(8 * t, 8 * t + 8):
                    yield
                    yield
                    p_norm(u)
                    if u % 8 < 7:
                        yield
                        p_max(u + 1)
                    yield
                    if t == 0:
                        p_turn(u)

            def sample_attention():
                dve.wait_ge(s_bs, 32)
                dve.wait_ge(s_gsi, 16 * NH)
                s_max(0)
                for b in range(DB):
                    yield
                    yield
                    smp_norm(b)
                    if b + 1 < DB:
                        yield
                        s_max(b + 1)
                    yield

            dve.wait_ge(s_zout, 16 * N_ZOUT)
            for _ in prompt_attention(0):
                pass
            for n in range(4):
                add1(0, n)
            rms2(0)
            for n in range(4):
                modulate2(0, n)
            for _ in experts(0, 0):
                pass

            def beside_dots():
                yield from experts(0, 1)
                yield from prompt_attention(1)
                for _ in range(KV_PAUSE):
                    yield
                yield from sample_attention()
                for n in range(4):
                    for _ in range(OUT_PAUSE):
                        yield
                    add1(1, n)
                yield
                rms2(1)
                for n in range(4):
                    yield
                    modulate2(1, n)

            beside = beside_dots()
            for r in range(128):
                dve.wait_ge(s_row[r % NROW], 16 * (r // NROW + 1))
                buf = rows_ring[:, r % NROW, :]
                V.tensor_tensor_reduce(out=buf, in0=buf, in1=H2_0, scale=1.0, scalar=0.0, op0=ALU.mult, op1=ALU.add, accum_out=dots[:, 0, r:r + 1]).then_inc(s_rowfree, 1)
                next(beside, None)
            for _ in beside:
                pass
            dve.wait_ge(s_rowfree, 128)
            dve.sem_inc(s_dots, 1)

            def weights(t):
                n = NROWS[t]
                dve.wait_ge(s_gelu, t + 1)
                g = gw[:, t].rearrange("p a b -> p (a b)") if t < 2 else gw_s
                V.tensor_tensor(dots[:, t, 0:n], dots[:, t, 0:n], g, ALU.mult)
                wait(dve, s_yst, 16 * t)
                link(V.memset(acc, 0.0))
                if t == 0:
                    dve.sem_inc(s_w0, 1)

            def finish(t):
                link(V.tensor_tensor(acc, acc, GB2[:, 0, :], ALU.mult))
                V.tensor_tensor(acc, acc, x1(t), ALU.add).then_inc(s_y, 1)

            def beside_sums():
                for _ in range(WQ_PAUSE):
                    yield
                for t in (1, 2):
                    for half in range(2):
                        yield from experts(t, half)
                sample_experts()

            weights(0)
            beside = beside_sums()
            for r in range(128):
                k = 128 + r
                next(beside, None)
                if r in PE_ROWS:
                    dve.sem_inc(s_rowfree, 1)
                    continue
                dve.wait_ge(s_row[k % NROW], 16 * (k // NROW + 1))
                V.scalar_tensor_tensor(out=acc, in0=rows_ring[:, k % NROW, :], scalar=dots[:, 0, r:r + 1], in1=acc, op0=ALU.mult, op1=ALU.add).then_inc(s_rowfree, 1)
                dve.wait_ge(s_rowfree, k + 1)
            for _ in beside:
                pass
            dve.wait_ge(s_prow, len(PE_ROWS))
            for n in range(4):
                cols = slice(n * SECTION, (n + 1) * SECTION)
                last = V.tensor_tensor(acc[:, cols], acc[:, cols], PS[:, n, :], ALU.add)
            link(last)
            dve.wait_ge(s_g2, 8)
            finish(0)

            for ph, (kind, t) in list(enumerate(PHASES))[N_INLINE:]:
                base = BASE[ph]
                turn = (base - LOOP_BASE) // 8
                copies = (base - LOOP_BASE) // 16
                n = NROWS[t]
                if kind == "v":
                    weights(t)
                with dve.Fori(0, n // 16, 1) as it:
                    if kind == "v":
                        V.tensor_copy(stage_w, dots[:, t, bass.ds(it * 16, 16)]).then_inc(s_stage, 1)
                        dve.wait_ge(s_stage, it + (copies + 2))
                    for s in range(16):
                        dve.wait_ge(s_lrow[s % 8], (it * 2 + (turn + s // 8)) * 16 + 16)
                        buf = loop_row[s % 8]
                        if kind == "u":
                            V.tensor_tensor_reduce(out=buf, in0=buf, in1=h2(t), scale=1.0, scalar=0.0, op0=ALU.mult, op1=ALU.add,
                                                   accum_out=stage_a[:, s:s + 1]).then_inc(s_rowfree, 1)
                        else:
                            V.scalar_tensor_tensor(out=acc, in0=buf, scalar=stage_w[:, s:s + 1], in1=acc, op0=ALU.mult, op1=ALU.add).then_inc(s_rowfree, 1)
                            dve.wait_ge(s_rowfree, it * 16 + (base + s + 1))
                    if kind == "u":
                        dve.wait_ge(s_rowfree, it * 16 + (base + 16))
                        V.tensor_copy(dots[:, t, bass.ds(it * 16, 16)], stage_a).then_inc(s_stage, 1)
                        dve.wait_ge(s_stage, it + (copies + 2))
                if kind == "u":
                    dve.sem_inc(s_dots, 1)
                elif t == 1:
                    finish(t)
                else:
                    dve.sem_inc(s_facc, 1)
                    dve.wait_ge(s_fold, 1)
                    for i in range(4):
                        cols = slice(i * SECTION, (i + 1) * SECTION)
                        last = V.tensor_tensor(acc[0:TS, cols], PS[0:TS, i, :], GB2[0:TS, 1, cols], ALU.mult)
                    link(last)
                    V.tensor_tensor(acc[0:TS, :], acc[0:TS, :], x1(2)[0:TS, :], ALU.add).then_inc(s_y, 1)


_INS = ["x_prompt", "x_sample", "cache_kv_cmp", "cache_kv_slc", "cache_kv_win", "state_pool", "page_table", "c_prompt", "c_sample",
        "w_ada", "b_ada", "g_norm1", "g_norm2", "w_in", "w_out", "g_qnorm", "g_knorm", "cmp_pe", "w_cmp", "w_pool", "pool_scale",
        "peer_wq", "peer_subkeys", "peer_u", "peer_v"]
_OUTS = [("y_prompt", (1, TP, D)), ("y_sample", (DB, DT, D)),
         ("cmp_prompt", (1, TP, 2, NKV, HD)), ("slc_prompt", (1, TP, 2, NKV, HD)), ("win_prompt", (1, TP, 2, NKV, HD)), ("pool_prompt", (1, POOL_BUF, POOL_W)),
         ("cmp_sample", (DB, DT, 2, NKV, HD)), ("slc_sample", (DB, DT, 2, NKV, HD)), ("win_sample", (DB, PAST, 2, NKV, HD)), ("pool_sample", (DB, POOL_BUF, POOL_W))]


def kernel(**inputs):
    import concourse.bacc as bacc
    from concourse.bass_utils import run_bass_kernel_spmd
    nc = bacc.Bacc("TRN2", target_bir_lowering=False, num_devices=1)
    arrays, ins, outs = {}, {}, {}
    for name, a in [(n, np.ascontiguousarray(inputs[n])) for n in _INS] + list(constants().items()):
        arrays[f"in_{name}"] = a
        ins[name] = nc.dram_tensor(f"in_{name}", a.shape, mybir.dt.from_np(a.dtype), kind="ExternalInput").ap()
    for name, shape in _OUTS:
        outs[name] = nc.dram_tensor(f"out_{name}", shape, F32, kind="ExternalOutput").ap()
    scratch = nc.dram_tensor("gates_scratch", (TS, 3 * NH), F32).ap()
    build(nc, ins, outs, scratch)
    r = run_bass_kernel_spmd(nc, [arrays], core_ids=[0])
    return tuple(r.results[0][f"out_{name}"] for name, _ in _OUTS)
```
